# Optimizing a Trainium2 kernel written in Bass

```python
import math
import jax, jax.numpy as jnp
from jax import lax
import numpy as np

D_MODEL = 1024
BATCH = 1
SEQ = 256
DEPTH = 1

N_META = 16
GDN_HEADS = 8
GDN_DK = 128
GDN_DV = 128
CONV_WIDTH = 4
CHUNK = 64
ATT_HEADS = 8
ATT_KV_HEADS = 2
ATT_HD = 128
ATT_GROUP = ATT_HEADS // ATT_KV_HEADS
IDX_HEADS = 8
IDX_HD = 64
TOPK_MAX = 256
Q_BLOCK = 128
ROPE_THETA = 10000.0
D_FF = 4 * D_MODEL
EPS = 1e-6

GDN_QK_W = GDN_HEADS * GDN_DK
GDN_V_W = GDN_HEADS * GDN_DV
ATT_Q_W = ATT_HEADS * ATT_HD
ATT_KV_W = ATT_KV_HEADS * ATT_HD
SPLITS = (GDN_QK_W, GDN_QK_W, GDN_V_W, GDN_V_W, GDN_HEADS, GDN_HEADS,
          ATT_Q_W, ATT_KV_W, ATT_KV_W, IDX_HEADS * IDX_HD, IDX_HD, IDX_HEADS,
          D_MODEL, D_MODEL)
N_IN = sum(SPLITS)


def _rmsnorm(x, g):
    xf = x.astype(jnp.float32)
    y = xf * lax.rsqrt(jnp.mean(xf * xf, axis=-1, keepdims=True) + EPS)
    return (y * g.astype(jnp.float32)).astype(x.dtype)

def _l2norm(x):
    return x * lax.rsqrt(jnp.sum(x * x, axis=-1, keepdims=True) + EPS)

def _rope_tables(pos, dim):
    inv = ROPE_THETA ** (-jnp.arange(0, dim, 2, dtype=jnp.float32) / dim)
    ang = pos.astype(jnp.float32)[:, None] * inv[None, :]
    return jnp.cos(ang), jnp.sin(ang)

def _apply_rope(x, cos, sin):
    half = x.shape[-1] // 2
    xf = x.astype(jnp.float32)
    x1, x2 = xf[..., :half], xf[..., half:]
    c = cos[None, :, None, :]
    s = sin[None, :, None, :]
    return jnp.concatenate([x1 * c - x2 * s, x2 * c + x1 * s], axis=-1).astype(x.dtype)

def _causal_conv(x, w):
    K = w.shape[0]
    T = x.shape[1]
    xp = jnp.pad(x, ((0, 0), (K - 1, 0), (0, 0)))
    y = xp[:, 0:T] * w[0]
    for j in range(1, K):
        y = y + xp[:, j:j + T] * w[j]
    return y

def _gated_delta_rule(q, k, v, beta, g):
    B_, T_, H, dk = q.shape
    dv = v.shape[-1]
    C = CHUNK
    pad = (-N_META) % C
    tail = (-(T_ + pad)) % C

    def padf(a):
        return jnp.pad(a, [(0, 0), (pad, tail)] + [(0, 0)] * (a.ndim - 2))

    q, k, v, beta, g = padf(q), padf(k), padf(v), padf(beta), padf(g)
    N = (T_ + pad + tail) // C

    def vec_chunks(a):
        return a.reshape(B_, N, C, H, a.shape[-1]).transpose(0, 3, 1, 2, 4)

    def sc_chunks(a):
        return a.reshape(B_, N, C, H).transpose(0, 3, 1, 2)

    q, k, v = vec_chunks(q), vec_chunks(k), vec_chunks(v)
    beta, g = sc_chunks(beta), sc_chunks(g)
    gc = jnp.cumsum(g, axis=-1)

    tri_incl = jnp.tril(jnp.ones((C, C), dtype=bool))
    tri_strict = jnp.tril(jnp.ones((C, C), dtype=bool), -1)
    decay = jnp.exp(jnp.where(tri_incl, gc[..., :, None] - gc[..., None, :], -jnp.inf))

    kb = k * beta[..., None]
    A = jnp.where(tri_strict, jnp.einsum('bhncd,bhnsd->bhncs', kb, k) * decay, 0.0)
    eye = jnp.eye(C, dtype=jnp.float32)
    Tm = lax.linalg.triangular_solve(A + eye, jnp.broadcast_to(eye, A.shape),
                                     left_side=True, lower=True, unit_diagonal=True)
    u = jnp.einsum('bhncs,bhnse->bhnce', Tm, v * beta[..., None])
    w = jnp.einsum('bhncs,bhnsd->bhncd', Tm, kb * jnp.exp(gc)[..., None])
    attn = jnp.einsum('bhncd,bhnsd->bhncs', q, k) * decay
    q_dec = q * jnp.exp(gc)[..., None]
    k_tail = k * jnp.exp(gc[..., -1:] - gc)[..., None]
    g_last = jnp.exp(gc[..., -1])

    def to_scan(a):
        return jnp.moveaxis(a, 2, 0)

    xs = (to_scan(q_dec), to_scan(attn), to_scan(u), to_scan(w), to_scan(k_tail), to_scan(g_last))

    def step(S, inp):
        qe, at, u_i, w_i, kt, gl = inp
        v_new = u_i - jnp.einsum('bhcd,bhde->bhce', w_i, S)
        o = jnp.einsum('bhcd,bhde->bhce', qe, S) + jnp.einsum('bhcs,bhse->bhce', at, v_new)
        S = S * gl[..., None, None] + jnp.einsum('bhcd,bhce->bhde', kt, v_new)
        return S, o

    S0 = jnp.zeros((B_, H, dk, dv), jnp.float32)
    _, o = lax.scan(step, S0, xs)
    o = o.transpose(1, 0, 3, 2, 4).reshape(B_, N * C, H, dv)
    return o[:, pad:pad + T_]

def _gdn_branch(q, k, v, z, b_raw, a_raw, conv_w, a_log, dt_bias, norm_w):
    B_, T_, _ = q.shape
    dt = q.dtype
    qkv = jax.nn.silu(_causal_conv(jnp.concatenate([q, k, v], axis=-1), conv_w))
    q, k, v = jnp.split(qkv, [GDN_QK_W, 2 * GDN_QK_W], axis=-1)
    q = q.reshape(B_, T_, GDN_HEADS, GDN_DK).astype(jnp.float32)
    k = k.reshape(B_, T_, GDN_HEADS, GDN_DK).astype(jnp.float32)
    v = v.reshape(B_, T_, GDN_HEADS, GDN_DV).astype(jnp.float32)
    q = _l2norm(q) * (GDN_DK ** -0.5)
    k = _l2norm(k)
    beta = jax.nn.sigmoid(b_raw.astype(jnp.float32))
    g = -jnp.exp(a_log.astype(jnp.float32)) * jax.nn.softplus(a_raw.astype(jnp.float32) + dt_bias.astype(jnp.float32))
    o = _gated_delta_rule(q, k, v, beta, g)
    zf = z.reshape(B_, T_, GDN_HEADS, GDN_DV).astype(jnp.float32)
    o = _rmsnorm(o, norm_w) * jax.nn.silu(zf)
    return o.reshape(B_, T_, GDN_V_W).astype(dt)

def _dsa_branch(q, k, v, qi, ki, wi, rope_att, rope_idx, n_visible):
    B_, T_, _ = q.shape
    cos_a, sin_a = rope_att
    cos_i, sin_i = rope_idx
    q = _apply_rope(q.reshape(B_, T_, ATT_HEADS, ATT_HD), cos_a, sin_a)
    k = _apply_rope(k.reshape(B_, T_, ATT_KV_HEADS, ATT_HD), cos_a, sin_a)
    v = v.reshape(B_, T_, ATT_KV_HEADS, ATT_HD)
    qi = _apply_rope(qi.reshape(B_, T_, IDX_HEADS, IDX_HD), cos_i, sin_i)
    ki = _apply_rope(ki.reshape(B_, T_, 1, IDX_HD), cos_i, sin_i)[:, :, 0]
    wi = wi * ((IDX_HEADS * IDX_HD) ** -0.5)
    kv = jnp.concatenate([k, v], axis=-1)
    topk = min(TOPK_MAX, n_visible // 4)
    nb = -(-T_ // Q_BLOCK)
    Tq = nb * Q_BLOCK

    def to_blocks(a):
        a = jnp.pad(a, [(0, 0), (0, Tq - T_)] + [(0, 0)] * (a.ndim - 2))
        return jnp.moveaxis(a.reshape((B_, nb, Q_BLOCK) + a.shape[2:]), 1, 0)

    key_pos = jnp.arange(T_, dtype=jnp.int32)

    def block(args):
        qb, qib, wib, posb = args
        s = jnp.einsum('bqhd,bsd->bqhs', qib, ki)
        s = jnp.einsum('bqhs,bqh->bqs', jax.nn.relu(s), wib).astype(jnp.float32)
        s = jnp.where(key_pos[None, None, :] <= posb[None, :, None], s, -jnp.inf)
        _, idx = lax.top_k(s, topk)
        kv_sel = jax.vmap(lambda a, i: a[i])(kv, idx)
        k_sel, v_sel = jnp.split(kv_sel, 2, axis=-1)
        qg = qb.reshape(B_, Q_BLOCK, ATT_KV_HEADS, ATT_GROUP, ATT_HD)
        logits = jnp.einsum('bqgrd,bqkgd->bqgrk', qg, k_sel).astype(jnp.float32) * (ATT_HD ** -0.5)
        valid = (idx <= posb[None, :, None])[:, :, None, None, :]
        p = jax.nn.softmax(jnp.where(valid, logits, -jnp.inf), axis=-1).astype(v.dtype)
        o = jnp.einsum('bqgrk,bqkgd->bqgrd', p, v_sel)
        return o.reshape(B_, Q_BLOCK, ATT_Q_W)

    pos_blocks = jnp.arange(Tq, dtype=jnp.int32).reshape(nb, Q_BLOCK)
    out = lax.map(block, (to_blocks(q), to_blocks(qi), to_blocks(wi), pos_blocks))
    return jnp.moveaxis(out, 0, 1).reshape(B_, Tq, ATT_Q_W)[:, :T_]

def first_inputs(seed: int = 0) -> dict:
    key = jax.random.key(seed)
    ks = jax.random.split(key, 20)
    f32 = jnp.float32

    def nrm(k, shape, scale):
        return jax.random.normal(k, shape, f32) * scale

    def gain(k, shape):
        return 1.0 + 0.02 * jax.random.normal(k, shape, f32)

    dt = jnp.exp(jax.random.uniform(ks[5], (DEPTH, GDN_HEADS), f32, math.log(1e-3), math.log(1e-1)))
    return {
        "x": jax.random.normal(ks[0], (BATCH, SEQ, D_MODEL), f32),
        "meta_tokens": nrm(ks[1], (N_META, D_MODEL), 1.0),
        "pre_mix_norm": gain(ks[2], (DEPTH, D_MODEL)),
        "w_in": nrm(ks[3], (DEPTH, D_MODEL, N_IN), D_MODEL ** -0.5),
        "conv_w": nrm(ks[4], (DEPTH, CONV_WIDTH, 2 * GDN_QK_W + GDN_V_W), CONV_WIDTH ** -0.5),
        "a_log": jnp.log(jax.random.uniform(ks[6], (DEPTH, GDN_HEADS), f32, 1.0, 16.0)),
        "dt_bias": jnp.log(jnp.expm1(dt)),
        "gdn_norm": gain(ks[7], (DEPTH, GDN_DV)),
        "w_branch_gdn": nrm(ks[8], (DEPTH, GDN_V_W, D_MODEL), GDN_V_W ** -0.5),
        "w_branch_dsa": nrm(ks[9], (DEPTH, ATT_Q_W, D_MODEL), ATT_Q_W ** -0.5),
        "w_out": nrm(ks[10], (DEPTH, D_MODEL, D_MODEL), D_MODEL ** -0.5),
        "post_mix_norm": gain(ks[11], (DEPTH, D_MODEL)),
        "pre_mlp_norm": gain(ks[12], (DEPTH, D_MODEL)),
        "w_up": nrm(ks[13], (DEPTH, D_MODEL, D_FF), D_MODEL ** -0.5),
        "w_down": nrm(ks[14], (DEPTH, D_FF, D_MODEL), D_FF ** -0.5),
        "post_mlp_norm": gain(ks[15], (DEPTH, D_MODEL)),
    }

def first_block(x, meta_tokens, pre_mix_norm, w_in, conv_w, a_log, dt_bias, gdn_norm,
              w_branch_gdn, w_branch_dsa, w_out, post_mix_norm, pre_mlp_norm, w_up, w_down,
              post_mlp_norm):
    B_, L, _ = x.shape
    meta = jnp.broadcast_to(meta_tokens.astype(x.dtype)[None], (B_, N_META, D_MODEL))
    h = jnp.concatenate([meta, x], axis=1)
    T_ = h.shape[1]
    pos = jnp.arange(T_, dtype=jnp.int32)
    rope_att = _rope_tables(pos, ATT_HD)
    rope_idx = _rope_tables(pos, IDX_HD)
    split_at = [int(i) for i in np.cumsum(SPLITS)[:-1]]

    for l in range(DEPTH):
        n = _rmsnorm(h, pre_mix_norm[l])
        proj = jnp.einsum('btd,dn->btn', n, w_in[l])
        (gq, gk, gv, gz, gb, ga, aq, ak, av, iq, ik, iw, gate_a, gate_b) = jnp.split(proj, split_at, axis=-1)
        y_gdn = _gdn_branch(gq, gk, gv, gz, gb, ga, conv_w[l], a_log[l], dt_bias[l], gdn_norm[l])
        y_dsa = _dsa_branch(aq, ak, av, iq, ik, iw, rope_att, rope_idx, L)
        merged = (jax.nn.sigmoid(gate_a) * jnp.einsum('btv,vd->btd', y_gdn, w_branch_gdn[l])
                  + jax.nn.sigmoid(gate_b) * jnp.einsum('btv,vd->btd', y_dsa, w_branch_dsa[l]))
        mix = jnp.einsum('btd,de->bte', merged, w_out[l])
        h = h + _rmsnorm(mix, post_mix_norm[l])
        n2 = _rmsnorm(h, pre_mlp_norm[l])
        u = jnp.square(jax.nn.relu(jnp.einsum('btd,df->btf', n2, w_up[l])))
        h = h + _rmsnorm(jnp.einsum('btf,fd->btd', u, w_down[l]), post_mlp_norm[l])

    return h[:, N_META:]


DEPTH_2 = 2

N_A_LAYERS = DEPTH_2 // 2
N_B_LAYERS = DEPTH_2 - N_A_LAYERS
RET_HEADS = 4
RET_QK_DIM = D_MODEL // RET_HEADS
RET_V_DIM = 2 * RET_QK_DIM
RET_CHUNK = 128
DIFF_HEAD_DIM = 64
DIFF_HEADS = D_MODEL // (2 * DIFF_HEAD_DIM)
D_FF_2 = ((8 * D_MODEL // 3 + 127) // 128) * 128
CONV_WIDTH_2 = 3
ROPE_BASE = 10000.0


def rms_norm(x, g=None):
    xf = x.astype(jnp.float32)
    y = xf * lax.rsqrt(jnp.mean(xf * xf, axis=-1, keepdims=True) + EPS)
    if g is not None:
        y = y * g.astype(jnp.float32)
    return y.astype(x.dtype)

def rotary(x, pos):
    half = x.shape[-1] // 2
    inv = 1.0 / (ROPE_BASE ** jnp.linspace(0.0, 1.0, half, dtype=jnp.float32))
    ang = pos.astype(jnp.float32)[:, None] * inv[None, :]
    cos = jnp.cos(ang)[None, :, None, :]
    sin = jnp.sin(ang)[None, :, None, :]
    xf = x.astype(jnp.float32)
    x1, x2 = xf[..., :half], xf[..., half:]
    return jnp.concatenate([x1 * cos - x2 * sin, x1 * sin + x2 * cos], axis=-1).astype(x.dtype)

def retention(xn, w_in, w_out):
    B, S, _ = xn.shape
    H, dk, dv, C = RET_HEADS, RET_QK_DIM, RET_V_DIM, RET_CHUNK
    dt = xn.dtype
    proj = xn @ w_in
    q, k, v, g = jnp.split(proj, [H * dk, 2 * H * dk, 2 * H * dk + H * dv], axis=-1)
    pos = jnp.arange(S)
    q = rotary(q.reshape(B, S, H, dk), pos)
    k = rotary(k.reshape(B, S, H, dk), pos) * (dk ** -0.5)
    v = v.reshape(B, S, H, dv)

    log_gamma = jnp.log1p(-jnp.power(2.0, -5.0 - jnp.arange(H, dtype=jnp.float32)))
    idx = jnp.arange(C, dtype=jnp.float32)
    rel = idx[:, None] - idx[None, :]
    decay_mask = jnp.where(rel[None] >= 0,
                           jnp.exp(log_gamma[:, None, None] * jnp.maximum(rel, 0.0)[None]),
                           0.0).astype(dt)
    q_decay = jnp.exp(log_gamma[None, :] * (idx[:, None] + 1.0)).astype(dt)
    k_decay = jnp.exp(log_gamma[None, :] * (C - 1.0 - idx[:, None])).astype(dt)
    chunk_decay = jnp.exp(log_gamma * C).astype(dt)

    n = S // C

    def to_chunks(t):
        return jnp.moveaxis(t.reshape(B, n, C, H, t.shape[-1]), 1, 0)

    def step(state, qkv):
        qc, kc, vc = qkv
        s = jnp.einsum('bihd,bjhd->bhij', qc, kc) * decay_mask[None]
        inner = jnp.einsum('bhij,bjhe->bihe', s, vc)
        cross = jnp.einsum('bihd,bhde->bihe', qc * q_decay[None, :, :, None], state)
        new_state = (state * chunk_decay[None, :, None, None]
                     + jnp.einsum('bjhd,bjhe->bhde', kc * k_decay[None, :, :, None], vc))
        return new_state, inner + cross

    state0 = jnp.zeros((B, H, dk, dv), dt)
    _, out = lax.scan(step, state0, (to_chunks(q), to_chunks(k), to_chunks(v)))
    out = jnp.moveaxis(out, 0, 1).reshape(B, S, H, dv)
    out = rms_norm(out).reshape(B, S, H * dv)
    return (jax.nn.silu(g) * out) @ w_out

def diff_attention(xn, k_sh, v_sh, w_q, lam_params, subln_g, w_out, lambda_init):
    B, S, _ = xn.shape
    H, d = DIFF_HEADS, DIFF_HEAD_DIM
    q = (xn @ w_q).reshape(B, S, H, 2, d) * (d ** -0.5)
    nb = S // Q_BLOCK
    q_blocks = jnp.moveaxis(q.reshape(B, nb, Q_BLOCK, H, 2, d), 1, 0)
    lp = lam_params.astype(jnp.float32)
    lam = jnp.exp(jnp.sum(lp[0] * lp[1])) - jnp.exp(jnp.sum(lp[2] * lp[3])) + lambda_init
    kpos = jnp.arange(S)

    def block(args):
        i, qb = args
        qpos = i * Q_BLOCK + jnp.arange(Q_BLOCK)
        s = jnp.einsum('bqhcd,bkhcd->bhcqk', qb, k_sh).astype(jnp.float32)
        s = jnp.where(kpos[None, :] <= qpos[:, None], s, -jnp.inf)
        p = jax.nn.softmax(s, axis=-1)
        a = p[:, :, 0] - lam * p[:, :, 1]
        return jnp.einsum('bhqk,bkhe->bqhe', a.astype(v_sh.dtype), v_sh)

    o = lax.map(block, (jnp.arange(nb), q_blocks))
    o = jnp.moveaxis(o, 0, 1).reshape(B, S, H, 2 * d)
    o = rms_norm(o, subln_g) * (1.0 - lambda_init)
    return o.reshape(B, S, H * 2 * d) @ w_out

def conv_ffn(xn, w_up, conv_w, conv_b, w_down):
    S = xn.shape[1]
    h = xn @ w_up
    hp = jnp.pad(h, ((0, 0), (CONV_WIDTH_2 - 1, 0), (0, 0)))
    hc = conv_b
    for j in range(CONV_WIDTH_2):
        hc = hc + hp[:, j:j + S] * conv_w[j]
    g, u = jnp.split(hc, 2, axis=-1)
    return (jax.nn.silu(g) * u) @ w_down

def second_inputs(seed: int = 0) -> dict:
    key = jax.random.key(seed)
    ks = jax.random.split(key, 24)
    D, F = D_MODEL, D_FF_2
    ret_in = 2 * RET_HEADS * RET_QK_DIM + 2 * RET_HEADS * RET_V_DIM
    ret_v = RET_HEADS * RET_V_DIM
    diff_w = DIFF_HEADS * 2 * DIFF_HEAD_DIM

    def w(k, shape, fan_in):
        return jax.random.normal(k, shape, jnp.float32) * (fan_in ** -0.5)

    def gain(k, shape):
        return 1.0 + 0.02 * jax.random.normal(k, shape, jnp.float32)

    return {
        "x": jax.random.normal(ks[0], (BATCH, SEQ, D), jnp.float32),
        "a_norm_pre": gain(ks[1], (N_A_LAYERS, D)),
        "a_norm_post": gain(ks[2], (N_A_LAYERS, D)),
        "a_w_in": w(ks[3], (N_A_LAYERS, D, ret_in), D),
        "a_w_out": w(ks[4], (N_A_LAYERS, ret_v, D), ret_v),
        "kv_norm": gain(ks[5], (D,)),
        "w_kv": w(ks[6], (D, 2 * diff_w), D),
        "b_norm_pre": gain(ks[7], (N_B_LAYERS, D)),
        "b_norm_post": gain(ks[8], (N_B_LAYERS, D)),
        "b_w_q": w(ks[9], (N_B_LAYERS, D, diff_w), D),
        "b_lambda": 0.1 * jax.random.normal(ks[10], (N_B_LAYERS, 4, DIFF_HEAD_DIM), jnp.float32),
        "b_subln": gain(ks[11], (N_B_LAYERS, 2 * DIFF_HEAD_DIM)),
        "b_w_out": w(ks[12], (N_B_LAYERS, diff_w, D), diff_w),
        "ffn_norm_pre": gain(ks[13], (DEPTH_2, D)),
        "ffn_norm_post": gain(ks[14], (DEPTH_2, D)),
        "ffn_w_up": w(ks[15], (DEPTH_2, D, 2 * F), D),
        "ffn_conv_w": w(ks[16], (DEPTH_2, CONV_WIDTH_2, 2 * F), CONV_WIDTH_2),
        "ffn_conv_b": 0.02 * jax.random.normal(ks[17], (DEPTH_2, 2 * F), jnp.float32),
        "ffn_w_down": w(ks[18], (DEPTH_2, F, D), F),
    }

def second_block(x, a_norm_pre, a_norm_post, a_w_in, a_w_out, kv_norm, w_kv,
              b_norm_pre, b_norm_post, b_w_q, b_lambda, b_subln, b_w_out,
              ffn_norm_pre, ffn_norm_post, ffn_w_up, ffn_conv_w, ffn_conv_b, ffn_w_down):
    B, S, _ = x.shape
    H, d = DIFF_HEADS, DIFF_HEAD_DIM
    k_sh = None
    v_sh = None
    for layer in range(DEPTH_2):
        if layer < N_A_LAYERS:
            i = layer
            h = retention(rms_norm(x, a_norm_pre[i]), a_w_in[i], a_w_out[i])
            x = x + rms_norm(h, a_norm_post[i])
        else:
            i = layer - N_A_LAYERS
            if i == 0:
                kv = rms_norm(x, kv_norm) @ w_kv
                k_flat, v_flat = jnp.split(kv, 2, axis=-1)
                k_sh = k_flat.reshape(B, S, H, 2, d)
                v_sh = v_flat.reshape(B, S, H, 2 * d)
            lambda_init = 0.8 - 0.6 * math.exp(-0.3 * layer)
            h = diff_attention(rms_norm(x, b_norm_pre[i]), k_sh, v_sh, b_w_q[i],
                               b_lambda[i], b_subln[i], b_w_out[i], lambda_init)
            x = x + rms_norm(h, b_norm_post[i])
        h = conv_ffn(rms_norm(x, ffn_norm_pre[layer]), ffn_w_up[layer],
                     ffn_conv_w[layer], ffn_conv_b[layer], ffn_w_down[layer])
        x = x + rms_norm(h, ffn_norm_post[layer])
    return x


def setup_inputs(seed=0):
    out = dict(first_inputs(seed))
    for name, value in second_inputs(seed + 1).items():
        if name != "x":
            out[name + "_2"] = value
    return out


def reference(
    x, meta_tokens, pre_mix_norm, w_in, conv_w, a_log, dt_bias, gdn_norm, w_branch_gdn,
    w_branch_dsa, w_out, post_mix_norm, pre_mlp_norm, w_up, w_down, post_mlp_norm, a_norm_pre_2,
    a_norm_post_2, a_w_in_2, a_w_out_2, kv_norm_2, w_kv_2, b_norm_pre_2, b_norm_post_2, b_w_q_2,
    b_lambda_2, b_subln_2, b_w_out_2, ffn_norm_pre_2, ffn_norm_post_2, ffn_w_up_2, ffn_conv_w_2,
    ffn_conv_b_2, ffn_w_down_2,
):
    x = first_block(
        x, meta_tokens, pre_mix_norm, w_in, conv_w, a_log, dt_bias, gdn_norm, w_branch_gdn,
        w_branch_dsa, w_out, post_mix_norm, pre_mlp_norm, w_up, w_down, post_mlp_norm,
    )
    return second_block(
        x, a_norm_pre_2, a_norm_post_2, a_w_in_2, a_w_out_2, kv_norm_2, w_kv_2, b_norm_pre_2,
        b_norm_post_2, b_w_q_2, b_lambda_2, b_subln_2, b_w_out_2, ffn_norm_pre_2,
        ffn_norm_post_2, ffn_w_up_2, ffn_conv_w_2, ffn_conv_b_2, ffn_w_down_2,
    )


_drawn_inputs = setup_inputs


def setup_inputs(seed=0):
    import zlib

    import numpy as np

    out = dict(_drawn_inputs(seed))
    spreads = {}
    factors = {'post_mlp_norm': 2.693,
     'a_norm_post_2': 4.49,
     'kv_norm_2': 5.011,
     'b_norm_pre_2': 7.735,
     'b_norm_post_2': 63.671,
     'b_subln_2': 58.531,
     'ffn_norm_pre_2': 2.99,
     'ffn_norm_post_2': 4.402,
     'ffn_conv_b_2': 3.004}
    for name, (base, spread) in spreads.items():
        noise = np.random.default_rng([zlib.crc32(name.encode()), seed]).standard_normal(out[name].shape)
        drawn = base * np.exp(spread * noise) if base else spread * noise
        out[name] = __import__('jax').numpy.asarray(drawn.astype(out[name].dtype))
    for name, factor in factors.items():
        out[name] = (out[name] * factor).astype(out[name].dtype)
    return out
```

```python
import math
from contextlib import ExitStack

import numpy as np
import concourse.bass as bass
from concourse import mybir

F32 = mybir.dt.float32
F32R = mybir.dt.float32r
ALU = mybir.AluOpType
ACT = mybir.ActivationFunctionType
AX = mybir.AxisListType

P = 128
D = 1024
KT = D // P
NCOL = 256
SLOT = KT * NCOL
META = 16
SEQ = 256
T1 = META + SEQ
H1 = 8
TOPK = 64
ROUNDS = TOPK // 8
IDX_SCALE = (8 * 64) ** -0.5
ATT_SCALE = 128 ** -0.5
EPS = 1e-6
FF1 = 4096
FF2 = 2816
FT2 = FF2 // P
LAMBDA_INIT = 0.8 - 0.6 * math.exp(-0.3)
BIG = 1e30
TAKEN = -3e38

STREAM = [("small", 1), ("qkv", 12), ("iq", 2), ("av", 1), ("ak", 1), ("aq", 4), ("z", 4), ("ga", 4),
          ("gb", 4), ("wbd", 4), ("wbg", 4), ("wout", 4), ("up", 16), ("down", 16), ("rq", 4), ("rk", 4),
          ("rv", 8), ("rg", 8), ("ro", 8), ("fu0", 22), ("fd0", 12), ("dk", 4), ("dv", 4), ("dq", 4),
          ("do", 4), ("fu1", 22), ("fd1", 12)]
FIRST = {}
_at = 0
for _name, _count in STREAM:
    FIRST[_name] = _at
    _at += _count
NSLOT = _at

PARAMS = [("pre_mix", 8), ("conv", 96), ("gdn", 1), ("post_mix", 8), ("pre_mlp", 8), ("post_mlp", 8),
          ("a_pre", 8), ("a_post", 8), ("kv", 8), ("b_pre", 8), ("b_post", 8), ("subln", 1),
          ("f_pre0", 8), ("f_pre1", 8), ("f_post0", 8), ("f_post1", 8),
          ("f_conv0", 3 * 2 * FT2), ("f_conv1", 3 * 2 * FT2), ("f_bias0", 2 * FT2), ("f_bias1", 2 * FT2),
          ("alog", 8), ("dtb", 8), ("lam", 256)]
PCOL = {}
_at = 0
for _name, _count in PARAMS:
    PCOL[_name] = _at
    _at += _count
NPAR = _at

CONST1 = [("ident", 128), ("upper", 128), ("upper16", 128), ("ones16", 128), ("spread", 128), ("head", 8),
          ("levels", 7 * 128), ("cosa", T1), ("sina", T1), ("cosi", T1), ("sini", T1), ("turna", 128),
          ("turni", 128), ("past", 2 * T1)]
CONST2 = [("rcos", SEQ), ("rsin", SEQ), ("decay", 4 * SEQ), ("past2", 2 * SEQ)]
CCOL = {}
_at = 0
for _name, _count in CONST1:
    CCOL[_name] = _at
    _at += _count
NC1 = _at
_at = 0
for _name, _count in CONST2:
    CCOL[_name] = _at
    _at += _count
NC2 = _at
NLEVEL = 7
CHUNKS = [(META, P), (META + P, P), (0, META)]


class Chain:

    def __init__(self, eng, sem):
        self.eng, self.sem, self.n = eng, sem, 0

    def link(self, ins):
        ins.then_inc(self.sem, 1)
        self.n = self.n + 1
        self.eng.wait_ge(self.sem, self.n)


def slots(eng, name, step, body=4, chain=None, links=0, lead=0):
    first, count = FIRST[name], dict(STREAM)[name]
    for j in range(lead):
        step(first + j, 0, j)
    loops = (count - lead) // body if count - lead >= 2 * body else 0
    if loops:
        before = chain.n if chain else 0
        with eng.Fori(0, loops) as it:
            if chain:
                chain.n = before + it * (links * body)
            for j in range(lead, lead + body):
                step(first + j, it, j)
        if chain:
            chain.n = before + loops * links * body
    for j in range(lead + loops * body, count):
        step(first + j, 0, j)


def program(nc, stream, params, const1, const2, x_in, y_out, upto=None, dumps=()):
    ctx = ExitStack()
    with ctx:
        base = -(-nc.sbuf_base // 64) * 64
        arena = ctx.enter_context(nc.sbuf_tensor("arena", [P, (nc.sbuf_usable_end - base) // 4 - 32], F32))
        del arena

        def at(name, off, shape, dt=F32):
            return nc.alloc_sbuf_tensor_at(name, shape, dt, offset=base + off)

        RAW_N = 4
        raw = at("raw", 0, [P, RAW_N, KT, NCOL])
        whi = at("whi", 32768, [P, 2, KT, NCOL], F32R)
        wlo = at("wlo", 49152, [P, 2, KT, NCOL], F32R)
        par = at("par", 65536, [P, NPAR])
        cursor = [65536 + 4 * NPAR]

        def nxt(name, shape):
            cursor[0] = -(-cursor[0] // 32) * 32
            t = at(name, cursor[0], shape)
            cursor[0] += 4 * int(np.prod(shape[1:]))
            return t

        ones = nxt("ones", [P, P])
        eps = nxt("eps", [P, 2])
        small = nxt("small", [P, 3, 24])
        bg = nxt("bg", [P, 3, 16])
        gtmp = nxt("gtmp", [P, 3, 3, 8])
        bcg = nxt("bcg", [P, 2, 17])
        gcum = nxt("gcum", [P, 17])
        sel16 = nxt("sel16", [P, 16])
        ktsc = nxt("ktsc", [P, 9])
        egl = nxt("egl", [P, 8])
        lamt = nxt("lamt", [P, 8])
        aexp = nxt("aexp", [P, 8])
        wix = nxt("wix", [P, 2, 8])
        rmax = nxt("rmax", [P, 16])
        rsum = nxt("rsum", [P, 16])
        rinv = nxt("rinv", [P, 16])
        top8 = nxt("top8", [P, 8])
        rinv2 = nxt("rinv2", [P, 16])
        rstd = nxt("rstd", [P, T1])
        PC = -(-cursor[0] // 64) * 64
        c1 = at("c1", PC, [P, NC1])
        c2 = at("c2", PC + 512, [P, NC2])
        HB = PC + 4 * NC1
        h = at("h", HB, [P, KT, T1])
        B = HB + 8704
        xhi = at("xhi", B, [P, KT, T1], F32R)
        xlo = at("xlo", B + 8704, [P, KT, T1], F32R)
        qkv = at("qkv", B + 17408, [P, 24, T1])
        aq = at("aq", B + 43520, [P, 8, SEQ])
        ak = at("ak", B + 51712, [P, 2, T1])
        av = at("av", B + 53888, [P, 3, NCOL])
        iq = at("iq", B + 56960, [P, 4, SEQ])
        ik = at("ik", B + 61056, [P, T1])
        ctmp = at("ctmp", B + 62144, [P, 2, 2, T1])
        lm = at("lm", B + 62144, [P, 8, T1])
        ibias = at("ibias", B + 70848, [P, T1])
        iscore = at("iscore", B + 71936, [P, T1])
        iwork = at("iwork", B + 73024, [P, T1])
        irelu = at("irelu", B + 74112, [P, 2, T1])
        zs = at("zs", B + 43520, [P, 8, SEQ])
        gas = at("gas", B + 51712, [P, 8, SEQ])
        gbs = at("gbs", B + 59904, [P, 8, SEQ])
        m1 = at("m1", B + 68096, [P, 8, SEQ])
        yhi = at("yhi", B + 76288, [P, 8, SEQ], F32R)
        ylo = at("ylo", B + 84480, [P, 8, SEQ], F32R)
        prob = at("prob", B + 92672, [P, 8, T1])
        yo = at("yo", B + 101376, [P, 8, SEQ])
        pT = at("pT", B + 109568, [P, 2, 3, P])
        rtmp = at("rtmp", B + 62144, [P, 8, SEQ])
        xf = at("xf", B + 109568, [P, KT, T1])
        sq = at("sq", B + 92672, [P, KT, T1])
        rn = at("rn", B + 101376, [P, 8, T1])
        eg = at("eg", B + 76288, [P, 8, P])
        dm = at("dm", B + 80384, [P, 8, P])
        kb = at("kb", B + 84480, [P, 8, P])
        att = at("att", B + 88576, [P, 8, P])
        at_ = at("at_", B + 92672, [P, 8, P])
        al = at("al", B + 96768, [P, 8, P])
        tu = at("tu", B + 100864, [P, 4, 4, P])
        xs = at("xs", B + 109056, [P, 8, P])
        vb = at("vb", B + 113152, [P, 8, P])
        ktok = at("ktok", B, [P, 8, P])
        vn = at("vn", B + 4096, [P, 8, P])
        st = at("st", B + 8192, [P, 8, P])
        ktm = at("ktm", B + 12288, [P, 8, P])
        og = at("og", B + 59904, [P, 8, SEQ])
        sq2 = at("sq2", B + 92672, [P, 8, SEQ])
        rn2 = at("rn2", B + 101376, [P, 8, SEQ])
        rt = at("rt", B + 82944, [P, 2, 2, SEQ])
        ut = at("ut", B + 87040, [P, 2, 2, SEQ])
        uhi = at("uhi", B + 17408, [P, 32, SEQ], F32R)
        ulo = at("ulo", B + 50176, [P, 32, SEQ], F32R)
        rq = at("rq", B + 17408, [P, 8, SEQ])
        rk = at("rk", B + 25600, [P, 8, SEQ])
        rv = at("rv", B + 33792, [P, 2, 2048])
        rg = at("rg", B + 50176, [P, 16, SEQ])
        rp = at("rp", B + 66560, [P, 4, 384])
        ro = at("ro", B + 72704, [P, 16, SEQ])
        rsq = at("rsq", B + 89088, [P, 2, 4, SEQ])
        rrn = at("rrn", B + 97280, [P, 2, SEQ])
        rt1 = at("rt1", B + 99328, [P, 2, SEQ])
        rt2 = at("rt2", B + 101376, [P, 2, SEQ])
        rhi = at("rhi", B, [P, 16, SEQ], F32R)
        rlo = at("rlo", B + 17408, [P, 16, SEQ], F32R)
        fhi = at("fhi", B + 17408, [P, FT2, SEQ], F32R)
        flo = at("flo", B + 39936, [P, FT2, SEQ], F32R)
        ft = at("ft", B + 62464, [P, 2, 2, SEQ])
        fs = at("fs", B + 66560, [P, 2, SEQ])
        fu = at("fu", B + 68608, [P, 2, SEQ])
        x2hi = at("x2hi", B + 17408, [P, 8, SEQ], F32R)
        x2lo = at("x2lo", B + 25600, [P, 8, SEQ], F32R)
        dk = at("dk", B + 33792, [P, 8, SEQ])
        dq = at("dq", B + 41984, [P, 8, SEQ])
        dv = at("dv", B + 50176, [P, 2, 1024])
        lm2 = at("lm2", B + 58368, [P, 16, SEQ])
        am = at("am", B + 74752, [P, 8, SEQ])
        aT = at("aT", B + 84992, [P, 2, 2, P])
        do = at("do", B + 17408, [P, 8, SEQ])

        PS = [ctx.enter_context(nc.psum_tensor(f"lin{n}", [P, 2, 512], F32)) for n in range(2)]
        AUX = [ctx.enter_context(nc.psum_tensor(f"aux{n}", [P, 512], F32)) for n in range(4)]

        def sem(name):
            return ctx.enter_context(nc.semaphore(name))

        w_loaded = [sem(f"w_loaded{r}") for r in range(RAW_N)]
        hi_ready = sem("hi_ready")
        lo_ready = sem("lo_ready")
        slot_done = sem("slot_done")
        pair_free = [sem(f"pair_free{n}") for n in range(2)]
        aux_full = [sem(f"aux_full{n}") for n in range(4)]
        aux_free = [sem(f"aux_free{n}") for n in range(4)]
        par_in = sem("par_in")
        c1_in = sem("c1_in")
        c2_in = sem("c2_in")
        x_loaded = sem("x_loaded")
        set_up = sem("set_up")
        out_done = sem("out_done")
        act_own = sem("act_own")
        dve_own = sem("dve_own")
        pool_own = sem("pool_own")
        named = {}

        def S(name):
            if name not in named:
                named[name] = sem(name)
            return named[name]

        filled = [0] * 4
        USE = {}

        def use(bank, *names):
            for name in names:
                filled[bank] += 1
                USE[name] = (bank, filled[bank], 0)

        def use_loop(count, banks_names):
            per = [0] * 4
            for bank, name in banks_names:
                per[bank] += 1
                USE[name] = (bank, filled[bank] + per[bank], 1)
            for bank, name in banks_names:
                USE[name] = (bank, USE[name][1], per[bank])
            for n in range(4):
                filled[n] += per[n] * count

        def fill(name, it=0):
            bank, n, per = USE[name]
            if n > 1 or per:
                nc.tensor.wait_ge(aux_free[bank], n - 1 + it * per)
            return AUX[bank]

        def is_full(ins, name):
            ins.then_inc(aux_full[USE[name][0]], 1)

        def full(eng, name, it=0):
            bank, n, per = USE[name]
            eng.wait_ge(aux_full[bank], n + it * per)
            return AUX[bank]

        def is_free(ins, name):
            ins.then_inc(aux_free[USE[name][0]], 1)

        def pcol(name, n=0, count=1):
            return par[:, PCOL[name] + n:PCOL[name] + n + count]

        def pdyn(name, n, count=1):
            return par[:, bass.ds(PCOL[name] + n, count)]

        def cst(name, rows=P, t=c1, lo=0, n=None):
            a = CCOL[name] + lo
            width = dict(CONST1 + CONST2)[name] - lo if n is None else n
            return t[0:rows, a:a + width]

        ident = cst("ident")

        use(2, "norm_mix")
        use(0, "rot_ik")
        use(1, "rot_iq0")
        use(2, "rot_iq1")
        use(3, "rot_ak0")
        use(0, "rot_ak1")
        for n in range(4):
            use((n + 1) % 4, f"rot_aq{n}")
        for t in range(2):
            for hh in range(H1):
                use(hh % 4, f"idx{t}_{hh}")
            for hh in range(H1):
                use(hh % 4, f"log{t}_{hh}")
            for hh in range(H1):
                use(hh % 2, f"tr{t}_{hh}")
                if hh % 4 == 3:
                    use(2 + hh // 4, f"pv{t}_{hh // 4}")
        for w in "qk":
            for hh in range(H1):
                use(hh % 4, f"l2{w}{hh}")
        use(0, "sel")
        use(1, "cum")
        PROBLEMS = [[16], list(range(8)), list(range(8, 16))]
        LEVELS = [4, NLEVEL, NLEVEL]
        for s, probs in enumerate(PROBLEMS):
            ng = -(-len(probs) // 4)
            for g in range(ng):
                use(2 * g % 4, f"gb{s}_{g}")
                use((2 * g + 1) % 4, f"bb{s}_{g}")
            for g in range(ng):
                use(g, f"kk{s}_{g}")
                if s:
                    use(2 + g, f"qk{s}_{g}")
            for g in range(ng):
                use(g, f"vt{s}_{g}")
                if s < 2:
                    use(2 + g, f"kt{s}_{g}")
            if s:
                use_loop(LEVELS[s], [(0, f"x{s}_0"), (1, f"x{s}_1"), (2, f"y{s}_0"), (3, f"y{s}_1"),
                                     (0, f"y{s}_2"), (1, f"y{s}_3")])
            else:
                use_loop(LEVELS[s], [(0, f"x{s}_0"), (2, f"y{s}_0")])
            for g in range(ng):
                if s:
                    use(g, f"r{s}_{g}")
            for g in range(ng):
                use(2 + g, f"v{s}_{g}")
            for g in range(2):
                if s:
                    use(g, f"o{s}_{g}")
                if s < 2:
                    use(2 + g, f"s{s}_{g}")
        for n in range(4):
            use(n, f"ng{n}")
        use(0, "norm_postmix")
        use(1, "norm_mlp")
        use(2, "norm_postmlp")
        use(3, "norm_ret")
        for hh in range(4):
            use(hh, f"rs{hh}")
        for hh in range(4):
            use(0, f"ro{hh}_0")
            use(1, f"ro{hh}_1")
            use(2 + hh % 2, f"rn{hh}")
        use(0, "norm_postret")
        use(1, "norm_ffn0")
        use(2, "norm_postffn0")
        use(3, "norm_diff")
        for t in range(2):
            for n in range(4):
                for c in range(2):
                    use(2 * (n % 2) + c, f"ds{t}_{n}_{c}")
            for hh in range(H1):
                use(hh % 2, f"dt{t}_{hh}")
                if hh % 4 == 3:
                    use(2 + hh // 4, f"dp{t}_{hh // 4}")
        for n in range(4):
            use(n, f"nd{n}")
        use(0, "norm_postdiff")
        use(1, "norm_ffn1")
        use(2, "norm_postffn1")

        def load_hi(s0, it):
            if s0 >= NSLOT:
                return
            nc.scalar.wait_ge(w_loaded[s0 % 4], 16 * (s0 // 4 + 1) + 16 * it)
            if s0 >= 2:
                nc.scalar.wait_ge(slot_done, s0 - 1 + 4 * it)
            nc.scalar.copy(whi[:, s0 % 2], raw[:, s0 % 4]).then_inc(hi_ready, 1)

        def load_lo(s0, it):
            if s0 >= NSLOT:
                return
            nc.vector.wait_ge(hi_ready, s0 + 1 + 4 * it)
            nc.vector.tensor_tensor(wlo[:, s0 % 2], raw[:, s0 % 4], whi[:, s0 % 2].bitcast(F32),
                                    ALU.subtract).then_inc(lo_ready, 1)

        def slot_in(s0, it):
            nc.tensor.wait_ge(lo_ready, s0 + 1 + 4 * it)

        def pair_in(u0, it, per):
            if u0 >= 2:
                nc.tensor.wait_ge(pair_free[u0 % 2], u0 // 2 + it * per)

        def mm3(out, s0, kt, cols, hi, lo, start, stop, swap=False):
            wh, wl = whi[:, s0 % 2, kt, cols], wlo[:, s0 % 2, kt, cols]
            if swap:
                trio = ((hi, wh), (hi, wl), (lo, wh))
            else:
                trio = ((wh, hi), (wh, lo), (wl, hi))
            for n, (a, b) in enumerate(trio):
                ins = nc.tensor.matmul(out, a, b, start=start and n == 0, stop=stop and n == 2)
            return ins

        def feature_slot(s0, pair, hi, lo, tiles=(0, 1), kts=KT, k0=0, start=True, stop=True):
            T = hi.shape[-1]
            for t in tiles:
                for kt in range(kts):
                    ins = mm3(PS[pair][:, t, 0:T], s0, kt, slice(t * P, t * P + P), hi[:, k0 + kt], lo[:, k0 + kt],
                              start and kt == 0, stop and kt == kts - 1)
            return ins

        def token_slot(s0, out, hi, lo, cols, m, t0):
            for kt in range(KT):
                ins = mm3(out, s0, kt, cols, hi[:, kt, t0:t0 + m], lo[:, kt, t0:t0 + m], kt == 0, kt == KT - 1,
                          swap=True)
            return ins

        GROUP = {"down": 4, "ro": 2, "fd0": 3, "fd1": 3}
        pair_first = {}
        n = 0
        for name, count in STREAM:
            pair_first[name] = n
            n += count // GROUP.get(name, 1)

        def pe_layer(name, hi, lo, body=4, lead=0):
            def step(s0, it, j):
                u0 = pair_first[name] + j
                slot_in(s0, it)
                pair_in(u0, it, body // 2)
                feature_slot(s0, u0 % 2, hi, lo).then_inc(slot_done, 1)
            slots(nc.tensor, name, step, body, lead=lead)

        def pe_groups(name, hi, lo, group, kts_last, body):
            def step(s0, it, j):
                g = j % group
                u0 = pair_first[name] + j // group
                slot_in(s0, it * (body // 4))
                if g == 0:
                    pair_in(u0, it, body // group // 2)
                kts = kts_last if g == group - 1 else KT
                T = hi.shape[-1]
                for t in range(2):
                    for kt in range(kts):
                        ins = mm3(PS[u0 % 2][:, t, 0:T], s0, kt, slice(t * P, t * P + P), hi[:, g * KT + kt],
                                  lo[:, g * KT + kt], g == 0 and kt == 0, g == group - 1 and kt == kts - 1)
                ins.then_inc(slot_done, 1)
            slots(nc.tensor, name, step, body)

        def bc(a, n):
            return a.unsqueeze(1).to_broadcast([a.shape[0], n, a.shape[1]])

        def wide(a, w):
            return a.rearrange("p (n w) -> p n w", w=w)

        def after(eng, name, it=0):
            bank, n, per = USE[name]
            eng.wait_ge(aux_free[bank], n + it * per)

        def pair_done(eng, u):
            eng.wait_ge(pair_free[u % 2], u // 2 + 1)

        hx = h[:, :, META:T1]

        def norm_view(name):
            return (h[:], T1) if name == "mix" else (hx, SEQ)

        def has(name):
            return name in FIRST

        def seg(probs):
            return (len(probs) + 3) // 4

        block = ctx.enter_context(nc.Block())

        @block.sync
        def _(sp):
            sp.dma_start(h[:], x_in).then_inc(x_loaded, 16)
            sp.dma_start(par[:], params).then_inc(par_in, 16)
            for s in range(4):
                sp.dma_start(raw[:, s], stream[s]).then_inc(w_loaded[s], 16)
            sp.dma_start(c1[:], const1).then_inc(c1_in, 16)
            with sp.Fori(1, NSLOT // 4) as it:
                for r in range(4):
                    sp.wait_ge(lo_ready, it * 4 + (r - 3))
                    sp.dma_start(raw[:, r], stream[bass.ds(it * 4 + r, 1)].rearrange("o p k n -> (o p) k n")).then_inc(w_loaded[r], 16)
            for s in range(NSLOT // 4 * 4, NSLOT):
                sp.wait_ge(lo_ready, s - 3)
                sp.dma_start(raw[:, s % 4], stream[s]).then_inc(w_loaded[s % 4], 16)
            if upto:
                for e in ("pe", "act", "dve", "pool"):
                    sp.wait_ge(S("end_" + e), 1)
                for n, (src, dst) in enumerate(dumps):
                    sp.dma_start(dst, eval_dump(src)).then_inc(out_done, 16)
                sp.wait_ge(out_done, 16 * len(dumps))
                return
            sp.wait_ge(S("h_postffn1"), 1)
            sp.dma_start(y_out, hx).then_inc(out_done, 16)
            sp.wait_ge(out_done, 16)

        scope = dict(locals())

        def eval_dump(src):
            return src(scope)


        def pool_body(pool, own):
            if upto in ("A", "B", "C"):
                return
            for s in range(3):
                npb = len(PROBLEMS[s])
                n = npb
                first = sum(LEVELS[:s])
                pool.wait_ge(S("at_ready"), s + 1)
                with pool.Fori(0, LEVELS[s]) as it:
                    after_x = USE[f"x{s}_{seg(PROBLEMS[s]) - 1}"]
                    if s == 0:
                        pool.wait_ge(aux_full[after_x[0]], after_x[1] - after_x[2] + it * after_x[2])
                    else:
                        pool.wait_ge(aux_full[after_x[0]], after_x[1] - after_x[2] + it * after_x[2])
                    lev = c1[:, bass.ds(it * P + CCOL["levels"], P)]
                    nc.gpsimd.tensor_tensor(al[:, 0:n], at_[:, 0:n], bc(lev, n), ALU.mult).then_inc(S("al_ready"), 1)
            if upto in ("D",):
                return
            pool.wait_ge(S("ygdn_lo"), 1)
            pool.dma_start(c2[:], const2).then_inc(c2_in, 16)
            for k in range(2):
                if not has(f"fu{k}"):
                    return
                def tail(s0, it, j):
                    n0 = k * FT2 + j
                    pool.wait_ge(S("f_silu"), n0 + 1 + 4 * it)
                    if n0 >= 2:
                        pool.wait_ge(S("f_hi"), n0 - 1 + 4 * it)
                    nc.gpsimd.tensor_tensor(fu[:, s0 % 2], fs[:, s0 % 2], ft[:, s0 % 2, 1], ALU.mult)\
                        .then_inc(S("f_prod"), 1)
                    pool.wait_ge(S("f_prod"), n0 + 1 + 4 * it)
                    pool.wait_ge(S("f_hi"), n0 + 1 + 4 * it)
                    nc.gpsimd.tensor_tensor(flo[:, bass.ds(j + 4 * it, 1)], fu[:, s0 % 2].unsqueeze(1),
                                            fhi[:, bass.ds(j + 4 * it, 1)].bitcast(F32), ALU.subtract).then_inc(S("f_lo"), 1)
                slots(pool, f"fu{k}", tail)


        def act_pre(act, name, hi, until=0):
            src, T = norm_view(name)
            nc.scalar.activation(sq[:, :, 0:T], src, ACT.Square).then_inc(S("sq_" + name), 1)
            act_root(act, name, T)
            act_high(act, name, hi, T, until)

        def act_root(act, name, T):
            b = full(act, "norm_" + name)
            is_free(nc.scalar.activation(rstd[:, 0:T], b[:, 0:T], ACT.Sqrt, scale=1.0 / D, bias=eps[:, 0:1]),
                    "norm_" + name)

        def act_high(act, name, hi, T, until=0):
            if until:
                act.wait_ge(slot_done, until)
            for half in range(2):
                act.wait_ge(S("xf_" + name), half + 1)
                a = slice(4 * half, 4 * half + 4)
                nc.scalar.copy(hi[:, a, 0:T], xf[:, a, 0:T]).then_inc(S("xhi_" + name), 1)

        def act_layer_out(act, name):
            group = GROUP.get(name, 1)
            for j in range(dict(STREAM)[name]):
                s = FIRST[name] + j
                act.wait_ge(slot_done, s + 1)
                if j % group == group - 1:
                    g = j // group
                    u = pair_first[name] + g
                    nc.scalar.copy(yo[:, 2 * g:2 * g + 2], PS[u % 2][:, :, 0:SEQ])
                    nc.scalar.activation(sq[:, 2 * g:2 * g + 2, 0:SEQ], PS[u % 2][:, :, 0:SEQ], ACT.Square)\
                        .then_inc(pair_free[u % 2], 1)
                load_hi(s + 2, 0)

        def act_body(act, own):
            act.wait_ge(set_up, 1)
            act.wait_ge(x_loaded, 16)
            nc.scalar.activation(sq[:], h[:], ACT.Square).then_inc(S("sq_mix"), 1)
            load_hi(0, 0)
            load_hi(1, 0)
            act_root(act, "mix", T1)
            act_high(act, "mix", xhi, T1)
            act.wait_ge(slot_done, 1)
            nc.scalar.copy(ik[:], PS[0][:, 0, 0:T1])
            nc.scalar.copy(small[:, 0:2, :], wide(PS[0][:, 1, 0:64], 32)[:, :, 0:24])
            nc.scalar.copy(small[0:META, 2, :], PS[0][0:META, 1, 64:88]).then_inc(pair_free[0], 1)
            load_hi(2, 0)
            act.wait_ge(par_in, 16)

            def conv(s0, it, j):
                u0 = pair_first["qkv"] + j
                act.wait_ge(slot_done, s0 + 1 + 4 * it)
                for t in range(2):
                    col = (2 * j + t) * 4 + 3 + it * 32
                    ins = nc.scalar.activation(ctmp[:, u0 % 2, t], PS[u0 % 2][:, t, 0:T1], ACT.Copy,
                                               scale=pdyn("conv", col))
                ins.then_inc(S("conv_tap"), 1)
                load_hi(s0 + 2, it)
                act.wait_ge(pair_free[u0 % 2], u0 // 2 + 1 + 2 * it)
                nc.scalar.activation(qkv[:, bass.ds(2 * j + 8 * it, 2)], ctmp[:, u0 % 2], ACT.Silu)\
                    .then_inc(S("conv_silu"), 1)
            slots(act, "qkv", conv)
            for name, dst in (("iq", iq[:]), ("av", av[:]), ("ak", ak[:]), ("aq", aq[:])):
                for j in range(dict(STREAM)[name]):
                    s = FIRST[name] + j
                    u = pair_first[name] + j
                    act.wait_ge(slot_done, s + 1)
                    if name == "av":
                        nc.scalar.copy(av[:, 0:2], PS[u % 2][:, :, 0:NCOL])
                        nc.scalar.copy(av[0:META, 2], PS[u % 2][0:META, 0, NCOL:2 * NCOL]).then_inc(pair_free[u % 2], 1)
                    elif name == "ak":
                        nc.scalar.copy(ak[:], PS[u % 2][:, :, 0:T1]).then_inc(pair_free[u % 2], 1)
                    else:
                        nc.scalar.copy(dst[:, 2 * j:2 * j + 2], PS[u % 2][:, :, META:T1]).then_inc(pair_free[u % 2], 1)
                    load_hi(s + 2, 0)
            if upto == "A":
                return
            for t in range(2):
                W = META + P + t * P
                for hh in range(H1):
                    b = full(act, f"idx{t}_{hh}")
                    n = t * H1 + hh
                    if n >= 2:
                        act.wait_ge(S("relu_used"), n - 1)
                    is_free(nc.scalar.activation(irelu[:, hh % 2, 0:W], b[:, 0:W], ACT.Relu), f"idx{t}_{hh}")
                act.wait_ge(S("rmax"), t + 1)
                if t:
                    full(act, "tr0_7")
                for hh in range(H1):
                    ins = nc.scalar.activation(prob[:, hh, 0:W], lm[:, hh, 0:W], ACT.Exp, bias=rmax[:, hh:hh + 1],
                                               accum_out=rsum[:, hh:hh + 1])
                ins.then_inc(S("exp"), 1)
                for hh in range(H1 + 1):
                    if hh < H1:
                        b = full(act, f"tr{t}_{hh}")
                        if hh >= 2 or t:
                            done = hh - 2 if hh >= 2 else hh + 6
                            if done % 4 == 3:
                                full(act, f"pv{t if hh >= 2 else t - 1}_{done // 4}")
                            else:
                                act.wait_ge(S("pv_mm"), pv_count(t if hh >= 2 else t - 1, done))
                        if t:
                            nc.scalar.copy(pT[:, hh % 2, 0:2], wide(b[:, 0:2 * P], P))
                        else:
                            nc.scalar.copy(pT[:, hh % 2, 0], b[:, 0:P])
                        is_free(nc.scalar.copy(pT[0:META, hh % 2, 2], b[0:META, 2 * P:3 * P]), f"tr{t}_{hh}")
                    if hh % 4 == 0 and hh:
                        g = hh // 4 - 1
                        b = full(act, f"pv{t}_{g}")
                        is_free(nc.scalar.copy(yo[:, 4 * g:4 * g + 4, t * P:t * P + P], wide(b[:], P)), f"pv{t}_{g}")
            own.link(nc.scalar.copy(rsum[:, 0:1], rsum[:, 0:1]))
            nc.scalar.copy(yhi[:], yo[:]).then_inc(S("yhi"), 1)
            if upto == "B":
                return
            for name, dst, func in (("z", zs, ACT.Silu), ("ga", gas, ACT.Sigmoid), ("gb", gbs, ACT.Sigmoid)):
                for j in range(4):
                    s, u = FIRST[name] + j, pair_first[name] + j
                    act.wait_ge(slot_done, s + 1)
                    nc.scalar.activation(dst[:, 2 * j:2 * j + 2], PS[u % 2][:, :, META:T1], func)\
                        .then_inc(pair_free[u % 2], 1)
                    load_hi(s + 2, 0)
            for j in range(4):
                load_hi(FIRST["wbd"] + j + 2, 0)
            if upto == "C":
                return
            act_gdn(act, own)
            if upto == "D":
                return
            for name in ("wbg",):
                for j in range(4):
                    act.wait_ge(S("merged"), j + 1)
                    nc.scalar.copy(xhi[:, 2 * j:2 * j + 2, 0:SEQ], yo[:, 2 * j:2 * j + 2]).then_inc(S("mhi"), 1)
                    load_hi(FIRST[name] + j + 2, 0)
            act_layer_out(act, "wout")
            act_root(act, "postmix", SEQ)
            act.wait_ge(S("h_postmix"), 1)
            act_pre(act, "mlp", xhi, FIRST["up"])

            def up(s0, it, j):
                u0 = pair_first["up"] + j
                act.wait_ge(slot_done, s0 + 1 + 4 * it)
                own.link(nc.scalar.activation(rt[:, u0 % 2], PS[u0 % 2][:, :, 0:SEQ], ACT.Relu))
                nc.scalar.activation(uhi[:, bass.ds(2 * j + 8 * it, 2)], rt[:, u0 % 2], ACT.Square)\
                    .then_inc(pair_free[u0 % 2], 1)
                load_hi(s0 + 2, it)
            slots(act, "up", up, chain=own, links=1)
            act_layer_out(act, "down")
            act_root(act, "postmlp", SEQ)
            if upto == "G":
                return
            act_second(act, own)

        def pv_count(t, hh):
            return t * 6 + (hh // 4) * 3 + hh % 4 + 1

        def act_gdn(act, own):
            for w in range(2):
                nc.scalar.activation(sq[:], qkv[:, 8 * w:8 * w + 8], ACT.Square).then_inc(S("l2sq"), 1)
                if w:
                    act.wait_ge(S("l2done"), 1)
                for hh in range(H1):
                    name = f"l2{'qk'[w]}{hh}"
                    b = full(act, name)
                    is_free(nc.scalar.activation(rn[:, hh], b[:, 0:T1], ACT.Sqrt, scale=[float(P), 1.0][w],
                                                 bias=eps[:, 1 - w:2 - w]), name)
            nc.scalar.activation(bg[:, :, 0:8], small[:, :, 0:8], ACT.Sigmoid)
            nc.scalar.activation(aexp[:], pcol("alog", 0, 8), ACT.Exp)
            act.wait_ge(S("g_arg"), 1)
            own.link(nc.scalar.activation(gtmp[:, 1], gtmp[:, 0], ACT.Abs))
            own.link(nc.scalar.activation(gtmp[:, 1], gtmp[:, 1], ACT.Exp, scale=-1.0))
            nc.scalar.activation(gtmp[:, 1], gtmp[:, 1], ACT.Ln, bias=ones[:, 0:1]).then_inc(S("g_ln"), 1)
            act.wait_ge(S("ktsc"), 1)
            nc.scalar.activation(ktsc[:], ktsc[:], ACT.Exp)
            is_free(nc.scalar.activation(egl[:], AUX[USE["cum"][0]][:, 20:28], ACT.Exp), "cum")
            ndm = 0
            for s, probs in enumerate(PROBLEMS):
                n = len(probs)
                for g in range(seg(probs)):
                    m = min(4, n - 4 * g)
                    ndm += 1
                    act.wait_ge(S("dm_arg"), ndm)
                    name = f"gb{s}_{g}"
                    is_free(nc.scalar.activation(eg[:, 4 * g:4 * g + m], wide(AUX[USE[name][0]][:, 0:m * P], P), ACT.Exp),
                            name)
                    nc.scalar.activation(dm[:, 4 * g:4 * g + m], dm[:, 4 * g:4 * g + m], ACT.Exp)\
                        .then_inc(S("dm_exp"), 1)
                lev0 = sum(LEVELS[:s])
                with act.Fori(0, LEVELS[s]) as it:
                    for g in range(seg(probs)):
                        m = min(4, n - 4 * g)
                        b = full(act, f"x{s}_{g}", it)
                        is_free(nc.scalar.copy(xs[:, 4 * g:4 * g + m], wide(b[:, 0:m * P], P)), f"x{s}_{g}")
                for g in range(seg(probs)):
                    m = min(4, n - 4 * g)
                    b = full(act, f"v{s}_{g}")
                    is_free(nc.scalar.copy(vn[:, 4 * g:4 * g + m], wide(b[:, 0:m * P], P)), f"v{s}_{g}")
                for g in range(2):
                    if s:
                        b = full(act, f"o{s}_{g}")
                        is_free(nc.scalar.copy(og[:, 4 * g:4 * g + 4, (s - 1) * P:s * P], wide(b[:], P)), f"o{s}_{g}")
            head_norm_act(act, own, og, "ng", "ogn", 1.0 / P)
            act.wait_ge(S("ogdone"), 1)
            nc.scalar.copy(yhi[:], sq2[:]).then_inc(S("ygdn_hi"), 1)

        def head_norm_act(act, own, src, use_name, sem_name, scale):
            own.link(nc.scalar.copy(rsum[:, 0:1], rsum[:, 0:1]))
            nc.scalar.activation(sq2[:], src[:], ACT.Square).then_inc(S(sem_name), 1)
            for n in range(4):
                b = full(act, f"{use_name}{n}")
                is_free(nc.scalar.activation(rn2[:, 2 * n:2 * n + 2], wide(b[:], SEQ), ACT.Sqrt, scale=scale,
                                             bias=eps[:, 0:1]), f"{use_name}{n}")

        def act_second(act, own):
            act.wait_ge(S("h_postmlp"), 1)
            act_pre(act, "ret", xhi)
            for name in ("rq", "rk"):
                for j in range(4):
                    s = FIRST[name] + j
                    act.wait_ge(slot_done, s + 1)
                    load_hi(s + 2, 0)

            def values(s0, it, j):
                u0 = pair_first["rv"] + j
                act.wait_ge(slot_done, s0 + 1 + 4 * it)
                nc.scalar.copy(rv[:, :, bass.ds(j * NCOL + 4 * NCOL * it, NCOL)], PS[u0 % 2][:, :, 0:NCOL])\
                    .then_inc(pair_free[u0 % 2], 1)
                load_hi(s0 + 2, it)
            slots(act, "rv", values)

            def gate(s0, it, j):
                u0 = pair_first["rg"] + j
                act.wait_ge(slot_done, s0 + 1 + 4 * it)
                nc.scalar.activation(rg[:, bass.ds(2 * j + 8 * it, 2)], PS[u0 % 2][:, :, 0:SEQ], ACT.Silu)\
                    .then_inc(pair_free[u0 % 2], 1)
                load_hi(s0 + 2, it)
            slots(act, "rg", gate)
            for hh in range(4):
                if hh >= 2:
                    full(act, f"rn{hh - 2}")
                for e in range(2):
                    b = full(act, f"ro{hh}_{e}")
                    nc.scalar.copy(ro[:, 4 * hh + 2 * e:4 * hh + 2 * e + 2], wide(b[:], SEQ))
                    is_free(nc.scalar.activation(rsq[:, hh % 2, 2 * e:2 * e + 2], wide(b[:], SEQ), ACT.Square),
                            f"ro{hh}_{e}")
                b = full(act, f"rn{hh}")
                is_free(nc.scalar.activation(rrn[:, hh % 2], b[:, 0:SEQ], ACT.Sqrt, scale=1.0 / 512, bias=eps[:, 0:1]),
                        f"rn{hh}")
                act.wait_ge(S("ro_done"), hh + 1)
                nc.scalar.copy(rhi[:, 4 * hh:4 * hh + 4], ro[:, 4 * hh:4 * hh + 4]).then_inc(S("rhi"), 1)
            act_layer_out(act, "ro")
            act_root(act, "postret", SEQ)
            act_ffn(act, own, 0)
            if upto == "I":
                return
            act.wait_ge(S("h_postffn0"), 1)
            src, T = norm_view("diff")
            nc.scalar.activation(sq[:, :, 0:T], src, ACT.Square).then_inc(S("sq_diff"), 1)
            act_root(act, "diff", T)
            act_high(act, "diff", xhi, T)
            for half in range(2):
                act.wait_ge(S("xf_diff"), 3 + half)
                a = slice(4 * half, 4 * half + 4)
                nc.scalar.copy(x2hi[:, a], xf[:, a, 0:SEQ]).then_inc(S("xhi_diff"), 1)
            act.wait_ge(S("lam"), 1)
            nc.scalar.activation(lamt[:, 2:4], lamt[:, 0:2], ACT.Exp).then_inc(S("lam_exp"), 1)
            for name in ("dk", "dv", "dq"):
                for j in range(4):
                    s, u = FIRST[name] + j, pair_first[name] + j
                    act.wait_ge(slot_done, s + 1)
                    if name == "dv":
                        nc.scalar.copy(dv[:, :, j * NCOL:(j + 1) * NCOL], PS[u % 2][:, :, 0:NCOL])\
                            .then_inc(pair_free[u % 2], 1)
                    else:
                        dst = dk if name == "dk" else dq
                        nc.scalar.copy(dst[:, 2 * j:2 * j + 2], PS[u % 2][:, :, 0:SEQ]).then_inc(pair_free[u % 2], 1)
                    load_hi(s + 2, 0)
            for t in range(2):
                W = P + t * P
                act.wait_ge(S("rmax2"), t + 1)
                for n in range(16):
                    ins = nc.scalar.activation(lm2[:, n, 0:W], lm2[:, n, 0:W], ACT.Exp, bias=rmax[:, n:n + 1],
                                               accum_out=rsum[:, n:n + 1])
                ins.then_inc(S("exp2"), 1)
                for hh in range(H1 + 1):
                    if hh < H1:
                        b = full(act, f"dt{t}_{hh}")
                        if hh >= 2 or t:
                            done = hh - 2 if hh >= 2 else hh + 6
                            if done % 4 == 3:
                                full(act, f"dp{t if hh >= 2 else t - 1}_{done // 4}")
                            else:
                                act.wait_ge(S("dp_mm"), pv_count(t if hh >= 2 else t - 1, done))
                        is_free(nc.scalar.copy(aT[:, hh % 2, 0:1 + t], wide(b[:, 0:W], P)), f"dt{t}_{hh}")
                    if hh % 4 == 0 and hh:
                        g = hh // 4 - 1
                        b = full(act, f"dp{t}_{g}")
                        is_free(nc.scalar.copy(do[:, 4 * g:4 * g + 4, t * P:t * P + P], wide(b[:], P)), f"dp{t}_{g}")
            head_norm_act(act, own, do, "nd", "don", 1.0 / P)
            act.wait_ge(S("dodone"), 1)
            nc.scalar.copy(yhi[:], do[:]).then_inc(S("dohi"), 1)
            act_layer_out(act, "do")
            act_root(act, "postdiff", SEQ)
            act_ffn(act, own, 1)

        def act_ffn(act, own, k):
            act.wait_ge(S(["h_postret", "h_postdiff"][k]), 1)
            act_pre(act, f"ffn{k}", xhi, FIRST[f"fu{k}"])

            def conv(s0, it, j):
                u0 = pair_first[f"fu{k}"] + j
                n0 = k * FT2 + j
                p = s0 % 2
                act.wait_ge(slot_done, s0 + 1 + 4 * it)
                if n0 >= 2:
                    act.wait_ge(S("f_prod"), n0 - 1 + 4 * it)
                for t in range(2):
                    ins = nc.scalar.activation(ft[:, p, t], PS[u0 % 2][:, t, 0:SEQ], ACT.Identity,
                                               scale=pdyn(f"f_conv{k}", (t * FT2 + j) * 3 + 2 + 12 * it),
                                               bias=pdyn(f"f_bias{k}", t * FT2 + j + 4 * it))
                ins.then_inc(S("f_tap"), 1)
                load_hi(s0 + 2, it)
                act.wait_ge(pair_free[u0 % 2], u0 // 2 + 1 + 2 * it)
                nc.scalar.activation(fs[:, p], ft[:, p, 0], ACT.Silu).then_inc(S("f_silu"), 1)
                act.wait_ge(S("f_prod"), n0 + 1 + 4 * it)
                nc.scalar.copy(fhi[:, bass.ds(j + 4 * it, 1)], fu[:, p].unsqueeze(1)).then_inc(S("f_hi"), 1)
            slots(act, f"fu{k}", conv)
            act_layer_out(act, f"fd{k}")
            act_root(act, f"postffn{k}", SEQ)


        def dve_norm(dve, own, name, gain, src, T, halves=2):
            for kt in range(KT):
                ins = nc.vector.scalar_tensor_tensor(xf[:, kt, 0:T], src[:, kt], pcol(gain, kt), rstd[:, 0:T],
                                                     ALU.mult, ALU.mult)
                if kt % 4 == 3:
                    ins.then_inc(S("xf_" + name), 1)

        def dve_low(dve, name, lo, hi, T, first=0):
            for half in range(2):
                dve.wait_ge(S("xhi_" + name), first + half + 1)
                a = slice(4 * half, 4 * half + 4)
                nc.vector.tensor_tensor(lo[:, a, 0:T], xf[:, a, 0:T], hi[:, a, 0:T].bitcast(F32), ALU.subtract)\
                    .then_inc(S("xlo_" + name), 1)

        def dve_pre(dve, own, name, gain, hi, lo):
            src, T = norm_view(name)
            after(dve, "norm_" + name)
            own.link(nc.vector.reciprocal(rstd[:, 0:T], rstd[:, 0:T]))
            dve_norm(dve, own, name, gain, src, T)
            dve_low(dve, name, lo, hi, T)

        def dve_post(dve, own, name, gain):
            after(dve, "norm_" + name)
            own.link(nc.vector.reciprocal(rstd[:, 0:SEQ], rstd[:, 0:SEQ]))
            for kt in range(KT):
                ins = nc.vector.scalar_tensor_tensor(xf[:, kt, 0:SEQ], yo[:, kt], pcol(gain, kt), rstd[:, 0:SEQ],
                                                     ALU.mult, ALU.mult)
            own.link(ins)
            nc.vector.tensor_tensor(hx, hx, xf[:, :, 0:SEQ], ALU.add).then_inc(S("h_" + name), 1)
            dve.wait_ge(S("h_" + name), 1)

        def dve_idle_layer(name):
            def step(s0, it, j):
                load_lo(s0 + 2, it)
            slots(nc.vector, name, step, NSLOT if name == STREAM[-1][0] else 4)

        def dve_body(dve, own):
            dve.wait_ge(par_in, 16)
            load_lo(0, 0)
            load_lo(1, 0)
            dve_pre(dve, own, "mix", "pre_mix", xhi, xlo)
            load_lo(2, 0)

            def conv(s0, it, j):
                u0 = pair_first["qkv"] + j
                dve.wait_ge(S("conv_tap"), j + 1 + 4 * it)
                for tap in (2, 1, 0):
                    sh = 3 - tap
                    for t in range(2):
                        col = (2 * j + t) * 4 + tap + it * 32
                        ins = nc.vector.scalar_tensor_tensor(
                            ctmp[:, u0 % 2, t, sh:T1], PS[u0 % 2][:, t, 0:T1 - sh], pdyn("conv", col),
                            ctmp[:, u0 % 2, t, sh:T1], ALU.mult, ALU.add)
                    if tap:
                        own.link(ins)
                ins.then_inc(pair_free[u0 % 2], 1)
                load_lo(s0 + 2, it)
            slots(dve, "qkv", conv, chain=own, links=2)
            for name in ("iq", "av", "ak", "aq"):
                for j in range(dict(STREAM)[name]):
                    load_lo(FIRST[name] + j + 2, 0)
            dve.wait_ge(c1_in, 16)
            dve.wait_ge(S("conv_silu"), 12)
            turned = 0
            for name, x, W, c, sn, t0 in rotations():
                n = x.shape[1]
                b = full(dve, name)
                is_free(nc.vector.tensor_tensor(ctmp[:, 0, 0:n, 0:W], wide(b[:, 0:n * W], W),
                                                bc(cst(sn, lo=t0, n=W), n), ALU.mult), name)
                after(dve, name)
                own.link(nc.vector.tensor_tensor(x, x, bc(cst(c, lo=t0, n=W), n), ALU.mult))
                nc.vector.tensor_tensor(x, x, ctmp[:, 0, 0:n, 0:W], ALU.add).then_inc(S("rope"), 1)
                turned += 1
                dve.wait_ge(S("rope"), turned)
            if upto == "A":
                return
            own.link(nc.vector.tensor_scalar(wix[:], small[:, 0:2, 16:24], IDX_SCALE, None, ALU.mult))
            for t in range(2):
                W = META + P + t * P
                past = cst("past", lo=t * T1, n=W)
                for hh in range(H1):
                    after(dve, f"idx{t}_{hh}")
                    w = wix[:, t, hh:hh + 1]
                    n = t * H1 + hh
                    if n:
                        dve.wait_ge(S("relu_used"), n)
                    if hh == 0:
                        ins = nc.vector.tensor_scalar(iscore[:, 0:W], irelu[:, hh % 2, 0:W], w, None, ALU.mult)
                    else:
                        ins = nc.vector.scalar_tensor_tensor(iscore[:, 0:W], irelu[:, hh % 2, 0:W], w, iscore[:, 0:W],
                                                             ALU.mult, ALU.add)
                    ins.then_inc(S("relu_used"), 1)
                dve.wait_ge(S("relu_used"), t * H1 + H1)
                own.link(nc.vector.tensor_tensor(iwork[:, 0:W], iscore[:, 0:W], past, ALU.add))
                for _ in range(ROUNDS):
                    own.link(nc.vector.max(top8[:], iwork[:, 0:W]))
                    own.link(nc.vector.match_replace(iwork[:, 0:W], top8[:], iwork[:, 0:W], TAKEN))
                own.link(nc.vector.tensor_scalar(ibias[:, 0:W], iwork[:, 0:W], TAKEN, BIG, ALU.is_equal, ALU.mult))
                own.link(nc.vector.scalar_tensor_tensor(ibias[:, 0:W], ibias[:, 0:W], -BIG, past, ALU.add, ALU.add))
                for hh in range(H1):
                    b = full(dve, f"log{t}_{hh}")
                    is_free(nc.vector.scalar_tensor_tensor(lm[:, hh, 0:W], b[:, 0:W], ATT_SCALE, ibias[:, 0:W],
                                                           ALU.mult, ALU.add), f"log{t}_{hh}")
                for hh in range(4, 8):
                    after(dve, f"log{t}_{hh}")
                nc.vector.tensor_reduce(rmax[:, 0:8], lm[:, :, 0:W], AX.X, ALU.max, negate=True)\
                    .then_inc(S("rmax"), 1)
                dve.wait_ge(S("exp"), t + 1)
                own.link(nc.vector.reciprocal(rinv[:, 0:8], rsum[:, 0:8]))
                nc.vector.tensor_tensor(prob[:, :, 0:W], prob[:, :, 0:W],
                                        rinv[:, 0:8].unsqueeze(2).to_broadcast([P, 8, W]), ALU.mult)\
                    .then_inc(S("prob"), 1)
            dve.wait_ge(S("yhi"), 1)
            nc.vector.tensor_tensor(ylo[:], yo[:], yhi[:].bitcast(F32), ALU.subtract).then_inc(S("ylo"), 1)
            if upto == "B":
                return
            for name in ("z", "ga", "gb"):
                for j in range(4):
                    load_lo(FIRST[name] + j + 2, 0)
            for j in range(4):
                s, u = FIRST["wbd"] + j, pair_first["wbd"] + j
                dve.wait_ge(slot_done, s + 1)
                if j == 0:
                    pair_done(dve, pair_first["gb"] + 3)
                nc.vector.tensor_tensor(m1[:, 2 * j:2 * j + 2], PS[u % 2][:, :, 0:SEQ], gbs[:, 2 * j:2 * j + 2],
                                        ALU.mult).then_inc(pair_free[u % 2], 1)
                load_lo(s + 2, 0)
            if upto == "C":
                return
            dve_gdn(dve, own)
            if upto == "D":
                return
            for j in range(4):
                s, u = FIRST["wbg"] + j, pair_first["wbg"] + j
                a = slice(2 * j, 2 * j + 2)
                dve.wait_ge(slot_done, s + 1)
                nc.vector.tensor_tensor(yo[:, a], PS[u % 2][:, :, 0:SEQ], gas[:, a], ALU.mult).then_inc(pair_free[u % 2], 1)
                pair_done(dve, u)
                nc.vector.tensor_tensor(yo[:, a], yo[:, a], m1[:, a], ALU.add).then_inc(S("merged"), 1)
                dve.wait_ge(S("mhi"), j + 1)
                nc.vector.tensor_tensor(xlo[:, a, 0:SEQ], yo[:, a], xhi[:, a, 0:SEQ].bitcast(F32), ALU.subtract)\
                    .then_inc(S("mlo"), 1)
                load_lo(s + 2, 0)
            dve_idle_layer("wout")
            dve_post(dve, own, "postmix", "post_mix")
            dve_pre(dve, own, "mlp", "pre_mlp", xhi, xlo)

            def up(s0, it, j):
                u0 = pair_first["up"] + j
                dve.wait_ge(pair_free[u0 % 2], u0 // 2 + 1 + 2 * it)
                p = u0 % 2
                own.link(nc.vector.tensor_tensor(ut[:, p], rt[:, p], rt[:, p], ALU.mult))
                nc.vector.tensor_tensor(ulo[:, bass.ds(2 * j + 8 * it, 2)], ut[:, p],
                                        uhi[:, bass.ds(2 * j + 8 * it, 2)].bitcast(F32), ALU.subtract)\
                    .then_inc(S("ulo"), 1)
                load_lo(s0 + 2, it)
            slots(dve, "up", up, chain=own, links=1)
            dve_idle_layer("down")
            dve_post(dve, own, "postmlp", "post_mlp")
            if upto == "G":
                return
            dve_second(dve, own)

        def dve_gdn(dve, own):
            own.link(nc.vector.tensor_tensor(gtmp[:, 0], small[:, :, 8:16], bc(pcol("dtb", 0, 8), 3), ALU.add))
            nc.vector.tensor_scalar(top8[:, 0:1], ones[:, 0:1], 1.0, None, ALU.mult).then_inc(S("g_arg"), 1)
            for w in range(2):
                for hh in range(4, 8):
                    after(dve, f"l2{'qk'[w]}{hh}")
                own.link(nc.vector.reciprocal(rn[:], rn[:]))
                nc.vector.tensor_tensor(qkv[:, 8 * w:8 * w + 8], qkv[:, 8 * w:8 * w + 8], rn[:], ALU.mult)\
                    .then_inc(S("l2done"), 1)
            dve.wait_ge(S("l2done"), 2)
            for n in range(2):
                ins = nc.vector.tensor_copy(wide(og[:, n, 0:P], META), qkv[:, 8 + 8 * n:16 + 8 * n, 0:META])
            ins.then_inc(S("meta_kv"), 1)
            dve.wait_ge(S("meta_kv"), 1)
            dve.wait_ge(S("g_ln"), 1)
            own.link(nc.vector.scalar_tensor_tensor(gtmp[:, 0], gtmp[:, 0], 0.0, gtmp[:, 1], ALU.max, ALU.add))
            nc.vector.scalar_tensor_tensor(bg[:, :, 8:16], gtmp[:, 0], -1.0, bc(aexp[:], 3), ALU.mult, ALU.mult)\
                .then_inc(S("bg"), 1)
            dve.wait_ge(S("bg"), 1)
            nc.vector.tensor_copy(bcg[:, 0, 0:16].rearrange("p (c n) -> p c n", n=8), bg[:, 0:2, 0:8])
            nc.vector.tensor_copy(bcg[:, 1, 0:16].rearrange("p (c n) -> p c n", n=8), bg[:, 0:2, 8:16])
            b = full(dve, "sel")
            is_free(nc.vector.tensor_tensor(wide(sel16[:], 8), wide(b[:, 0:16], 8), bc(cst("head"), 2), ALU.mult), "sel")
            after(dve, "sel")
            nc.vector.tensor_reduce(bcg[:, :, 16:17], wide(sel16[:], 8), AX.X, ALU.add).then_inc(S("bcg"), 1)
            dve.wait_ge(S("bcg"), 1)
            b = full(dve, "cum")
            own.link(nc.vector.tensor_copy(gcum[:], b[:, 0:17]))
            nc.vector.tensor_tensor(ktsc[:, 0:8], b[:, 20:28], gcum[:, 0:8], ALU.subtract)
            nc.vector.tensor_tensor(ktsc[:, 8:9], b[:, 28:29], gcum[:, 16:17], ALU.subtract).then_inc(S("ktsc"), 1)
            nexp = 0
            for s, probs in enumerate(PROBLEMS):
                n = len(probs)
                ng = seg(probs)
                upper = cst("upper") if s else cst("upper16")
                if s:
                    after(dve, f"s{s - 1}_1") if s == 1 else None
                for g in range(ng):
                    m = min(4, n - 4 * g)
                    b = full(dve, f"gb{s}_{g}")
                    for q in range(m):
                        ins = nc.vector.tensor_scalar(dm[:, 4 * g + q], b[:, q * P:q * P + P],
                                                      gcum[:, probs[4 * g + q]:probs[4 * g + q] + 1], 0.0,
                                                      ALU.subtract, ALU.min)
                    ins.then_inc(S("dm_arg"), 1)
                    b = full(dve, f"bb{s}_{g}")
                    is_free(nc.vector.tensor_tensor(kb[:, 4 * g:4 * g + m], wide(b[:, 0:m * P], P), kview(s, g, m),
                                                    ALU.mult), f"bb{s}_{g}")
                for g in range(ng):
                    m = min(4, n - 4 * g)
                    nexp += 1
                    dve.wait_ge(S("dm_exp"), nexp)
                    a = slice(4 * g, 4 * g + m)
                    own.link(nc.vector.tensor_tensor(dm[:, a], dm[:, a], bc(upper, m), ALU.mult))
                    b = full(dve, f"kk{s}_{g}")
                    is_free(nc.vector.tensor_tensor(at_[:, a], wide(b[:, 0:m * P], P), dm[:, a], ALU.mult), f"kk{s}_{g}")
                    if s:
                        b = full(dve, f"qk{s}_{g}")
                        is_free(nc.vector.tensor_tensor(att[:, a], wide(b[:, 0:m * P], P), dm[:, a], ALU.mult),
                                f"qk{s}_{g}")
                for g in range(ng):
                    after(dve, f"kk{s}_{g}")
                for g in range(-(-n // 2)):
                    ins = nc.vector.tensor_copy(tu[:, g], bc(ident, 4))
                ins.then_inc(S("at_ready"), 1)
                if s:
                    own.link(nc.vector.tensor_tensor(kb[:, 0:n], kb[:, 0:n], eg[:, 0:n], ALU.mult))
                    q = qkv[:, 0:8, META + (s - 1) * P:META + s * P]
                    nc.vector.tensor_tensor(q, q, eg[:, 0:n], ALU.mult).then_inc(S("ke"), 1)
                for g in range(ng):
                    m = min(4, n - 4 * g)
                    b = full(dve, f"vt{s}_{g}")
                    for q in range(m):
                        p_ = probs[4 * g + q]
                        ins = nc.vector.tensor_scalar(vb[:, 4 * g + q], b[:, q * P:q * P + P], bcg[:, 0, p_:p_ + 1], None,
                                                      ALU.mult)
                    is_free(ins, f"vt{s}_{g}")
                    if s < 2:
                        if s == 0 and g == 0:
                            after(dve, "cum")
                        b = full(dve, f"kt{s}_{g}")
                        for q in range(m):
                            c = 8 if s == 0 else 4 * g + q
                            ins = nc.vector.tensor_scalar(ktok[:, 4 * g + q], b[:, q * P:q * P + P], ktsc[:, c:c + 1],
                                                          None, ALU.mult)
                        is_free(ins, f"kt{s}_{g}")
                if s == 0:
                    after(dve, "kt0_0")
                    for hh in range(H1):
                        ins = nc.vector.tensor_scalar(ktm[:, hh], ktok[:, 0], cst("head", lo=hh, n=1), None, ALU.mult)
                    ins.then_inc(S("ktm"), 1)
                with dve.Fori(0, LEVELS[s]) as it:
                    for g in range(-(-n // 2)):
                        m = min(2, n - 2 * g)
                        b = full(dve, f"y{s}_{g}", it)
                        is_free(nc.vector.tensor_tensor(tu[:, g], wide(b[:], P), tu[:, g], ALU.add)
                                if m == 2 else
                                nc.vector.tensor_tensor(tu[:, g, 0:4:2], wide(b[:], P)[:, 0:4:2], tu[:, g, 0:4:2], ALU.add),
                                f"y{s}_{g}")
                for g in range(ng):
                    a = slice(4 * g, 4 * g + 4)
                    if s:
                        b = full(dve, f"r{s}_{g}")
                        is_free(nc.vector.tensor_tensor(vb[:, a], vb[:, a], wide(b[:], P), ALU.subtract), f"r{s}_{g}")
                if s < 2:
                    for g in range(2):
                        a = slice(4 * g, 4 * g + 4)
                        b = full(dve, f"s{s}_{g}")
                        if s == 0:
                            is_free(nc.vector.tensor_copy(st[:, a], wide(b[:], P)), f"s{s}_{g}")
                        else:
                            full(dve, f"o{s}_{g}")
                            for q in range(4):
                                hh = 4 * g + q
                                ins = nc.vector.scalar_tensor_tensor(st[:, hh], st[:, hh], egl[:, hh:hh + 1],
                                                                     b[:, q * P:q * P + P], ALU.mult, ALU.add)
                            is_free(ins, f"s{s}_{g}")
            head_norm_dve(dve, own, "ng")
            own.link(nc.vector.tensor_tensor(og[:], og[:], rn2[:], ALU.mult))
            nc.vector.scalar_tensor_tensor(sq2[:], og[:], pcol("gdn"), zs[:], ALU.mult, ALU.mult).then_inc(S("ogdone"), 1)
            dve.wait_ge(S("ygdn_hi"), 1)
            nc.vector.tensor_tensor(ylo[:], sq2[:], yhi[:].bitcast(F32), ALU.subtract).then_inc(S("ygdn_lo"), 1)

        def head_norm_dve(dve, own, use_name):
            for n in range(4):
                after(dve, f"{use_name}{n}")
            own.link(nc.vector.reciprocal(rn2[:], rn2[:]))

        def kview(s, g, m):
            if s == 0:
                return og[:, 0:1, 0:P]
            t0 = META + (s - 1) * P
            return qkv[:, 8 + 4 * g:8 + 4 * g + m, t0:t0 + P]

        def rotations():
            yield "rot_ik", ik[:].unsqueeze(1), T1, "cosi", "sini", 0
            for n in range(2):
                yield f"rot_iq{n}", iq[:, 2 * n:2 * n + 2], SEQ, "cosi", "sini", META
            for n in range(2):
                yield f"rot_ak{n}", ak[:, n:n + 1], T1, "cosa", "sina", 0
            for n in range(4):
                yield f"rot_aq{n}", aq[:, 2 * n:2 * n + 2], SEQ, "cosa", "sina", META

        def dve_second(dve, own):
            dve_pre(dve, own, "ret", "a_pre", xhi, xlo)
            dve.wait_ge(c2_in, 16)
            cos, sin = cst("rcos", t=c2), cst("rsin", t=c2)
            for name, dst in (("rq", rq), ("rk", rk)):
                for j in range(4):
                    s, u = FIRST[name] + j, pair_first[name] + j
                    dve.wait_ge(slot_done, s + 1)
                    x = PS[u % 2][:, :, 0:SEQ]
                    nc.vector.tensor_tensor(rt1[:], x, bc(cos, 2), ALU.mult)
                    nc.vector.tensor_tensor(rt2[:], x, bc(sin, 2), ALU.mult).then_inc(pair_free[u % 2], 1)
                    pair_done(dve, u)
                    nc.vector.tensor_tensor(dst[:, 2 * j], rt1[:, 0], rt2[:, 1], ALU.subtract)
                    own.link(nc.vector.tensor_tensor(dst[:, 2 * j + 1], rt1[:, 1], rt2[:, 0], ALU.add))
                    load_lo(s + 2, 0)
            nc.vector.tensor_scalar(top8[:, 0:1], ones[:, 0:1], 1.0, None, ALU.mult).then_inc(S("rqk"), 1)
            dve_idle_layer("rv")
            dve_idle_layer("rg")
            for hh in range(4):
                b = full(dve, f"rs{hh}")
                dec = cst("decay", t=c2, lo=hh * SEQ, n=SEQ)
                nc.vector.tensor_tensor(rp[:, hh, 0:SEQ], b[:, 0:SEQ], dec, ALU.mult)
                is_free(nc.vector.tensor_tensor(rp[:, hh, SEQ:384], b[:, SEQ:384], dec[:, 0:P], ALU.mult), f"rs{hh}")
            for hh in range(4):
                a = slice(4 * hh, 4 * hh + 4)
                after(dve, f"rn{hh}")
                own.link(nc.vector.reciprocal(rrn[:, hh % 2], rrn[:, hh % 2]))
                own.link(nc.vector.tensor_tensor(ro[:, a], ro[:, a], bc(rrn[:, hh % 2], 4), ALU.mult))
                nc.vector.tensor_tensor(ro[:, a], ro[:, a], rg[:, a], ALU.mult).then_inc(S("ro_done"), 1)
                dve.wait_ge(S("rhi"), hh + 1)
                nc.vector.tensor_tensor(rlo[:, a], ro[:, a], rhi[:, a].bitcast(F32), ALU.subtract)\
                    .then_inc(S("rlo"), 1)
            dve_idle_layer("ro")
            dve_post(dve, own, "postret", "a_post")
            dve_ffn(dve, own, 0)
            if upto == "I":
                return
            src, T = norm_view("diff")
            after(dve, "norm_diff")
            own.link(nc.vector.reciprocal(rstd[:, 0:T], rstd[:, 0:T]))
            dve_norm(dve, own, "diff", "kv", src, T)
            dve_low(dve, "diff", xlo, xhi, T)
            dve.wait_ge(S("xlo_diff"), 2)
            dve_norm(dve, own, "diff", "b_pre", src, T)
            dve_low(dve, "diff", x2lo, x2hi, T, 2)
            for n in range(2):
                own.link(nc.vector.tensor_tensor(am[:, n, 0:64], pcol("lam", 128 * n, 64), pcol("lam", 128 * n + 64, 64),
                                                 ALU.mult))
            nc.vector.tensor_reduce(lamt[:, 0:2].unsqueeze(2), am[:, 0:2, 0:64], AX.X, ALU.add).then_inc(S("lam"), 1)
            dve.wait_ge(S("lam_exp"), 1)
            own.link(nc.vector.scalar_tensor_tensor(lamt[:, 4:5], lamt[:, 2:3], LAMBDA_INIT, lamt[:, 3:4], ALU.add,
                                                    ALU.subtract))
            for name in ("dk", "dv", "dq"):
                dve_idle_layer(name)
            for t in range(2):
                W = P + t * P
                past = cst("past2", t=c2, lo=t * SEQ, n=W)
                for n in range(4):
                    for c in range(2):
                        name = f"ds{t}_{n}_{c}"
                        b = full(dve, name)
                        is_free(nc.vector.scalar_tensor_tensor(lm2[:, 4 * n + c:4 * n + c + 3:2, 0:W],
                                                               wide(b[:], SEQ)[:, :, 0:W], 64 ** -0.5, bc(past, 2),
                                                               ALU.mult, ALU.add), name)
                for n in range(2, 4):
                    for c in range(2):
                        after(dve, f"ds{t}_{n}_{c}")
                nc.vector.tensor_reduce(rmax[:].unsqueeze(2), lm2[:, :, 0:W], AX.X, ALU.max, negate=True)\
                    .then_inc(S("rmax2"), 1)
                dve.wait_ge(S("exp2"), t + 1)
                own.link(nc.vector.reciprocal(rinv[:], rsum[:]))
                odd = rinv[:].rearrange("p (n c) -> p n c", c=2)[:, :, 1:2]
                own.link(nc.vector.tensor_scalar(rinv2[:, 0:8].unsqueeze(2), odd, lamt[:, 4:5], None, ALU.mult))
                if t:
                    full(dve, "dt0_7")
                for hh in range(H1):
                    own.link(nc.vector.tensor_scalar(lm2[:, 2 * hh + 1, 0:W], lm2[:, 2 * hh + 1, 0:W],
                                                     rinv2[:, hh:hh + 1], None, ALU.mult))
                    nc.vector.scalar_tensor_tensor(am[:, hh, 0:W], lm2[:, 2 * hh, 0:W], rinv[:, 2 * hh:2 * hh + 1],
                                                   lm2[:, 2 * hh + 1, 0:W], ALU.mult, ALU.subtract).then_inc(S("am"), 1)
            head_norm_dve(dve, own, "nd")
            own.link(nc.vector.scalar_tensor_tensor(do[:], do[:], 1.0 - LAMBDA_INIT, rn2[:], ALU.mult, ALU.mult))
            nc.vector.tensor_scalar(do[:], do[:], pcol("subln"), None, ALU.mult).then_inc(S("dodone"), 1)
            dve.wait_ge(S("dohi"), 1)
            nc.vector.tensor_tensor(ylo[:], do[:], yhi[:].bitcast(F32), ALU.subtract).then_inc(S("dolo"), 1)
            dve_idle_layer("do")
            dve_post(dve, own, "postdiff", "b_post")
            dve_ffn(dve, own, 1)

        def dve_ffn(dve, own, k):
            dve_pre(dve, own, f"ffn{k}", f"f_pre{k}", xhi, xlo)

            def conv(s0, it, j):
                u0 = pair_first[f"fu{k}"] + j
                p = s0 % 2
                dve.wait_ge(S("f_tap"), k * FT2 + j + 1 + 4 * it)
                for tap in (1, 0):
                    sh = 2 - tap
                    for t in range(2):
                        col = (t * FT2 + j) * 3 + tap + 12 * it
                        ins = nc.vector.scalar_tensor_tensor(
                            ft[:, p, t, sh:SEQ], PS[u0 % 2][:, t, 0:SEQ - sh], pdyn(f"f_conv{k}", col),
                            ft[:, p, t, sh:SEQ], ALU.mult, ALU.add)
                    if tap:
                        own.link(ins)
                ins.then_inc(pair_free[u0 % 2], 1)
                load_lo(s0 + 2, it)
            slots(dve, f"fu{k}", conv, chain=own, links=1)
            dve_idle_layer(f"fd{k}")
            dve_post(dve, own, f"postffn{k}", f"f_post{k}")


        def pe_norm(pe, name, wait_for_squares=True):
            src, T = norm_view(name)
            b = fill("norm_" + name)
            if wait_for_squares:
                pe.wait_ge(S("sq_" + name), 1)
            for kt in range(KT):
                ins = nc.tensor.matmul(b[:, 0:T], ones[:], sq[:, kt, 0:T], start=kt == 0, stop=kt == KT - 1)
            is_full(ins, "norm_" + name)

        def pe_post(pe, name, layer):
            last = pair_first[layer] + dict(STREAM)[layer] // GROUP.get(layer, 1) - 1
            pair_done(pe, last - 1)
            pair_done(pe, last)
            pe_norm(pe, name, False)

        def pe_body(pe):
            pe.wait_ge(set_up, 1)
            pe_norm(pe, "mix")
            pe.wait_ge(S("xlo_mix"), 2)
            slot_in(0, 0)
            feature_slot(0, 0, xhi, xlo, tiles=(0,))
            for c, (t0, m) in enumerate(CHUNKS):
                ins = token_slot(0, PS[0][0:m, 1, 32 * c:32 * c + 24], xhi, xlo, slice(P, P + 24), m, t0)
            ins.then_inc(slot_done, 1)
            pe_layer("qkv", xhi, xlo, lead=4)
            pe_layer("iq", xhi, xlo)
            s, u = FIRST["av"], pair_first["av"]
            slot_in(s, 0)
            pair_in(u, 0, 0)
            for c, (t0, m) in enumerate(CHUNKS):
                out = PS[u % 2][0:m, c, 0:NCOL] if c < 2 else PS[u % 2][0:m, 0, NCOL:2 * NCOL]
                ins = token_slot(s, out, xhi, xlo, slice(0, NCOL), m, t0)
            ins.then_inc(slot_done, 1)
            pe_layer("ak", xhi, xlo)
            pe_layer("aq", xhi, xlo)
            pe.wait_ge(c1_in, 16)
            for name, x, W, c, sn, t0 in rotations():
                turn = cst("turni" if c == "cosi" else "turna")
                if name == "rot_ik":
                    pair_done(pe, 0)
                elif name[:6] == "rot_iq":
                    pair_done(pe, pair_first["iq"] + int(name[6:]))
                elif name[:6] == "rot_ak":
                    pair_done(pe, pair_first["ak"])
                else:
                    pair_done(pe, pair_first["aq"] + int(name[6:]))
                b = fill(name)
                for n in range(x.shape[1]):
                    ins = nc.tensor.matmul(b[:, n * W:n * W + W], turn, x[:, n], start=True, stop=True)
                is_full(ins, name)
            if upto == "A":
                return
            for t in range(2):
                W = META + P + t * P
                if t == 0:
                    pe.wait_ge(S("rope"), 3)
                for hh in range(H1):
                    b = fill(f"idx{t}_{hh}")
                    r = slice(64 * (hh % 2), 64 * (hh % 2) + 64)
                    is_full(nc.tensor.matmul(b[:, 0:W], iq[r, hh // 2, t * P:t * P + P], ik[r, 0:W], start=True,
                                             stop=True), f"idx{t}_{hh}")
                if t == 0:
                    pe.wait_ge(S("rope"), 9)
                for hh in range(H1):
                    b = fill(f"log{t}_{hh}")
                    is_full(nc.tensor.matmul(b[:, 0:W], aq[:, hh, t * P:t * P + P], ak[:, hh // 4, 0:W], start=True,
                                             stop=True), f"log{t}_{hh}")
                pe.wait_ge(S("prob"), t + 1)
                for hh in range(H1 + 1):
                    if hh < H1:
                        b = fill(f"tr{t}_{hh}")
                        for c, (t0, m) in enumerate(CHUNKS):
                            if c == 1 and t == 0:
                                continue
                            ins = nc.tensor.transpose(b[0:m, c * P:c * P + P], prob[:, hh, t0:t0 + m], ident)
                        is_full(ins, f"tr{t}_{hh}")
                    if hh:
                        g = hh - 1
                        after(pe, f"tr{t}_{g}")
                        name = f"pv{t}_{g // 4}"
                        b = fill(name) if g % 4 == 0 else AUX[USE[name][0]]
                        cs = [c for c in range(3) if t or c != 1]
                        for c in cs:
                            m = CHUNKS[c][1]
                            ins = nc.tensor.matmul(b[:, (g % 4) * P:(g % 4) * P + P],
                                                   av[0:m, c, (g // 4) * P:(g // 4) * P + P], pT[0:m, g % 2, c],
                                                   start=c == 0, stop=c == 2)
                        if g % 4 == 3:
                            is_full(ins, name)
                        else:
                            ins.then_inc(S("pv_mm"), 1)
            if upto == "B":
                return
            for name in ("z", "ga", "gb"):
                pe_layer(name, xhi, xlo)
            pe.wait_ge(S("ylo"), 1)
            pe_layer("wbd", yhi, ylo)
            if upto == "C":
                return
            pe_gdn(pe)
            if upto == "D":
                return
            pe.wait_ge(S("ygdn_lo"), 1)
            pe_layer("wbg", yhi, ylo)
            pe.wait_ge(S("mlo"), 4)
            pe_layer("wout", xhi[:, :, 0:SEQ], xlo[:, :, 0:SEQ])
            pe_post(pe, "postmix", "wout")
            pe_norm(pe, "mlp")
            pe.wait_ge(S("xlo_mlp"), 2)
            pe_layer("up", xhi[:, :, 0:SEQ], xlo[:, :, 0:SEQ])
            pe.wait_ge(S("ulo"), 16)
            pe_groups("down", uhi, ulo, 4, KT, 8)
            pe_post(pe, "postmlp", "down")
            if upto == "G":
                return
            pe_second(pe)

        def pe_gdn(pe):
            for w in range(2):
                pe.wait_ge(S("l2sq"), w + 1)
                for hh in range(H1):
                    b = fill(f"l2{'qk'[w]}{hh}")
                    is_full(nc.tensor.matmul(b[:, 0:T1], ones[:], sq[:, hh], start=True, stop=True), f"l2{'qk'[w]}{hh}")
            pe.wait_ge(S("bg"), 1)
            b = fill("sel")
            is_full(nc.tensor.matmul(b[:, 0:16], cst("spread", META), bg[0:META, 2, :], start=True, stop=True), "sel")
            pe.wait_ge(S("bcg"), 1)
            b = fill("cum")
            g = bcg[:, 1]
            nc.tensor.matmul(b[:, 0:16], cst("upper"), g[:, 0:16], start=True, stop=True)
            nc.tensor.matmul(b[:, 16:17], cst("upper16"), g[:, 16:17], start=True, stop=True)
            nc.tensor.matmul(b[:, 20:28], ones[:], g[:, 0:8], start=True, stop=True)
            is_full(nc.tensor.matmul(b[:, 28:29], cst("ones16"), g[:, 16:17], start=True, stop=True), "cum")
            pe.wait_ge(S("meta_kv"), 1)
            lev0 = 0
            for s, probs in enumerate(PROBLEMS):
                n, ng = len(probs), seg(probs)
                t0 = META + (s - 1) * P
                tok = slice(t0, t0 + P)

                def feat(base, q):
                    return qkv[:, base + q, tok] if s else og[:, base // 8 - 1, 0:P]
                for g in range(ng):
                    m = min(4, n - 4 * g)
                    b = fill(f"gb{s}_{g}")
                    for q in range(m):
                        j = probs[4 * g + q]
                        ins = nc.tensor.matmul(b[:, q * P:q * P + P], bcg[:, 1, j:j + 1].to_broadcast([P, P]),
                                               cst("upper" if s else "upper16"), start=True, stop=True)
                    is_full(ins, f"gb{s}_{g}")
                    b = fill(f"bb{s}_{g}")
                    for q in range(m):
                        j = probs[4 * g + q]
                        ins = nc.tensor.matmul(b[:, q * P:q * P + P], bcg[:, 0, j:j + 1].to_broadcast([P, P]), ident,
                                               start=True, stop=True)
                    is_full(ins, f"bb{s}_{g}")
                for g in range(ng):
                    m = min(4, n - 4 * g)
                    after(pe, f"bb{s}_{g}")
                    b = fill(f"kk{s}_{g}")
                    for q in range(m):
                        ins = nc.tensor.matmul(b[:, q * P:q * P + P], feat(8, 4 * g + q), kb[:, 4 * g + q], start=True,
                                               stop=True)
                    is_full(ins, f"kk{s}_{g}")
                    if s:
                        b = fill(f"qk{s}_{g}")
                        for q in range(m):
                            ins = nc.tensor.matmul(b[:, q * P:q * P + P], feat(8, 4 * g + q), feat(0, 4 * g + q),
                                                   start=True, stop=True)
                        is_full(ins, f"qk{s}_{g}")
                for g in range(ng):
                    m = min(4, n - 4 * g)
                    b = fill(f"vt{s}_{g}")
                    for q in range(m):
                        ins = nc.tensor.transpose(b[:, q * P:q * P + P], feat(16, 4 * g + q), ident)
                    is_full(ins, f"vt{s}_{g}")
                    if s < 2:
                        b = fill(f"kt{s}_{g}")
                        for q in range(m):
                            ins = nc.tensor.transpose(b[:, q * P:q * P + P], feat(8, 4 * g + q), ident)
                        is_full(ins, f"kt{s}_{g}")
                pe.wait_ge(S("at_ready"), s + 1)
                with pe.Fori(0, LEVELS[s]) as it:
                    pe.wait_ge(S("al_ready"), lev0 + 1 + it)
                    for g in range(ng):
                        m = min(4, n - 4 * g)
                        for k in range(-(-m // 2)):
                            ub = USE[f"y{s}_{2 * g + k}"]
                            pe.wait_ge(aux_free[ub[0]], ub[1] - ub[2] + it * ub[2])
                        b = fill(f"x{s}_{g}", it)
                        for q in range(m):
                            p_ = 4 * g + q
                            ins = nc.tensor.matmul(b[:, q * P:q * P + P], al[:, p_], tu[:, p_ // 2, p_ % 2], start=True,
                                                   stop=True)
                        is_full(ins, f"x{s}_{g}")
                    for g in range(-(-n // 2)):
                        m = min(2, n - 2 * g)
                        after(pe, f"x{s}_{g // 2}", it)
                        b = fill(f"y{s}_{g}", it)
                        for q in range(m):
                            p_ = 2 * g + q
                            nc.tensor.matmul(b[:, q * P:q * P + P], tu[:, g, 2 + q], xs[:, p_], start=True, stop=True)
                            ins = nc.tensor.matmul(b[:, (2 + q) * P:(3 + q) * P], xs[:, p_], tu[:, g, 2 + q], start=True,
                                                   stop=True)
                        is_full(ins, f"y{s}_{g}")
                lev0 += LEVELS[s]
                ylast = range(-(-n // 2))
                if s:
                    pe.wait_ge(S("ke"), s)
                    for g in range(2):
                        after(pe, f"s{s - 1}_{g}")
                        b = fill(f"r{s}_{g}")
                        for q in range(4):
                            ins = nc.tensor.matmul(b[:, q * P:q * P + P], kb[:, 4 * g + q], st[:, 4 * g + q], start=True,
                                                   stop=True)
                        is_full(ins, f"r{s}_{g}")
                for g in range(ng):
                    m = min(4, n - 4 * g)
                    for k in range(-(-m // 2)):
                        ub = USE[f"y{s}_{2 * g + k}"]
                        pe.wait_ge(aux_free[ub[0]], ub[1] + (LEVELS[s] - 1) * ub[2])
                    if s:
                        after(pe, f"r{s}_{g}")
                    else:
                        after(pe, "vt0_0")
                    b = fill(f"v{s}_{g}")
                    for q in range(m):
                        p_ = 4 * g + q
                        ins = nc.tensor.matmul(b[:, q * P:q * P + P], tu[:, p_ // 2, 2 + p_ % 2], vb[:, p_], start=True,
                                               stop=True)
                    is_full(ins, f"v{s}_{g}")
                if s == 0:
                    pe.wait_ge(S("ktm"), 1)
                for g in range(2):
                    after(pe, f"v{s}_{g if s else 0}")
                    if s:
                        b = fill(f"o{s}_{g}")
                        for q in range(4):
                            hh = 4 * g + q
                            nc.tensor.matmul(b[:, q * P:q * P + P], st[:, hh], feat(0, hh), start=True, stop=False)
                            ins = nc.tensor.matmul(b[:, q * P:q * P + P], vn[:, hh], att[:, hh], start=False, stop=True)
                        is_full(ins, f"o{s}_{g}")
                    if s < 2:
                        b = fill(f"s{s}_{g}")
                        for q in range(4):
                            hh = 4 * g + q
                            if s:
                                ins = nc.tensor.matmul(b[:, q * P:q * P + P], ktok[:, hh], vn[:, hh], start=True, stop=True)
                            else:
                                ins = nc.tensor.matmul(b[:, q * P:q * P + P], ktm[:, hh], vn[:, 0], start=True, stop=True)
                        is_full(ins, f"s{s}_{g}")
            pe.wait_ge(S("ogn"), 1)
            pe_head_norm(pe, "ng")

        def pe_head_norm(pe, use_name):
            for n in range(4):
                b = fill(f"{use_name}{n}")
                is_full(nc.tensor.matmul(b[:], ones[:], sq2[:, 2 * n:2 * n + 2], start=True, stop=True), f"{use_name}{n}")

        def pe_tokens(pe, name, hi, lo):
            def step(s0, it, j):
                u0 = pair_first[name] + j
                slot_in(s0, it)
                pair_in(u0, it, 2)
                for c in range(2):
                    ins = token_slot(s0, PS[u0 % 2][:, c, 0:NCOL], hi, lo, slice(0, NCOL), P, c * P)
                ins.then_inc(slot_done, 1)
            slots(pe, name, step)

        def pe_second(pe):
            x_hi, x_lo = xhi[:, :, 0:SEQ], xlo[:, :, 0:SEQ]
            pe_norm(pe, "ret")
            pe.wait_ge(S("xlo_ret"), 2)
            pe_layer("rq", x_hi, x_lo)
            pe_layer("rk", x_hi, x_lo)
            pe_tokens(pe, "rv", x_hi, x_lo)
            pe_layer("rg", x_hi, x_lo)
            pe.wait_ge(S("rqk"), 1)
            for hh in range(4):
                b = fill(f"rs{hh}")
                for e in range(2):
                    nc.tensor.matmul(b[:, 0:SEQ], rk[:, 2 * hh + e, 0:P], rq[:, 2 * hh + e], start=e == 0, stop=e == 1)
                for e in range(2):
                    ins = nc.tensor.matmul(b[:, SEQ:384], rk[:, 2 * hh + e, P:SEQ], rq[:, 2 * hh + e, P:SEQ],
                                           start=e == 0, stop=e == 1)
                is_full(ins, f"rs{hh}")
            pair_done(pe, pair_first["rv"] + 6)
            pair_done(pe, pair_first["rv"] + 7)
            for hh in range(4):
                after(pe, f"rs{hh}")
                for e in range(2):
                    b = fill(f"ro{hh}_{e}")
                    for q in range(2):
                        a = slice((4 * hh + 2 * e + q) * P, (4 * hh + 2 * e + q + 1) * P)
                        lo = slice(q * SEQ, q * SEQ + P)
                        up = slice(q * SEQ + P, (q + 1) * SEQ)
                        nc.tensor.matmul(b[:, lo], rv[:, 0, a], rp[:, hh, 0:P], start=True, stop=True)
                        nc.tensor.matmul(b[:, up], rv[:, 0, a], rp[:, hh, P:SEQ], start=True, stop=False)
                        ins = nc.tensor.matmul(b[:, up], rv[:, 1, a], rp[:, hh, SEQ:384], start=False, stop=True)
                    is_full(ins, f"ro{hh}_{e}")
                after(pe, f"ro{hh}_0")
                after(pe, f"ro{hh}_1")
                b = fill(f"rn{hh}")
                for e in range(4):
                    ins = nc.tensor.matmul(b[:, 0:SEQ], ones[:], rsq[:, hh % 2, e], start=e == 0, stop=e == 3)
                is_full(ins, f"rn{hh}")
            pe.wait_ge(S("rlo"), 4)
            pe_groups("ro", rhi, rlo, 2, KT, 4)
            pe_post(pe, "postret", "ro")
            pe_ffn(pe, 0)
            if upto == "I":
                return
            pe_norm(pe, "diff")
            pe.wait_ge(S("xlo_diff"), 2)
            pe_layer("dk", x_hi, x_lo)
            pe_tokens(pe, "dv", x_hi, x_lo)
            pe.wait_ge(S("xlo_diff"), 4)
            pe_layer("dq", x2hi, x2lo)
            pair_done(pe, pair_first["dq"] + 2)
            pair_done(pe, pair_first["dq"] + 3)
            for t in range(2):
                W = P + t * P
                for n in range(4):
                    for c in range(2):
                        b = fill(f"ds{t}_{n}_{c}")
                        r = slice(64 * c, 64 * c + 64)
                        for q in range(2):
                            ins = nc.tensor.matmul(b[:, q * SEQ:q * SEQ + W], dq[r, 2 * n + q, t * P:t * P + P],
                                                   dk[r, 2 * n + q, 0:W], start=True, stop=True)
                        is_full(ins, f"ds{t}_{n}_{c}")
                for hh in range(H1 + 1):
                    if hh < H1:
                        pe.wait_ge(S("am"), t * H1 + hh + 1)
                        b = fill(f"dt{t}_{hh}")
                        for c in range(1 + t):
                            ins = nc.tensor.transpose(b[:, c * P:c * P + P], am[:, hh, c * P:c * P + P], ident)
                        is_full(ins, f"dt{t}_{hh}")
                    if hh:
                        g = hh - 1
                        after(pe, f"dt{t}_{g}")
                        name = f"dp{t}_{g // 4}"
                        b = fill(name) if g % 4 == 0 else AUX[USE[name][0]]
                        for c in range(1 + t):
                            ins = nc.tensor.matmul(b[:, (g % 4) * P:(g % 4) * P + P], dv[:, c, g * P:g * P + P],
                                                   aT[:, g % 2, c], start=c == 0, stop=c == t)
                        if g % 4 == 3:
                            is_full(ins, name)
                        else:
                            ins.then_inc(S("dp_mm"), 1)
            pe.wait_ge(S("don"), 1)
            pe_head_norm(pe, "nd")
            pe.wait_ge(S("dolo"), 1)
            pe_layer("do", yhi, ylo)
            pe_post(pe, "postdiff", "do")
            pe_ffn(pe, 1)

        def pe_ffn(pe, k):
            pe_norm(pe, f"ffn{k}")
            pe.wait_ge(S(f"xlo_ffn{k}"), 2)
            pe_layer(f"fu{k}", xhi[:, :, 0:SEQ], xlo[:, :, 0:SEQ])
            pe.wait_ge(S("f_lo"), FT2 * (k + 1))
            pe_groups(f"fd{k}", fhi, flo, 3, FT2 - 2 * KT, 12)
            pe_post(pe, f"postffn{k}", f"fd{k}")

        @block.gpsimd
        def _(pool):
            own = Chain(pool, pool_own)
            nc.gpsimd.memset(ones[:], 1.0)
            nc.gpsimd.memset(eps[:, 0:1], EPS)
            nc.gpsimd.memset(eps[:, 1:2], P * EPS)
            nc.gpsimd.memset(small[:], 0.0).then_inc(set_up, 1)
            pool_body(pool, own)
            if upto:
                pool.memset(top8[:], 0.0).then_inc(S("end_pool"), 1)

        @block.scalar
        def _(act):
            act_body(act, Chain(act, act_own))
            if upto:
                act.copy(rsum[:, 0:1], ones[:, 0:1]).then_inc(S("end_act"), 1)

        @block.vector
        def _(dve):
            dve_body(dve, Chain(dve, dve_own))
            if upto:
                nc.vector.memset(top8[:, 0:1], 0.0).then_inc(S("end_dve"), 1)

        @block.tensor
        def _(pe):
            pe_body(pe)
            if upto:
                nc.tensor.wait_ge(aux_free[3], 1) if filled[3] and upto != "A" else None
                nc.tensor.matmul(AUX[3][0:1, 0:1], ones[:, 0:1], ones[:, 0:1], start=True, stop=True)\
                    .then_inc(S("end_pe"), 1)



def tiles_of(v):
    return np.ascontiguousarray(v.reshape(-1, P).T)


def slots_of(w):
    k, n = w.shape
    if k % D:
        w = np.concatenate([w, np.zeros((-k % D, n), w.dtype)])
        k = w.shape[0]
    return w.reshape(k // D, KT, P, n // NCOL, NCOL).transpose(3, 0, 2, 1, 4).reshape(-1, P, KT, NCOL)


def pairs_of(w):
    g, u = w[:, :FF2].reshape(D, FT2, P), w[:, FF2:].reshape(D, FT2, P)
    return slots_of(np.stack([g, u], 2).reshape(D, 2 * FF2))


def constants():
    f = np.float32
    i = np.arange(P)
    same16 = (i[:, None] // 16) == (i[None, :] // 16)
    up = i[:, None] <= i[None, :]
    c = {"ident": np.eye(P), "upper": up, "upper16": up & same16, "ones16": same16,
         "spread": (i[:, None] == i[None, :] % 16), "head": i[:, None] // 16 == np.arange(8)[None, :]}
    lev = []
    for n in range(NLEVEL):
        b = 1 << n
        col = i[None, :] // b
        lev.append(-((col % 2 == 1) & (i[:, None] // b == col - 1)).astype(f))
    c["levels"] = np.concatenate(lev, 1)
    pos = np.arange(T1, dtype=f)
    for tag, dim in (("a", 128), ("i", 64)):
        inv = (f(10000.0) ** (-np.arange(0, dim, 2, dtype=f) / f(dim))).astype(f)
        ang = pos[None, :] * inv[i % (dim // 2)][:, None]
        c["cos" + tag], c["sin" + tag] = np.cos(ang), np.sin(ang)
        turn = np.zeros((P, P), f)
        for m in range(P):
            lo = m % dim < dim // 2
            turn[m + dim // 2 if lo else m - dim // 2, m] = -1.0 if lo else 1.0
        c["turn" + tag] = turn
    past = [np.where(pos[None, :] <= (META + t * P + i)[:, None], 0.0, -BIG) for t in range(2)]
    c["past"] = np.concatenate(past, 1)
    p2 = np.arange(SEQ, dtype=f)
    inv = (f(1.0) / (f(10000.0) ** np.linspace(0.0, 1.0, P, dtype=f))).astype(f)
    ang = inv[:, None] * p2[None, :]
    c["rcos"], c["rsin"] = np.cos(ang), np.sin(ang)
    log_gamma = np.log1p(-np.power(2.0, -5.0 - np.arange(4)))
    rel = p2[None, :] - i[:, None]
    c["decay"] = np.concatenate([np.where(rel >= 0, np.exp(lg * np.maximum(rel, 0)) / 16.0, 0.0) for lg in log_gamma], 1)
    c["past2"] = np.concatenate([np.where(p2[None, :] <= (t * P + i)[:, None], 0.0, -BIG) for t in range(2)], 1)
    return (np.concatenate([np.asarray(c[n], f) for n, _ in CONST1], 1),
            np.concatenate([np.asarray(c[n], f) for n, _ in CONST2], 1))


def laid_out(v):
    w = v["w_in"][0]
    at = np.cumsum([0, 1024, 1024, 1024, 1024, 8, 8, 1024, 256, 256, 512, 64, 8, 1024, 1024])
    gq, gk, gv, gz, gb, ga, aq, ak, av, iq, ik, iw, gate_a, gate_b = (w[:, a:b] for a, b in zip(at[:-1], at[1:]))
    small = np.concatenate([ik, ik, gb, ga, iw, np.zeros((D, NCOL - 152), w.dtype)], 1)
    ain = v["a_w_in_2"][0]
    kv = v["w_kv_2"]
    parts = {"small": small, "qkv": w[:, 0:3072], "iq": iq, "av": av, "ak": ak, "aq": aq, "z": gz, "ga": gate_a,
             "gb": gate_b, "wbd": v["w_branch_dsa"][0], "wbg": v["w_branch_gdn"][0], "wout": v["w_out"][0],
             "up": v["w_up"][0], "down": v["w_down"][0], "rq": ain[:, 0:1024], "rk": ain[:, 1024:2048],
             "rv": ain[:, 2048:4096], "rg": ain[:, 4096:6144], "ro": v["a_w_out_2"][0],
             "fd0": v["ffn_w_down_2"][0], "fd1": v["ffn_w_down_2"][1], "dk": kv[:, 0:1024], "dv": kv[:, 1024:2048],
             "dq": v["b_w_q_2"][0], "do": v["b_w_out_2"][0]}
    made = []
    for name, count in STREAM:
        if name[:2] == "fu":
            s = pairs_of(v["ffn_w_up_2"][int(name[2])])
        else:
            s = slots_of(parts[name])
        assert s.shape[0] == count, (name, s.shape, count)
        made.append(s)
    cols = {"pre_mix": tiles_of(v["pre_mix_norm"][0]),
            "conv": v["conv_w"][0].reshape(4, 24, P).transpose(2, 1, 0).reshape(P, 96),
            "gdn": tiles_of(v["gdn_norm"][0]), "post_mix": tiles_of(v["post_mix_norm"][0]),
            "pre_mlp": tiles_of(v["pre_mlp_norm"][0]), "post_mlp": tiles_of(v["post_mlp_norm"][0]),
            "a_pre": tiles_of(v["a_norm_pre_2"][0]), "a_post": tiles_of(v["a_norm_post_2"][0]),
            "kv": tiles_of(v["kv_norm_2"]), "b_pre": tiles_of(v["b_norm_pre_2"][0]),
            "b_post": tiles_of(v["b_norm_post_2"][0]), "subln": tiles_of(v["b_subln_2"][0]),
            "alog": np.tile(v["a_log"][0][None], (P, 1)), "dtb": np.tile(v["dt_bias"][0][None], (P, 1)),
            "lam": np.tile(v["b_lambda_2"][0].reshape(1, 256), (P, 1))}
    for k in range(2):
        cols[f"f_pre{k}"] = tiles_of(v["ffn_norm_pre_2"][k])
        cols[f"f_post{k}"] = tiles_of(v["ffn_norm_post_2"][k])
        cols[f"f_conv{k}"] = v["ffn_conv_w_2"][k].reshape(3, 2 * FT2, P).transpose(2, 1, 0).reshape(P, -1)
        cols[f"f_bias{k}"] = tiles_of(v["ffn_conv_b_2"][k])
    c1, c2 = constants()
    x = np.concatenate([v["meta_tokens"], v["x"][0]], 0).T.reshape(KT, P, T1).transpose(1, 0, 2)
    return {"stream": np.concatenate(made), "params": np.concatenate([cols[n] for n, _ in PARAMS], 1),
            "const1": c1, "const2": c2, "x": x}


def kernel(**inputs):
    import concourse.bacc as bacc
    from concourse.bass_utils import run_bass_kernel_spmd as run

    v = {name: np.asarray(a) for name, a in inputs.items()}
    arrays = {"in_" + n: np.ascontiguousarray(a) for n, a in laid_out(v).items()}
    nc = bacc.Bacc("TRN2", target_bir_lowering=False, num_devices=1)
    args = {n[3:]: nc.dram_tensor(n, a.shape, F32, kind="ExternalInput").ap() for n, a in arrays.items()}
    out = nc.dram_tensor("out", (P, KT, SEQ), F32, kind="ExternalOutput").ap()
    program(nc, args["stream"], args["params"], args["const1"], args["const2"], args["x"], out)
    r = run(nc, [arrays], core_ids=[0])
    y = r.results[0]["out"]
    return y.transpose(2, 1, 0).reshape(1, SEQ, D)
```

```python
import math
from contextlib import ExitStack

import numpy as np
import concourse.bass as bass
from concourse import mybir

F32 = mybir.dt.float32
F32R = mybir.dt.float32r
ALU = mybir.AluOpType
ACT = mybir.ActivationFunctionType
AX = mybir.AxisListType

P = 128
D = 1024
KT = D // P
NCOL = 256
SLOT = KT * NCOL
META = 16
SEQ = 256
T1 = META + SEQ
H1 = 8
TOPK = 64
ROUNDS = TOPK // 8
IDX_SCALE = (8 * 64) ** -0.5
ATT_SCALE = 128 ** -0.5
EPS = 1e-6
FF1 = 4096
FF2 = 2816
FT2 = FF2 // P
LAMBDA_INIT = 0.8 - 0.6 * math.exp(-0.3)
BIG = 1e30
TAKEN = -3e38

STREAM = [("small", 1), ("qkv", 12), ("iq", 2), ("av", 1), ("ak", 1), ("aq", 4), ("gb", 4), ("z", 4),
          ("ga", 4), ("wbd", 4), ("wbg", 4), ("wout", 4), ("up", 16), ("down", 16), ("rq", 4), ("rk", 4),
          ("rv", 8), ("rg", 8), ("ro", 8), ("fu0", 22), ("fd0", 12), ("dk", 4), ("dv", 4), ("dq", 4),
          ("do", 4), ("fu1", 22), ("fd1", 12)]
FIRST = {}
_at = 0
for _name, _count in STREAM:
    FIRST[_name] = _at
    _at += _count
NSLOT = _at

PARAMS = [("pre_mix", 8), ("conv", 96), ("gdn", 1), ("post_mix", 8), ("pre_mlp", 8), ("post_mlp", 8),
          ("a_pre", 8), ("a_post", 8), ("kv", 8), ("b_pre", 8), ("b_post", 8), ("subln", 1),
          ("f_pre0", 8), ("f_pre1", 8), ("f_post0", 8), ("f_post1", 8),
          ("f_conv0", 3 * 2 * FT2), ("f_conv1", 3 * 2 * FT2), ("f_bias0", 2 * FT2), ("f_bias1", 2 * FT2),
          ("alog", 8), ("dtb", 8), ("lam", 256)]
PCOL = {}
_at = 0
for _name, _count in PARAMS:
    PCOL[_name] = _at
    _at += _count
NPAR = _at

CONST1 = [("ident", 128), ("window", 32), ("upper", 128), ("upper16", 128), ("ones16", 128), ("spread", 128), ("head", 8),
          ("levels", 7 * 128), ("cosa", T1), ("sina", T1), ("cosi", T1), ("sini", T1), ("turna", 128),
          ("turni", 128), ("past", 2 * T1)]
CONST2 = [("rcos", SEQ), ("rsin", SEQ), ("decay", 4 * SEQ), ("past2", 2 * SEQ)]
CCOL = {}
_at = 0
for _name, _count in CONST1:
    CCOL[_name] = _at
    _at += _count
NC1 = _at
_at = 0
for _name, _count in CONST2:
    CCOL[_name] = _at
    _at += _count
NC2 = _at
NLEVEL = 7
GATE_SLOTS = [(name, j) for name in ("gb", "z", "ga") for j in range(4)]
CHUNKS = [(META, P), (META + P, P), (0, META)]


class Chain:

    def __init__(self, eng, sem):
        self.eng, self.sem, self.n = eng, sem, 0

    def link(self, ins):
        ins.then_inc(self.sem, 1)
        self.n = self.n + 1
        self.eng.wait_ge(self.sem, self.n)


def slots(eng, name, step, body=4, chain=None, links=0, lead=0):
    first, count = FIRST[name], dict(STREAM)[name]
    for j in range(lead):
        step(first + j, 0, j)
    loops = (count - lead) // body if count - lead >= 2 * body else 0
    if loops:
        before = chain.n if chain else 0
        with eng.Fori(0, loops) as it:
            if chain:
                chain.n = before + it * (links * body)
            for j in range(lead, lead + body):
                step(first + j, it, j)
        if chain:
            chain.n = before + loops * links * body
    for j in range(lead + loops * body, count):
        step(first + j, 0, j)


def program(nc, stream, params, const1, const2, x_in, y_out, upto=None, dumps=()):
    ctx = ExitStack()
    with ctx:
        base = -(-nc.sbuf_base // 64) * 64
        arena = ctx.enter_context(nc.sbuf_tensor("arena", [P, (nc.sbuf_usable_end - base) // 4 - 32], F32))
        del arena

        def at(name, off, shape, dt=F32):
            return nc.alloc_sbuf_tensor_at(name, shape, dt, offset=base + off)

        RAW_N = 4
        raw = at("raw", 0, [P, RAW_N, KT, NCOL])
        wlo = at("wlo", 0, [P, RAW_N, KT, NCOL], F32R)
        whi = at("whi", 32768, [P, RAW_N, KT, NCOL], F32R)
        par = at("par", 65536, [P, NPAR])
        cursor = [65536 + 4 * NPAR]

        def nxt(name, shape):
            cursor[0] = -(-cursor[0] // 32) * 32
            t = at(name, cursor[0], shape)
            cursor[0] += 4 * int(np.prod(shape[1:]))
            return t

        ones = nxt("ones", [P, P])
        eps = nxt("eps", [P, 2])
        small = nxt("small", [P, 3, 24])
        bg = nxt("bg", [P, 3, 16])
        gtmp = nxt("gtmp", [P, 3, 3, 8])
        bcg = nxt("bcg", [P, 2, 17])
        gcum = nxt("gcum", [P, 17])
        sel16 = nxt("sel16", [P, 16])
        ktsc = nxt("ktsc", [P, 9])
        egl = nxt("egl", [P, 8])
        lamt = nxt("lamt", [P, 8])
        aexp = nxt("aexp", [P, 8])
        wix = nxt("wix", [P, 2, 8])
        rmax = nxt("rmax", [P, 16])
        rsum = nxt("rsum", [P, 16])
        rinv = nxt("rinv", [P, 16])
        top8 = nxt("top8", [P, 8])
        rinv2 = nxt("rinv2", [P, 16])
        rstd = nxt("rstd", [P, T1])
        rhead = rstd[0:16]
        PC = -(-cursor[0] // 64) * 64
        c1 = at("c1", PC, [P, NC1])
        c2 = at("c2", PC + 640, [P, NC2])
        HB = PC + 4 * NC1
        h = at("h", HB, [P, KT, T1])
        B = HB + 8704
        xhi = at("xhi", B, [P, KT, T1], F32R)
        xlo = at("xlo", B + 8704, [P, KT, T1], F32R)
        qkv = at("qkv", B + 17408, [P, 24, T1])
        aq = at("aq", B + 43520, [P, 8, SEQ])
        ak = at("ak", B + 51712, [P, 2, T1])
        av = at("av", B + 53888, [P, 3, NCOL])
        iq = at("iq", B + 56960, [P, 4, SEQ])
        ik = at("ik", B + 61056, [P, T1])
        ctmp = at("ctmp", B + 62144, [P, 2, 2, T1])
        lm = at("lm", B + 62144, [P, 8, T1])
        ibias = at("ibias", B + 70848, [P, T1])
        iscore = at("iscore", B + 71936, [P, T1])
        iwork = at("iwork", B + 73024, [P, T1])
        irelu = at("irelu", B + 74112, [P, 2, T1])
        zs = at("zs", B + 76288, [P, 8, SEQ])
        gas = at("gas", B + 84480, [P, 8, SEQ])
        gbs = at("gbs", B + 92672, [P, 8, SEQ])
        shi = at("shi", B + 43520, [P, 8, SEQ], F32R)
        slo = at("slo", B + 51712, [P, 8, SEQ], F32R)
        m1 = at("m1", B + 59904, [P, 8, SEQ])
        yo = at("yo", B + 101376, [P, 8, SEQ])
        pT = at("pT", B + 109568, [P, 2, 3, P])
        rtmp = at("rtmp", B + 62144, [P, 8, SEQ])
        xf = at("xf", B + 83968, [P, KT, T1])
        sq = at("sq", B + 92672, [P, KT, T1])
        sqb = at("sqb", B + 101376, [P, 8, T1])
        kb = at("kb", B + 43520, [P, 8, P])
        att = at("att", B + 47616, [P, 8, P])
        at_ = at("at_", B + 51712, [P, 8, P])
        al = at("al", B + 55808, [P, 8, P])
        eg = at("eg", B + 68096, [P, 8, P])
        dm = at("dm", B + 72192, [P, 8, P])
        tu = at("tu", B + 92672, [P, 4, 4, P])
        xs = at("xs", B + 101376, [P, 8, P])
        vb = at("vb", B + 105472, [P, 8, P])
        ktok = at("ktok", B, [P, 8, P])
        vn = at("vn", B + 4096, [P, 8, P])
        st = at("st", B + 8192, [P, 8, P])
        ktm = at("ktm", B + 12288, [P, 8, P])
        og = at("og", B + 109568, [P, 8, SEQ])
        gsq = at("gsq", B + 43520, [P, 8, SEQ])
        ghi = at("ghi", B + 92672, [P, 8, SEQ], F32R)
        glo = at("glo", B + 100864, [P, 8, SEQ], F32R)
        merged = at("merged", B + 51712, [P, 8, SEQ])
        rt = at("rt", B + 82944, [P, 2, 2, SEQ])
        ut = at("ut", B + 87040, [P, 2, 2, SEQ])
        uhi = at("uhi", B + 17408, [P, 32, SEQ], F32R)
        ulo = at("ulo", B + 50176, [P, 32, SEQ], F32R)
        rq = at("rq", B + 17408, [P, 8, SEQ])
        rk = at("rk", B + 25600, [P, 8, SEQ])
        rv = at("rv", B + 33792, [P, 2, 2048])
        rg = at("rg", B + 50176, [P, 16, SEQ])
        rp = at("rp", B + 66560, [P, 4, 384])
        ro = at("ro", B + 72704, [P, 16, SEQ])
        rsq = at("rsq", B + 89088, [P, 2, 4, SEQ])
        rrn = at("rrn", B + 97280, [P, 2, SEQ])
        rt1 = at("rt1", B + 99328, [P, 2, SEQ])
        rt2 = at("rt2", B + 101376, [P, 2, SEQ])
        rhi = at("rhi", B, [P, 16, SEQ], F32R)
        rlo = at("rlo", B + 17408, [P, 16, SEQ], F32R)
        fhi = at("fhi", B + 17408, [P, FT2, SEQ], F32R)
        flo = at("flo", B + 39936, [P, FT2, SEQ], F32R)
        ft = at("ft", B + 62464, [P, 2, 2, SEQ])
        fs = at("fs", B + 66560, [P, 2, SEQ])
        fu = at("fu", B + 68608, [P, 2, SEQ])
        x2hi = at("x2hi", B + 17408, [P, 8, SEQ], F32R)
        x2lo = at("x2lo", B + 25600, [P, 8, SEQ], F32R)
        dk = at("dk", B + 33792, [P, 8, SEQ])
        dq = at("dq", B + 41984, [P, 8, SEQ])
        dv = at("dv", B + 50176, [P, 2, 1024])
        lm2 = at("lm2", B + 58368, [P, 16, SEQ])
        am = at("am", B + 74752, [P, 8, SEQ])
        aT = at("aT", B + 84992, [P, 2, 2, P])
        do = at("do", B + 17408, [P, 8, SEQ])
        dsq = at("dsq", B + 92672, [P, 8, SEQ])
        dhi = at("dhi", B + 76288, [P, 8, SEQ], F32R)
        dlo = at("dlo", B + 84480, [P, 8, SEQ], F32R)
        HEADS = {"ng": (og, gsq, ghi, glo), "nd": (do, dsq, dhi, dlo)}

        PS = [ctx.enter_context(nc.psum_tensor(f"lin{n}", [P, 2, 512], F32)) for n in range(2)]
        AUX = [ctx.enter_context(nc.psum_tensor(f"aux{n}", [P, 512], F32)) for n in range(4)]

        def sem(name):
            return ctx.enter_context(nc.semaphore(name))

        w_loaded = [sem(f"w_loaded{r}") for r in range(RAW_N)]
        hi_ready = sem("hi_ready")
        lo_ready = sem("lo_ready")
        slot_done = sem("slot_done")
        pair_free = [sem(f"pair_free{n}") for n in range(2)]
        aux_full = [sem(f"aux_full{n}") for n in range(4)]
        aux_free = [sem(f"aux_free{n}") for n in range(4)]
        par_in = sem("par_in")
        c1_in = sem("c1_in")
        c2_in = sem("c2_in")
        x_loaded = sem("x_loaded")
        set_up = sem("set_up")
        out_done = sem("out_done")
        act_own = sem("act_own")
        dve_own = sem("dve_own")
        pool_own = sem("pool_own")
        named = {}

        def S(name):
            if name not in named:
                named[name] = sem(name)
            return named[name]

        filled = [0] * 4
        USE = {}

        def use(bank, *names):
            for name in names:
                filled[bank] += 1
                USE[name] = (bank, filled[bank], 0)

        def use_loop(count, banks_names):
            per = [0] * 4
            for bank, name in banks_names:
                per[bank] += 1
                USE[name] = (bank, filled[bank] + per[bank], 1)
            for bank, name in banks_names:
                USE[name] = (bank, USE[name][1], per[bank])
            for n in range(4):
                filled[n] += per[n] * count

        def fill(name, it=0):
            bank, n, per = USE[name]
            if n > 1 or per:
                nc.tensor.wait_ge(aux_free[bank], n - 1 + it * per)
            return AUX[bank]

        def is_full(ins, name):
            ins.then_inc(aux_full[USE[name][0]], 1)

        def full(eng, name, it=0):
            bank, n, per = USE[name]
            eng.wait_ge(aux_full[bank], n + it * per)
            return AUX[bank]

        def is_free(ins, name):
            ins.then_inc(aux_free[USE[name][0]], 1)

        def pcol(name, n=0, count=1):
            return par[:, PCOL[name] + n:PCOL[name] + n + count]

        def pdyn(name, n, count=1):
            return par[:, bass.ds(PCOL[name] + n, count)]

        def cst(name, rows=P, t=c1, lo=0, n=None):
            a = CCOL[name] + lo
            width = dict(CONST1 + CONST2)[name] - lo if n is None else n
            return t[0:rows, a:a + width]

        ident = cst("ident")

        use(2, "norm_mix")
        use(0, "rot_ik")
        use(1, "rot_iq0")
        use(2, "rot_iq1")
        use(3, "rot_ak0")
        use(0, "rot_ak1")
        for n in range(4):
            use((n + 1) % 4, f"rot_aq{n}")
        for name in ("idx0", "log0", "idx1"):
            for hh in range(H1):
                use(hh % 4, f"{name}_{hh}")
        for t in range(2):
            if t:
                for hh in range(H1):
                    use(hh % 4, f"log1_{hh}")
            for hh in range(H1):
                use(hh % 2, f"tr{t}_{hh}")
                if hh % 4 == 3:
                    use(2 + hh // 4, f"pv{t}_{hh // 4}")
        use(0, "l2sum")
        for hh in range(16):
            use((hh + 1) % 4, f"l2b{hh}")
        use(0, "sel")
        use(1, "cum")
        PROBLEMS = [[16], list(range(8)), list(range(8, 16))]
        LEVELS = [4, NLEVEL, NLEVEL]
        for s, probs in enumerate(PROBLEMS):
            ng = -(-len(probs) // 4)
            for g in range(ng):
                use(2 * g % 4, f"gb{s}_{g}")
                use((2 * g + 1) % 4, f"bb{s}_{g}")
            for g in range(ng):
                use(g, f"kk{s}_{g}")
                if s:
                    use(2 + g, f"qk{s}_{g}")
            for g in range(ng):
                use(g, f"vt{s}_{g}")
                if s < 2:
                    use(2 + g, f"kt{s}_{g}")
            if s:
                use_loop(LEVELS[s], [(0, f"x{s}_0"), (1, f"x{s}_1"), (2, f"y{s}_0"), (3, f"y{s}_1"),
                                     (0, f"y{s}_2"), (1, f"y{s}_3")])
            else:
                use_loop(LEVELS[s], [(0, f"x{s}_0"), (2, f"y{s}_0")])
            for g in range(ng):
                if s:
                    use(g, f"r{s}_{g}")
            for g in range(ng):
                use(2 + g, f"v{s}_{g}")
            for g in range(2):
                if s:
                    use(g, f"o{s}_{g}")
                if s < 2:
                    use(2 + g, f"s{s}_{g}")
        use(0, "ngsum")
        for n in range(4):
            use((n + 1) % 4, f"ng{n}")
        use(0, "norm_postmix")
        use(1, "norm_mlp")
        use(2, "norm_postmlp")
        use(3, "norm_ret")
        for hh in range(4):
            use(hh, f"rs{hh}")
        for hh in range(4):
            use(0, f"ro{hh}_0")
            use(1, f"ro{hh}_1")
            use(2 + hh % 2, f"rn{hh}")
        use(0, "norm_postret")
        use(1, "norm_ffn0")
        use(2, "norm_postffn0")
        use(3, "norm_diff")
        for t in range(2):
            for n in range(4):
                for c in range(2):
                    use(2 * (n % 2) + c, f"ds{t}_{n}_{c}")
            for hh in range(H1):
                use(hh % 2, f"dt{t}_{hh}")
                if hh % 4 == 3:
                    use(2 + hh // 4, f"dp{t}_{hh // 4}")
        use(0, "ndsum")
        for n in range(4):
            use((n + 1) % 4, f"nd{n}")
        use(0, "norm_postdiff")
        use(1, "norm_ffn1")
        use(2, "norm_postffn1")

        def load_hi(s0, it):
            if s0 >= NSLOT:
                return
            nc.scalar.wait_ge(w_loaded[s0 % 4], 16 * (s0 // 4 + 1) + 16 * it)
            if s0 >= RAW_N:
                nc.scalar.wait_ge(slot_done, s0 - RAW_N + 1 + 4 * it)
            nc.scalar.copy(whi[:, s0 % 4], raw[:, s0 % 4]).then_inc(hi_ready, 1)

        def load_lo(s0, it):
            if s0 >= NSLOT:
                return
            nc.vector.wait_ge(hi_ready, s0 + 1 + 4 * it)
            nc.vector.tensor_tensor(wlo[:, s0 % 4], raw[:, s0 % 4], whi[:, s0 % 4].bitcast(F32),
                                    ALU.subtract).then_inc(lo_ready, 1)

        def slot_in(s0, it):
            nc.tensor.wait_ge(lo_ready, s0 + 1 + 4 * it)

        def pair_in(u0, it, per):
            if u0 >= 2:
                nc.tensor.wait_ge(pair_free[u0 % 2], u0 // 2 + it * per)

        def mm3(out, s0, kt, cols, hi, lo, start, stop, swap=False):
            wh, wl = whi[:, s0 % 4, kt, cols], wlo[:, s0 % 4, kt, cols]
            if swap:
                trio = ((hi, wh), (hi, wl), (lo, wh))
            else:
                trio = ((wh, hi), (wh, lo), (wl, hi))
            for n, (a, b) in enumerate(trio):
                ins = nc.tensor.matmul(out, a, b, start=start and n == 0, stop=stop and n == 2)
            return ins

        def feature_slot(s0, pair, hi, lo, tiles=(0, 1), kts=KT, k0=0, start=True, stop=True, ready=None):
            T = hi.shape[-1]
            for t in tiles:
                for kt in range(kts):
                    if ready and t == 0 and kt % 2 == 0:
                        nc.tensor.wait_ge(S(ready), kt // 2 + 1)
                    ins = mm3(PS[pair][:, t, 0:T], s0, kt, slice(t * P, t * P + P), hi[:, k0 + kt], lo[:, k0 + kt],
                              start and kt == 0, stop and kt == kts - 1)
            return ins

        def token_slot(s0, out, hi, lo, cols, m, t0):
            for kt in range(KT):
                ins = mm3(out, s0, kt, cols, hi[:, kt, t0:t0 + m], lo[:, kt, t0:t0 + m], kt == 0, kt == KT - 1,
                          swap=True)
            return ins

        GROUP = {"down": 4, "ro": 2, "fd0": 3, "fd1": 3}
        pair_first = {}
        n = 0
        for name, count in STREAM:
            pair_first[name] = n
            n += count // GROUP.get(name, 1)

        def pe_layer(name, hi, lo, body=4, lead=0, ready=None, norm=None):
            def step(s0, it, j):
                u0 = pair_first[name] + j
                slot_in(s0, it)
                pair_in(u0, it, body // 2)
                feature_slot(s0, u0 % 2, hi, lo, ready=ready if j == 0 else None).then_inc(slot_done, 1)
                if norm and j:
                    pe_sum_squares(norm, u0 - 1, j - 1)
            slots(nc.tensor, name, step, body, lead=lead)

        def pe_groups(name, hi, lo, group, kts_last, body, norm=None):
            def step(s0, it, j):
                g = j % group
                u0 = pair_first[name] + j // group
                slot_in(s0, it * (body // 4))
                if g == 0:
                    pair_in(u0, it, body // group // 2)
                kts = kts_last if g == group - 1 else KT
                T = hi.shape[-1]
                for t in range(2):
                    for kt in range(kts):
                        ins = mm3(PS[u0 % 2][:, t, 0:T], s0, kt, slice(t * P, t * P + P), hi[:, g * KT + kt],
                                  lo[:, g * KT + kt], g == 0 and kt == 0, g == group - 1 and kt == kts - 1)
                ins.then_inc(slot_done, 1)
                if norm and g == 0 and j:
                    pe_sum_squares(norm, u0 - 1, j // group - 1)
            slots(nc.tensor, name, step, body)

        def pe_sum_squares(norm, u, g):
            b = fill("norm_" + norm) if g == 0 else AUX[USE["norm_" + norm][0]]
            nc.tensor.wait_ge(pair_free[u % 2], u // 2 + 1)
            for kt in (2 * g, 2 * g + 1):
                ins = nc.tensor.matmul(b[:, 0:SEQ], ones[:], sq[:, kt, 0:SEQ], start=kt == 0, stop=kt == KT - 1)
            if g == KT // 2 - 1:
                is_full(ins, "norm_" + norm)

        def bc(a, n):
            return a.unsqueeze(1).to_broadcast([a.shape[0], n, a.shape[1]])

        def wide(a, w):
            return a.rearrange("p (n w) -> p n w", w=w)

        def after(eng, name, it=0):
            bank, n, per = USE[name]
            eng.wait_ge(aux_free[bank], n + it * per)

        def pair_done(eng, u):
            eng.wait_ge(pair_free[u % 2], u // 2 + 1)

        hx = h[:, :, META:T1]

        def norm_view(name):
            return (h[:], T1) if name == "mix" else (hx, SEQ)

        def has(name):
            return name in FIRST

        def seg(probs):
            return (len(probs) + 3) // 4

        block = ctx.enter_context(nc.Block())

        @block.sync
        def _(sp):
            sp.dma_start(h[:], x_in).then_inc(x_loaded, 16)
            sp.dma_start(par[:], params).then_inc(par_in, 16)
            for s in range(4):
                sp.dma_start(raw[:, s], stream[s]).then_inc(w_loaded[s], 16)
            sp.dma_start(c1[:], const1).then_inc(c1_in, 16)
            with sp.Fori(1, NSLOT // 4) as it:
                for r in range(4):
                    sp.wait_ge(slot_done, it * 4 + (r - 3))
                    sp.dma_start(raw[:, r], stream[bass.ds(it * 4 + r, 1)].rearrange("o p k n -> (o p) k n")).then_inc(w_loaded[r], 16)
            for s in range(NSLOT // 4 * 4, NSLOT):
                sp.wait_ge(slot_done, s - 3)
                sp.dma_start(raw[:, s % 4], stream[s]).then_inc(w_loaded[s % 4], 16)
            if upto:
                for e in ("pe", "act", "dve", "pool"):
                    sp.wait_ge(S("end_" + e), 1)
                for n, (src, dst) in enumerate(dumps):
                    sp.dma_start(dst, eval_dump(src)).then_inc(out_done, 16)
                sp.wait_ge(out_done, 16 * len(dumps))
                return
            sp.wait_ge(S("h_postffn1"), 4)
            sp.dma_start(y_out, hx).then_inc(out_done, 16)
            sp.wait_ge(out_done, 16)

        scope = dict(locals())

        def eval_dump(src):
            return src(scope)


        def pool_body(pool, own):
            if upto in ("A", "B", "C"):
                return
            for s in range(FIRST["gb"] + 3, FIRST["wbd"] + 3):
                pool.wait_ge(lo_ready, s)
                pool.wait_ge(hi_ready, s + 1)
                nc.gpsimd.tensor_tensor(wlo[:, s % 4], raw[:, s % 4], whi[:, s % 4].bitcast(F32), ALU.subtract)\
                    .then_inc(lo_ready, 1)
            for s in range(3):
                npb = len(PROBLEMS[s])
                n = npb
                first = sum(LEVELS[:s])
                pool.wait_ge(S("at_ready"), s + 1)
                with pool.Fori(0, LEVELS[s]) as it:
                    after_x = USE[f"x{s}_{seg(PROBLEMS[s]) - 1}"]
                    if s == 0:
                        pool.wait_ge(aux_full[after_x[0]], after_x[1] - after_x[2] + it * after_x[2])
                    else:
                        pool.wait_ge(aux_full[after_x[0]], after_x[1] - after_x[2] + it * after_x[2])
                    lev = c1[:, bass.ds(it * P + CCOL["levels"], P)]
                    nc.gpsimd.tensor_tensor(al[:, 0:n], at_[:, 0:n], bc(lev, n), ALU.mult).then_inc(S("al_ready"), 1)
            if upto in ("D",):
                return
            pool.wait_ge(S("nglo"), 4)
            pool.dma_start(c2[:], const2).then_inc(c2_in, 16)
            for k in range(2):
                if not has(f"fu{k}"):
                    return
                def tail(s0, it, j):
                    n0 = k * FT2 + j
                    pool.wait_ge(S("f_silu"), n0 + 1 + 4 * it)
                    if n0 >= 2:
                        pool.wait_ge(S("f_hi"), n0 - 1 + 4 * it)
                    nc.gpsimd.tensor_tensor(fu[:, s0 % 2], fs[:, s0 % 2], ft[:, s0 % 2, 1], ALU.mult)\
                        .then_inc(S("f_prod"), 1)
                    pool.wait_ge(S("f_prod"), n0 + 1 + 4 * it)
                    pool.wait_ge(S("f_hi"), n0 + 1 + 4 * it)
                    nc.gpsimd.tensor_tensor(flo[:, bass.ds(j + 4 * it, 1)], fu[:, s0 % 2].unsqueeze(1),
                                            fhi[:, bass.ds(j + 4 * it, 1)].bitcast(F32), ALU.subtract).then_inc(S("f_lo"), 1)
                slots(pool, f"fu{k}", tail)


        def act_pre(act, name, hi, until=0, after_h=None):
            src, T = norm_view(name)
            for c in range(4):
                if after_h:
                    act.wait_ge(S(after_h), c + 1)
                a = slice(2 * c, 2 * c + 2)
                nc.scalar.activation(sq[:, a, 0:T], src[:, a], ACT.Square).then_inc(S("sq_" + name), 1)
            act_root(act, name, T)
            act_high(act, name, hi, T, until)

        def act_root(act, name, T):
            b = full(act, "norm_" + name)
            is_free(nc.scalar.activation(rstd[:, 0:T], b[:, 0:T], ACT.Sqrt, scale=1.0 / D, bias=eps[:, 0:1]),
                    "norm_" + name)

        def act_high(act, name, hi, T, until=0):
            if until:
                act.wait_ge(slot_done, until)
            for c in range(4):
                act.wait_ge(S("xf_" + name), c + 1)
                a = slice(2 * c, 2 * c + 2)
                nc.scalar.copy(hi[:, a, 0:T], xf[:, a, 0:T]).then_inc(S("xhi_" + name), 1)

        def act_layer_out(act, name):
            group = GROUP.get(name, 1)
            for j in range(dict(STREAM)[name]):
                s = FIRST[name] + j
                act.wait_ge(slot_done, s + 1)
                if j % group == group - 1:
                    g = j // group
                    u = pair_first[name] + g
                    nc.scalar.copy(yo[:, 2 * g:2 * g + 2], PS[u % 2][:, :, 0:SEQ])
                    nc.scalar.activation(sq[:, 2 * g:2 * g + 2, 0:SEQ], PS[u % 2][:, :, 0:SEQ], ACT.Square)\
                        .then_inc(pair_free[u % 2], 1)
                load_hi(s + 3, 0)

        def act_body(act, own):
            act.wait_ge(set_up, 1)
            act.wait_ge(x_loaded, 16)
            for c in range(4):
                a = slice(2 * c, 2 * c + 2)
                nc.scalar.activation(sq[:, a], h[:, a], ACT.Square).then_inc(S("sq_mix"), 1)
            load_hi(0, 0)
            act_root(act, "mix", T1)
            act_high(act, "mix", xhi, T1)
            load_hi(1, 0)
            load_hi(2, 0)
            act.wait_ge(slot_done, 1)
            nc.scalar.copy(ik[:], PS[0][:, 0, 0:T1])
            nc.scalar.copy(small[:, 0:2, :], wide(PS[0][:, 1, 0:64], 32)[:, :, 0:24])
            nc.scalar.copy(small[0:META, 2, :], PS[0][0:META, 1, 64:88]).then_inc(pair_free[0], 1)
            load_hi(3, 0)
            act.wait_ge(par_in, 16)

            def conv(s0, it, j):
                u0 = pair_first["qkv"] + j
                act.wait_ge(slot_done, s0 + 1 + 4 * it)
                for t in range(2):
                    col = (2 * j + t) * 4 + 3 + it * 32
                    ins = nc.scalar.activation(ctmp[:, u0 % 2, t], PS[u0 % 2][:, t, 0:T1], ACT.Copy,
                                               scale=pdyn("conv", col))
                ins.then_inc(S("conv_tap"), 1)
                load_hi(s0 + 3, it)
                act.wait_ge(pair_free[u0 % 2], u0 // 2 + 1 + 2 * it)
                nc.scalar.activation(qkv[:, bass.ds(2 * j + 8 * it, 2)], ctmp[:, u0 % 2], ACT.Silu)\
                    .then_inc(S("conv_silu"), 1)
            slots(act, "qkv", conv)
            for name, dst in (("iq", iq[:]), ("av", av[:]), ("ak", ak[:]), ("aq", aq[:])):
                for j in range(dict(STREAM)[name]):
                    s = FIRST[name] + j
                    u = pair_first[name] + j
                    act.wait_ge(slot_done, s + 1)
                    if name == "av":
                        nc.scalar.copy(av[:, 0:2], PS[u % 2][:, :, 0:NCOL])
                        nc.scalar.copy(av[0:META, 2], PS[u % 2][0:META, 0, NCOL:2 * NCOL]).then_inc(pair_free[u % 2], 1)
                    elif name == "ak":
                        nc.scalar.copy(ak[:], PS[u % 2][:, :, 0:T1]).then_inc(pair_free[u % 2], 1)
                    else:
                        nc.scalar.copy(dst[:, 2 * j:2 * j + 2], PS[u % 2][:, :, META:T1]).then_inc(pair_free[u % 2], 1)
                    load_hi(s + 3, 0)
            if upto == "A":
                return
            gates = {"gb": (gbs, ACT.Sigmoid), "z": (zs, ACT.Silu), "ga": (gas, ACT.Sigmoid)}

            def gate_out(n):
                name, j = GATE_SLOTS[n]
                dst, func = gates[name]
                s, u = FIRST[name] + j, pair_first[name] + j
                act.wait_ge(slot_done, s + 1)
                nc.scalar.activation(dst[:, 2 * j:2 * j + 2], PS[u % 2][:, :, META:T1], func)\
                    .then_inc(pair_free[u % 2], 1)
                load_hi(s + 3, 0)

            def relus(t):
                W = META + P + t * P
                for hh in range(H1):
                    b = full(act, f"idx{t}_{hh}")
                    n = t * H1 + hh
                    if n >= 2:
                        act.wait_ge(S("relu_used"), n - 1)
                    is_free(nc.scalar.activation(irelu[:, hh % 2, 0:W], b[:, 0:W], ACT.Relu), f"idx{t}_{hh}")

            gate_out(0)
            gate_out(1)
            relus(0)
            gate_out(2)
            gate_out(3)
            for t in range(2):
                W = META + P + t * P
                act.wait_ge(S("rmax"), t + 1)
                for hh in range(H1):
                    ins = nc.scalar.activation(lm[:, hh, 0:W], lm[:, hh, 0:W], ACT.Exp, bias=rmax[:, hh:hh + 1],
                                               accum_out=rsum[:, hh:hh + 1])
                ins.then_inc(S("exp"), 1)
                if t == 0:
                    relus(1)
                    gate_out(4)
                    gate_out(5)
                else:
                    gate_out(9)
                for hh in range(H1 + 1):
                    if hh == 4 and t == 0:
                        gate_out(6)
                    if hh < H1:
                        b = full(act, f"tr{t}_{hh}")
                        if hh >= 2 or t:
                            done = hh - 2 if hh >= 2 else hh + 6
                            if done % 4 == 3:
                                full(act, f"pv{t if hh >= 2 else t - 1}_{done // 4}")
                            else:
                                act.wait_ge(S("pv_mm"), pv_count(t if hh >= 2 else t - 1, done))
                        if t:
                            nc.scalar.copy(pT[:, hh % 2, 0:2], wide(b[:, 0:2 * P], P))
                        else:
                            nc.scalar.copy(pT[:, hh % 2, 0], b[:, 0:P])
                        is_free(nc.scalar.copy(pT[0:META, hh % 2, 2], b[0:META, 2 * P:3 * P]), f"tr{t}_{hh}")
                    if hh % 4 == 0 and hh:
                        g = hh // 4 - 1
                        b = full(act, f"pv{t}_{g}")
                        is_free(nc.scalar.copy(yo[:, 4 * g:4 * g + 4, t * P:t * P + P], wide(b[:], P)), f"pv{t}_{g}")
                if t == 0:
                    gate_out(7)
                    gate_out(8)
            for g in range(2):
                after(act, f"pv1_{g}")
                nc.scalar.copy(shi[:, 4 * g:4 * g + 4], yo[:, 4 * g:4 * g + 4]).then_inc(S("shi"), 1)
            gate_out(10)
            gate_out(11)
            for j in range(4):
                load_hi(FIRST["wbd"] + j + 3, 0)
            if upto == "C":
                return
            act_gdn(act, own)
            if upto == "D":
                return
            for name in ("wbg",):
                for j in range(4):
                    act.wait_ge(S("merged"), j + 1)
                    nc.scalar.copy(xhi[:, 2 * j:2 * j + 2, 0:SEQ], merged[:, 2 * j:2 * j + 2]).then_inc(S("mhi"), 1)
                    load_hi(FIRST[name] + j + 3, 0)
            act_layer_out(act, "wout")
            act_root(act, "postmix", SEQ)
            act_pre(act, "mlp", xhi, FIRST["up"], "h_postmix")

            def up(s0, it, j):
                u0 = pair_first["up"] + j
                act.wait_ge(slot_done, s0 + 1 + 4 * it)
                if j >= 2:
                    act.wait_ge(S("ulo"), j - 1 + 4 * it)
                own.link(nc.scalar.activation(rt[:, u0 % 2], PS[u0 % 2][:, :, 0:SEQ], ACT.Relu))
                nc.scalar.activation(uhi[:, bass.ds(2 * j + 8 * it, 2)], rt[:, u0 % 2], ACT.Square)\
                    .then_inc(pair_free[u0 % 2], 1)
                load_hi(s0 + 3, it)
            slots(act, "up", up, chain=own, links=1, lead=4)
            act_layer_out(act, "down")
            act_root(act, "postmlp", SEQ)
            if upto == "G":
                return
            act_second(act, own)

        def pv_count(t, hh):
            return t * 6 + (hh // 4) * 3 + hh % 4 + 1

        def act_gdn(act, own):
            pair_done(act, pair_first["wbd"] + 2)
            pair_done(act, pair_first["wbd"] + 3)
            for w, dst in enumerate((sq, sqb)):
                nc.scalar.activation(dst[:], qkv[:, 8 * w:8 * w + 8], ACT.Square).then_inc(S("l2sq"), 1)
            act_head_root(act, "l2sum", 16, T1, 1.0)
            nc.scalar.activation(bg[:, :, 0:8], small[:, :, 0:8], ACT.Sigmoid)
            nc.scalar.activation(aexp[:], pcol("alog", 0, 8), ACT.Exp)
            act.wait_ge(S("g_arg"), 1)
            own.link(nc.scalar.activation(gtmp[:, 1], gtmp[:, 0], ACT.Abs))
            own.link(nc.scalar.activation(gtmp[:, 1], gtmp[:, 1], ACT.Exp, scale=-1.0))
            nc.scalar.activation(gtmp[:, 1], gtmp[:, 1], ACT.Ln, bias=ones[:, 0:1]).then_inc(S("g_ln"), 1)
            act.wait_ge(S("ktsc"), 1)
            nc.scalar.activation(ktsc[:], ktsc[:], ACT.Exp)
            is_free(nc.scalar.activation(egl[:], AUX[USE["cum"][0]][:, 20:28], ACT.Exp), "cum")
            ndm = 0
            for s, probs in enumerate(PROBLEMS):
                n = len(probs)
                for g in range(seg(probs)):
                    m = min(4, n - 4 * g)
                    ndm += 1
                    act.wait_ge(S("dm_arg"), ndm)
                    name = f"gb{s}_{g}"
                    is_free(nc.scalar.activation(eg[:, 4 * g:4 * g + m], wide(AUX[USE[name][0]][:, 0:m * P], P), ACT.Exp),
                            name)
                    nc.scalar.activation(dm[:, 4 * g:4 * g + m], dm[:, 4 * g:4 * g + m], ACT.Exp)\
                        .then_inc(S("dm_exp"), 1)
                lev0 = sum(LEVELS[:s])
                with act.Fori(0, LEVELS[s]) as it:
                    for g in range(seg(probs)):
                        m = min(4, n - 4 * g)
                        b = full(act, f"x{s}_{g}", it)
                        is_free(nc.scalar.copy(xs[:, 4 * g:4 * g + m], wide(b[:, 0:m * P], P)), f"x{s}_{g}")
                for g in range(seg(probs)):
                    m = min(4, n - 4 * g)
                    b = full(act, f"v{s}_{g}")
                    is_free(nc.scalar.copy(vn[:, 4 * g:4 * g + m], wide(b[:, 0:m * P], P)), f"v{s}_{g}")
                for g in range(2):
                    if s:
                        b = full(act, f"o{s}_{g}")
                        is_free(nc.scalar.copy(og[:, 4 * g:4 * g + 4, (s - 1) * P:s * P], wide(b[:], P)), f"o{s}_{g}")
            head_norm_act(act, "ng")

        def act_head_root(act, name, heads, T, scale):
            b = full(act, name)
            is_free(nc.scalar.activation(rhead[0:heads, 0:T], b[0:heads, 0:T], ACT.Sqrt, scale=scale,
                                         bias=eps[0:heads, 0:1]), name)

        def head_norm_act(act, tag):
            for g in range(2):
                bank, n, _ = USE[f"o2_{g}" if tag == "ng" else f"dp1_{g}"]
                act.wait_ge(aux_free[bank], n)
            src, squares, hi, _ = HEADS[tag]
            nc.scalar.activation(squares[:], src[:], ACT.Square).then_inc(S(tag + "sq"), 1)
            act_head_root(act, tag + "sum", 8, SEQ, 1.0 / P)
            for n in range(4):
                act.wait_ge(S(tag + "f"), n + 1)
                a = slice(2 * n, 2 * n + 2)
                nc.scalar.copy(hi[:, a], src[:, a]).then_inc(S(tag + "hi"), 1)

        def act_second(act, own):
            act_pre(act, "ret", xhi, after_h="h_postmlp")
            for name in ("rq", "rk"):
                for j in range(4):
                    s = FIRST[name] + j
                    act.wait_ge(slot_done, s + 1)
                    load_hi(s + 3, 0)

            def values(s0, it, j):
                u0 = pair_first["rv"] + j
                act.wait_ge(slot_done, s0 + 1 + 4 * it)
                nc.scalar.copy(rv[:, :, bass.ds(j * NCOL + 4 * NCOL * it, NCOL)], PS[u0 % 2][:, :, 0:NCOL])\
                    .then_inc(pair_free[u0 % 2], 1)
                load_hi(s0 + 3, it)
            slots(act, "rv", values)

            def gate(s0, it, j):
                u0 = pair_first["rg"] + j
                act.wait_ge(slot_done, s0 + 1 + 4 * it)
                nc.scalar.activation(rg[:, bass.ds(2 * j + 8 * it, 2)], PS[u0 % 2][:, :, 0:SEQ], ACT.Silu)\
                    .then_inc(pair_free[u0 % 2], 1)
                load_hi(s0 + 3, it)
            slots(act, "rg", gate)
            for hh in range(4):
                if hh >= 2:
                    full(act, f"rn{hh - 2}")
                for e in range(2):
                    b = full(act, f"ro{hh}_{e}")
                    nc.scalar.copy(ro[:, 4 * hh + 2 * e:4 * hh + 2 * e + 2], wide(b[:], SEQ))
                    is_free(nc.scalar.activation(rsq[:, hh % 2, 2 * e:2 * e + 2], wide(b[:], SEQ), ACT.Square),
                            f"ro{hh}_{e}")
                b = full(act, f"rn{hh}")
                is_free(nc.scalar.activation(rrn[:, hh % 2], b[:, 0:SEQ], ACT.Sqrt, scale=1.0 / 512, bias=eps[:, 0:1]),
                        f"rn{hh}")
                act.wait_ge(S("ro_done"), hh + 1)
                nc.scalar.copy(rhi[:, 4 * hh:4 * hh + 4], ro[:, 4 * hh:4 * hh + 4]).then_inc(S("rhi"), 1)
            act_layer_out(act, "ro")
            act_root(act, "postret", SEQ)
            act_ffn(act, own, 0)
            if upto == "I":
                return
            act_pre(act, "diff", xhi, after_h="h_postffn0")
            for c in range(4):
                act.wait_ge(S("xf_diff"), 5 + c)
                a = slice(2 * c, 2 * c + 2)
                nc.scalar.copy(x2hi[:, a], xf[:, a, 0:SEQ]).then_inc(S("xhi_diff"), 1)
            act.wait_ge(S("lam"), 1)
            nc.scalar.activation(lamt[:, 2:4], lamt[:, 0:2], ACT.Exp).then_inc(S("lam_exp"), 1)
            for name in ("dk", "dv", "dq"):
                for j in range(4):
                    s, u = FIRST[name] + j, pair_first[name] + j
                    act.wait_ge(slot_done, s + 1)
                    if name == "dv":
                        nc.scalar.copy(dv[:, :, j * NCOL:(j + 1) * NCOL], PS[u % 2][:, :, 0:NCOL])\
                            .then_inc(pair_free[u % 2], 1)
                    else:
                        dst = dk if name == "dk" else dq
                        nc.scalar.copy(dst[:, 2 * j:2 * j + 2], PS[u % 2][:, :, 0:SEQ]).then_inc(pair_free[u % 2], 1)
                    load_hi(s + 3, 0)
            for t in range(2):
                W = P + t * P
                act.wait_ge(S("rmax2"), t + 1)
                for n in range(16):
                    ins = nc.scalar.activation(lm2[:, n, 0:W], lm2[:, n, 0:W], ACT.Exp, bias=rmax[:, n:n + 1],
                                               accum_out=rsum[:, n:n + 1])
                ins.then_inc(S("exp2"), 1)
                for hh in range(H1 + 1):
                    if hh < H1:
                        b = full(act, f"dt{t}_{hh}")
                        if hh >= 2 or t:
                            done = hh - 2 if hh >= 2 else hh + 6
                            if done % 4 == 3:
                                full(act, f"dp{t if hh >= 2 else t - 1}_{done // 4}")
                            else:
                                act.wait_ge(S("dp_mm"), pv_count(t if hh >= 2 else t - 1, done))
                        is_free(nc.scalar.copy(aT[:, hh % 2, 0:1 + t], wide(b[:, 0:W], P)), f"dt{t}_{hh}")
                    if hh % 4 == 0 and hh:
                        g = hh // 4 - 1
                        b = full(act, f"dp{t}_{g}")
                        is_free(nc.scalar.copy(do[:, 4 * g:4 * g + 4, t * P:t * P + P], wide(b[:], P)), f"dp{t}_{g}")
            head_norm_act(act, "nd")
            act_layer_out(act, "do")
            act_root(act, "postdiff", SEQ)
            act_ffn(act, own, 1)

        def act_ffn(act, own, k):
            act_pre(act, f"ffn{k}", xhi, FIRST[f"fu{k}"], ["h_postret", "h_postdiff"][k])

            def conv(s0, it, j):
                u0 = pair_first[f"fu{k}"] + j
                n0 = k * FT2 + j
                p = s0 % 2
                act.wait_ge(slot_done, s0 + 1 + 4 * it)
                if n0 >= 2:
                    act.wait_ge(S("f_prod"), n0 - 1 + 4 * it)
                for t in range(2):
                    ins = nc.scalar.activation(ft[:, p, t], PS[u0 % 2][:, t, 0:SEQ], ACT.Identity,
                                               scale=pdyn(f"f_conv{k}", (t * FT2 + j) * 3 + 2 + 12 * it),
                                               bias=pdyn(f"f_bias{k}", t * FT2 + j + 4 * it))
                ins.then_inc(S("f_tap"), 1)
                load_hi(s0 + 3, it)
                act.wait_ge(pair_free[u0 % 2], u0 // 2 + 1 + 2 * it)
                nc.scalar.activation(fs[:, p], ft[:, p, 0], ACT.Silu).then_inc(S("f_silu"), 1)
                act.wait_ge(S("f_prod"), n0 + 1 + 4 * it)
                nc.scalar.copy(fhi[:, bass.ds(j + 4 * it, 1)], fu[:, p].unsqueeze(1)).then_inc(S("f_hi"), 1)
            slots(act, f"fu{k}", conv)
            act_layer_out(act, f"fd{k}")
            act_root(act, f"postffn{k}", SEQ)


        def dve_scale_split(dve, name, gain, hi, lo, first=0):
            src, T = norm_view(name)

            def low(c):
                dve.wait_ge(S("xhi_" + name), first + c + 1)
                a = slice(2 * c, 2 * c + 2)
                nc.vector.tensor_tensor(lo[:, a, 0:T], xf[:, a, 0:T], hi[:, a, 0:T].bitcast(F32), ALU.subtract)\
                    .then_inc(S("xlo_" + name), 1)
            if first:
                dve.wait_ge(S("xlo_" + name), first)
            for c in range(4):
                for kt in (2 * c, 2 * c + 1):
                    ins = nc.vector.scalar_tensor_tensor(xf[:, kt, 0:T], src[:, kt], pcol(gain, kt), rstd[:, 0:T],
                                                         ALU.mult, ALU.mult)
                ins.then_inc(S("xf_" + name), 1)
                if c:
                    low(c - 1)
            low(3)

        def dve_pre(dve, own, name, gain, hi, lo):
            src, T = norm_view(name)
            after(dve, "norm_" + name)
            own.link(nc.vector.reciprocal(rstd[:, 0:T], rstd[:, 0:T]))
            dve_scale_split(dve, name, gain, hi, lo)

        def dve_post(dve, own, name, gain):
            after(dve, "norm_" + name)
            own.link(nc.vector.reciprocal(rstd[:, 0:SEQ], rstd[:, 0:SEQ]))
            for c in range(4):
                a = slice(2 * c, 2 * c + 2)
                for kt in (2 * c, 2 * c + 1):
                    ins = nc.vector.scalar_tensor_tensor(xf[:, kt, 0:SEQ], yo[:, kt], pcol(gain, kt), rstd[:, 0:SEQ],
                                                         ALU.mult, ALU.mult)
                own.link(ins)
                nc.vector.tensor_tensor(hx[:, a], hx[:, a], xf[:, a, 0:SEQ], ALU.add).then_inc(S("h_" + name), 1)
            dve.wait_ge(S("h_" + name), 4)

        def dve_idle_layer(name):
            def step(s0, it, j):
                load_lo(s0 + 3, it)
            slots(nc.vector, name, step, NSLOT if name == STREAM[-1][0] else 4)

        def dve_body(dve, own):
            dve.wait_ge(par_in, 16)
            load_lo(0, 0)
            dve_pre(dve, own, "mix", "pre_mix", xhi, xlo)
            load_lo(1, 0)
            load_lo(2, 0)
            load_lo(3, 0)

            def conv(s0, it, j):
                u0 = pair_first["qkv"] + j
                dve.wait_ge(S("conv_tap"), j + 1 + 4 * it)
                for tap in (2, 1, 0):
                    sh = 3 - tap
                    for t in range(2):
                        col = (2 * j + t) * 4 + tap + it * 32
                        ins = nc.vector.scalar_tensor_tensor(
                            ctmp[:, u0 % 2, t, sh:T1], PS[u0 % 2][:, t, 0:T1 - sh], pdyn("conv", col),
                            ctmp[:, u0 % 2, t, sh:T1], ALU.mult, ALU.add)
                    if tap:
                        own.link(ins)
                ins.then_inc(pair_free[u0 % 2], 1)
                load_lo(s0 + 3, it)
            slots(dve, "qkv", conv, chain=own, links=2)
            for name in ("iq", "av", "ak", "aq"):
                for j in range(dict(STREAM)[name]):
                    load_lo(FIRST[name] + j + 3, 0)
            dve.wait_ge(c1_in, 16)
            dve.wait_ge(S("conv_silu"), 12)
            turned = 0
            for name, x, W, c, sn, t0 in rotations():
                n = x.shape[1]
                b = full(dve, name)
                is_free(nc.vector.tensor_tensor(ctmp[:, 0, 0:n, 0:W], wide(b[:, 0:n * W], W),
                                                bc(cst(sn, lo=t0, n=W), n), ALU.mult), name)
                after(dve, name)
                own.link(nc.vector.tensor_tensor(x, x, bc(cst(c, lo=t0, n=W), n), ALU.mult))
                nc.vector.tensor_tensor(x, x, ctmp[:, 0, 0:n, 0:W], ALU.add).then_inc(S("rope"), 1)
                turned += 1
                dve.wait_ge(S("rope"), turned)
            if upto == "A":
                return
            own.link(nc.vector.tensor_scalar(wix[:], small[:, 0:2, 16:24], IDX_SCALE, None, ALU.mult))
            def top_bias(t):
                W = META + P + t * P
                past = cst("past", lo=t * T1, n=W)
                for hh in range(H1):
                    after(dve, f"idx{t}_{hh}")
                    w = wix[:, t, hh:hh + 1]
                    n = t * H1 + hh
                    if n:
                        dve.wait_ge(S("relu_used"), n)
                    if hh == 0:
                        ins = nc.vector.tensor_scalar(iscore[:, 0:W], irelu[:, hh % 2, 0:W], w, None, ALU.mult)
                    else:
                        ins = nc.vector.scalar_tensor_tensor(iscore[:, 0:W], irelu[:, hh % 2, 0:W], w, iscore[:, 0:W],
                                                             ALU.mult, ALU.add)
                    ins.then_inc(S("relu_used"), 1)
                dve.wait_ge(S("relu_used"), t * H1 + H1)
                own.link(nc.vector.tensor_tensor(iwork[:, 0:W], iscore[:, 0:W], past, ALU.add))
                for _ in range(ROUNDS):
                    own.link(nc.vector.max(top8[:], iwork[:, 0:W]))
                    own.link(nc.vector.match_replace(iwork[:, 0:W], top8[:], iwork[:, 0:W], TAKEN))
                if t:
                    for hh in range(4, 8):
                        after(dve, f"log0_{hh}")
                own.link(nc.vector.tensor_scalar(ibias[:, 0:W], iwork[:, 0:W], TAKEN, BIG, ALU.is_equal, ALU.mult))
                own.link(nc.vector.scalar_tensor_tensor(ibias[:, 0:W], ibias[:, 0:W], -BIG, past, ALU.add, ALU.add))

            for t in range(2):
                W = META + P + t * P
                top_bias(t)
                if t:
                    full(dve, "tr0_7")
                for hh in range(H1):
                    b = full(dve, f"log{t}_{hh}")
                    is_free(nc.vector.scalar_tensor_tensor(lm[:, hh, 0:W], b[:, 0:W], ATT_SCALE, ibias[:, 0:W],
                                                           ALU.mult, ALU.add), f"log{t}_{hh}")
                for hh in range(4, 8):
                    after(dve, f"log{t}_{hh}")
                nc.vector.tensor_reduce(rmax[:, 0:8], lm[:, :, 0:W], AX.X, ALU.max, negate=True)\
                    .then_inc(S("rmax"), 1)
                dve.wait_ge(S("exp"), t + 1)
                own.link(nc.vector.reciprocal(rinv[:, 0:8], rsum[:, 0:8]))
                for g in range(2):
                    nc.vector.tensor_tensor(lm[:, 4 * g:4 * g + 4, 0:W], lm[:, 4 * g:4 * g + 4, 0:W],
                                            rinv[:, 4 * g:4 * g + 4].unsqueeze(2).to_broadcast([P, 4, W]), ALU.mult)\
                        .then_inc(S("prob"), 1)
            for g in range(2):
                dve.wait_ge(S("shi"), g + 1)
                nc.vector.tensor_tensor(slo[:, 4 * g:4 * g + 4], yo[:, 4 * g:4 * g + 4],
                                        shi[:, 4 * g:4 * g + 4].bitcast(F32), ALU.subtract).then_inc(S("slo"), 1)
            dve.wait_ge(lo_ready, FIRST["wbd"] + 3)
            for j in range(4):
                s, u = FIRST["wbd"] + j, pair_first["wbd"] + j
                dve.wait_ge(slot_done, s + 1)
                if j == 0:
                    for u_ in (2, 3):
                        pair_done(dve, pair_first["ga"] + u_)
                nc.vector.tensor_tensor(m1[:, 2 * j:2 * j + 2], PS[u % 2][:, :, 0:SEQ], gbs[:, 2 * j:2 * j + 2],
                                        ALU.mult).then_inc(pair_free[u % 2], 1)
                load_lo(s + 3, 0)
            if upto == "C":
                return
            dve_gdn(dve, own)
            if upto == "D":
                return
            for j in range(4):
                s, u = FIRST["wbg"] + j, pair_first["wbg"] + j
                a = slice(2 * j, 2 * j + 2)
                dve.wait_ge(slot_done, s + 1)
                nc.vector.tensor_tensor(merged[:, a], PS[u % 2][:, :, 0:SEQ], gas[:, a], ALU.mult)\
                    .then_inc(pair_free[u % 2], 1)
                pair_done(dve, u)
                nc.vector.tensor_tensor(merged[:, a], merged[:, a], m1[:, a], ALU.add).then_inc(S("merged"), 1)
                dve.wait_ge(S("mhi"), j + 1)
                nc.vector.tensor_tensor(xlo[:, a, 0:SEQ], merged[:, a], xhi[:, a, 0:SEQ].bitcast(F32), ALU.subtract)\
                    .then_inc(S("mlo"), 1)
                load_lo(s + 3, 0)
            dve_idle_layer("wout")
            dve_post(dve, own, "postmix", "post_mix")
            dve_pre(dve, own, "mlp", "pre_mlp", xhi, xlo)

            def up(s0, it, j):
                u0 = pair_first["up"] + j
                dve.wait_ge(pair_free[u0 % 2], u0 // 2 + 1 + 2 * it)
                p = u0 % 2
                own.link(nc.vector.tensor_tensor(ut[:, p], rt[:, p], rt[:, p], ALU.mult))
                nc.vector.tensor_tensor(ulo[:, bass.ds(2 * j + 8 * it, 2)], ut[:, p],
                                        uhi[:, bass.ds(2 * j + 8 * it, 2)].bitcast(F32), ALU.subtract)\
                    .then_inc(S("ulo"), 1)
                load_lo(s0 + 3, it)
            slots(dve, "up", up, chain=own, links=1)
            dve_idle_layer("down")
            dve_post(dve, own, "postmlp", "post_mlp")
            if upto == "G":
                return
            dve_second(dve, own)

        def dve_gdn(dve, own):
            own.link(nc.vector.tensor_tensor(gtmp[:, 0], small[:, :, 8:16], bc(pcol("dtb", 0, 8), 3), ALU.add))
            nc.vector.tensor_scalar(top8[:, 0:1], ones[:, 0:1], 1.0, None, ALU.mult).then_inc(S("g_arg"), 1)
            after(dve, "l2sum")
            nc.vector.reciprocal(rhead[:, 0:T1], rhead[:, 0:T1]).then_inc(S("l2r"), 1)
            for hh in range(16):
                b = full(dve, f"l2b{hh}")
                is_free(nc.vector.scalar_tensor_tensor(qkv[:, hh], qkv[:, hh], P ** -0.5 if hh < 8 else 1.0, b[:, 0:T1],
                                                       ALU.mult, ALU.mult), f"l2b{hh}")
            for hh in range(12, 16):
                after(dve, f"l2b{hh}")
            for n in range(2):
                ins = nc.vector.tensor_copy(wide(og[:, n, 0:P], META), qkv[:, 8 + 8 * n:16 + 8 * n, 0:META])
            ins.then_inc(S("meta_kv"), 1)
            dve.wait_ge(S("meta_kv"), 1)
            dve.wait_ge(S("g_ln"), 1)
            own.link(nc.vector.scalar_tensor_tensor(gtmp[:, 0], gtmp[:, 0], 0.0, gtmp[:, 1], ALU.max, ALU.add))
            nc.vector.scalar_tensor_tensor(bg[:, :, 8:16], gtmp[:, 0], -1.0, bc(aexp[:], 3), ALU.mult, ALU.mult)\
                .then_inc(S("bg"), 1)
            dve.wait_ge(S("bg"), 1)
            nc.vector.tensor_copy(bcg[:, 0, 0:16].rearrange("p (c n) -> p c n", n=8), bg[:, 0:2, 0:8])
            nc.vector.tensor_copy(bcg[:, 1, 0:16].rearrange("p (c n) -> p c n", n=8), bg[:, 0:2, 8:16])
            b = full(dve, "sel")
            is_free(nc.vector.tensor_tensor(wide(sel16[:], 8), wide(b[:, 0:16], 8), bc(cst("head"), 2), ALU.mult), "sel")
            after(dve, "sel")
            nc.vector.tensor_reduce(bcg[:, :, 16:17], wide(sel16[:], 8), AX.X, ALU.add).then_inc(S("bcg"), 1)
            dve.wait_ge(S("bcg"), 1)
            b = full(dve, "cum")
            own.link(nc.vector.tensor_copy(gcum[:], b[:, 0:17]))
            nc.vector.tensor_tensor(ktsc[:, 0:8], b[:, 20:28], gcum[:, 0:8], ALU.subtract)
            nc.vector.tensor_tensor(ktsc[:, 8:9], b[:, 28:29], gcum[:, 16:17], ALU.subtract).then_inc(S("ktsc"), 1)
            nexp = 0
            for s, probs in enumerate(PROBLEMS):
                n = len(probs)
                ng = seg(probs)
                upper = cst("upper") if s else cst("upper16")
                if s:
                    after(dve, f"s{s - 1}_1") if s == 1 else None
                for g in range(ng):
                    m = min(4, n - 4 * g)
                    b = full(dve, f"gb{s}_{g}")
                    for q in range(m):
                        ins = nc.vector.tensor_scalar(dm[:, 4 * g + q], b[:, q * P:q * P + P],
                                                      gcum[:, probs[4 * g + q]:probs[4 * g + q] + 1], 0.0,
                                                      ALU.subtract, ALU.min)
                    ins.then_inc(S("dm_arg"), 1)
                    b = full(dve, f"bb{s}_{g}")
                    is_free(nc.vector.tensor_tensor(kb[:, 4 * g:4 * g + m], wide(b[:, 0:m * P], P), kview(s, g, m),
                                                    ALU.mult), f"bb{s}_{g}")
                for g in range(ng):
                    m = min(4, n - 4 * g)
                    nexp += 1
                    dve.wait_ge(S("dm_exp"), nexp)
                    a = slice(4 * g, 4 * g + m)
                    own.link(nc.vector.tensor_tensor(dm[:, a], dm[:, a], bc(upper, m), ALU.mult))
                    b = full(dve, f"kk{s}_{g}")
                    is_free(nc.vector.tensor_tensor(at_[:, a], wide(b[:, 0:m * P], P), dm[:, a], ALU.mult), f"kk{s}_{g}")
                    if s:
                        b = full(dve, f"qk{s}_{g}")
                        is_free(nc.vector.tensor_tensor(att[:, a], wide(b[:, 0:m * P], P), dm[:, a], ALU.mult),
                                f"qk{s}_{g}")
                for g in range(ng):
                    after(dve, f"kk{s}_{g}")
                for g in range(-(-n // 2)):
                    ins = nc.vector.tensor_copy(tu[:, g], bc(ident, 4))
                ins.then_inc(S("at_ready"), 1)
                if s:
                    own.link(nc.vector.tensor_tensor(kb[:, 0:n], kb[:, 0:n], eg[:, 0:n], ALU.mult))
                    q = qkv[:, 0:8, META + (s - 1) * P:META + s * P]
                    nc.vector.tensor_tensor(q, q, eg[:, 0:n], ALU.mult).then_inc(S("ke"), 1)
                for g in range(ng):
                    m = min(4, n - 4 * g)
                    b = full(dve, f"vt{s}_{g}")
                    for q in range(m):
                        p_ = probs[4 * g + q]
                        ins = nc.vector.tensor_scalar(vb[:, 4 * g + q], b[:, q * P:q * P + P], bcg[:, 0, p_:p_ + 1], None,
                                                      ALU.mult)
                    is_free(ins, f"vt{s}_{g}")
                    if s < 2:
                        if s == 0 and g == 0:
                            after(dve, "cum")
                        b = full(dve, f"kt{s}_{g}")
                        for q in range(m):
                            c = 8 if s == 0 else 4 * g + q
                            ins = nc.vector.tensor_scalar(ktok[:, 4 * g + q], b[:, q * P:q * P + P], ktsc[:, c:c + 1],
                                                          None, ALU.mult)
                        is_free(ins, f"kt{s}_{g}")
                if s == 0:
                    after(dve, "kt0_0")
                    for hh in range(H1):
                        ins = nc.vector.tensor_scalar(ktm[:, hh], ktok[:, 0], cst("head", lo=hh, n=1), None, ALU.mult)
                    ins.then_inc(S("ktm"), 1)
                with dve.Fori(0, LEVELS[s]) as it:
                    for g in range(-(-n // 2)):
                        m = min(2, n - 2 * g)
                        b = full(dve, f"y{s}_{g}", it)
                        is_free(nc.vector.tensor_tensor(tu[:, g], wide(b[:], P), tu[:, g], ALU.add)
                                if m == 2 else
                                nc.vector.tensor_tensor(tu[:, g, 0:4:2], wide(b[:], P)[:, 0:4:2], tu[:, g, 0:4:2], ALU.add),
                                f"y{s}_{g}")
                for g in range(ng):
                    a = slice(4 * g, 4 * g + 4)
                    if s:
                        b = full(dve, f"r{s}_{g}")
                        is_free(nc.vector.tensor_tensor(vb[:, a], vb[:, a], wide(b[:], P), ALU.subtract), f"r{s}_{g}")
                if s < 2:
                    for g in range(2):
                        a = slice(4 * g, 4 * g + 4)
                        b = full(dve, f"s{s}_{g}")
                        if s == 0:
                            is_free(nc.vector.tensor_copy(st[:, a], wide(b[:], P)), f"s{s}_{g}")
                        else:
                            full(dve, f"o{s}_{g}")
                            for q in range(4):
                                hh = 4 * g + q
                                ins = nc.vector.scalar_tensor_tensor(st[:, hh], st[:, hh], egl[:, hh:hh + 1],
                                                                     b[:, q * P:q * P + P], ALU.mult, ALU.add)
                            is_free(ins, f"s{s}_{g}")
            dve_head_norm(dve, own, "ng", "gdn")

        def dve_head_norm(dve, own, tag, gain):
            x, _, hi, lo = HEADS[tag]
            after(dve, tag + "sum")
            nc.vector.reciprocal(rhead[0:8, 0:SEQ], rhead[0:8, 0:SEQ]).then_inc(S(tag + "r"), 1)
            for n in range(4):
                a = slice(2 * n, 2 * n + 2)
                b = full(dve, f"{tag}{n}")
                is_free(nc.vector.scalar_tensor_tensor(x[:, a], x[:, a], pcol(gain), wide(b[:], SEQ), ALU.mult, ALU.mult),
                        f"{tag}{n}")
                after(dve, f"{tag}{n}")
                if tag == "ng":
                    ins = nc.vector.tensor_tensor(x[:, a], x[:, a], zs[:, a], ALU.mult)
                else:
                    ins = nc.vector.tensor_scalar(x[:, a], x[:, a], 1.0 - LAMBDA_INIT, None, ALU.mult)
                ins.then_inc(S(tag + "f"), 1)
            for n in range(4):
                a = slice(2 * n, 2 * n + 2)
                dve.wait_ge(S(tag + "hi"), n + 1)
                nc.vector.tensor_tensor(lo[:, a], x[:, a], hi[:, a].bitcast(F32), ALU.subtract)\
                    .then_inc(S(tag + "lo"), 1)

        def kview(s, g, m):
            if s == 0:
                return og[:, 0:1, 0:P]
            t0 = META + (s - 1) * P
            return qkv[:, 8 + 4 * g:8 + 4 * g + m, t0:t0 + P]

        def rotations():
            yield "rot_ik", ik[:].unsqueeze(1), T1, "cosi", "sini", 0
            for n in range(2):
                yield f"rot_iq{n}", iq[:, 2 * n:2 * n + 2], SEQ, "cosi", "sini", META
            for n in range(2):
                yield f"rot_ak{n}", ak[:, n:n + 1], T1, "cosa", "sina", 0
            for n in range(4):
                yield f"rot_aq{n}", aq[:, 2 * n:2 * n + 2], SEQ, "cosa", "sina", META

        def dve_second(dve, own):
            dve_pre(dve, own, "ret", "a_pre", xhi, xlo)
            dve.wait_ge(c2_in, 16)
            cos, sin = cst("rcos", t=c2), cst("rsin", t=c2)
            for name, dst in (("rq", rq), ("rk", rk)):
                for j in range(4):
                    s, u = FIRST[name] + j, pair_first[name] + j
                    dve.wait_ge(slot_done, s + 1)
                    x = PS[u % 2][:, :, 0:SEQ]
                    nc.vector.tensor_tensor(rt1[:], x, bc(cos, 2), ALU.mult)
                    nc.vector.tensor_tensor(rt2[:], x, bc(sin, 2), ALU.mult).then_inc(pair_free[u % 2], 1)
                    pair_done(dve, u)
                    nc.vector.tensor_tensor(dst[:, 2 * j], rt1[:, 0], rt2[:, 1], ALU.subtract)
                    own.link(nc.vector.tensor_tensor(dst[:, 2 * j + 1], rt1[:, 1], rt2[:, 0], ALU.add))
                    load_lo(s + 3, 0)
            nc.vector.tensor_scalar(top8[:, 0:1], ones[:, 0:1], 1.0, None, ALU.mult).then_inc(S("rqk"), 1)
            dve_idle_layer("rv")
            dve_idle_layer("rg")
            for hh in range(4):
                b = full(dve, f"rs{hh}")
                dec = cst("decay", t=c2, lo=hh * SEQ, n=SEQ)
                nc.vector.tensor_tensor(rp[:, hh, 0:SEQ], b[:, 0:SEQ], dec, ALU.mult)
                is_free(nc.vector.tensor_tensor(rp[:, hh, SEQ:384], b[:, SEQ:384], dec[:, 0:P], ALU.mult), f"rs{hh}")
            for hh in range(4):
                a = slice(4 * hh, 4 * hh + 4)
                after(dve, f"rn{hh}")
                own.link(nc.vector.reciprocal(rrn[:, hh % 2], rrn[:, hh % 2]))
                own.link(nc.vector.tensor_tensor(ro[:, a], ro[:, a], bc(rrn[:, hh % 2], 4), ALU.mult))
                nc.vector.tensor_tensor(ro[:, a], ro[:, a], rg[:, a], ALU.mult).then_inc(S("ro_done"), 1)
                dve.wait_ge(S("rhi"), hh + 1)
                nc.vector.tensor_tensor(rlo[:, a], ro[:, a], rhi[:, a].bitcast(F32), ALU.subtract)\
                    .then_inc(S("rlo"), 1)
            dve_idle_layer("ro")
            dve_post(dve, own, "postret", "a_post")
            dve_ffn(dve, own, 0)
            if upto == "I":
                return
            dve_pre(dve, own, "diff", "kv", xhi, xlo)
            dve_scale_split(dve, "diff", "b_pre", x2hi, x2lo, 4)
            for n in range(2):
                own.link(nc.vector.tensor_tensor(am[:, n, 0:64], pcol("lam", 128 * n, 64), pcol("lam", 128 * n + 64, 64),
                                                 ALU.mult))
            nc.vector.tensor_reduce(lamt[:, 0:2].unsqueeze(2), am[:, 0:2, 0:64], AX.X, ALU.add).then_inc(S("lam"), 1)
            dve.wait_ge(S("lam_exp"), 1)
            own.link(nc.vector.scalar_tensor_tensor(lamt[:, 4:5], lamt[:, 2:3], LAMBDA_INIT, lamt[:, 3:4], ALU.add,
                                                    ALU.subtract))
            for name in ("dk", "dv", "dq"):
                dve_idle_layer(name)
            for t in range(2):
                W = P + t * P
                past = cst("past2", t=c2, lo=t * SEQ, n=W)
                for n in range(4):
                    for c in range(2):
                        name = f"ds{t}_{n}_{c}"
                        b = full(dve, name)
                        is_free(nc.vector.scalar_tensor_tensor(lm2[:, 4 * n + c:4 * n + c + 3:2, 0:W],
                                                               wide(b[:], SEQ)[:, :, 0:W], 64 ** -0.5, bc(past, 2),
                                                               ALU.mult, ALU.add), name)
                for n in range(2, 4):
                    for c in range(2):
                        after(dve, f"ds{t}_{n}_{c}")
                nc.vector.tensor_reduce(rmax[:].unsqueeze(2), lm2[:, :, 0:W], AX.X, ALU.max, negate=True)\
                    .then_inc(S("rmax2"), 1)
                dve.wait_ge(S("exp2"), t + 1)
                own.link(nc.vector.reciprocal(rinv[:], rsum[:]))
                odd = rinv[:].rearrange("p (n c) -> p n c", c=2)[:, :, 1:2]
                own.link(nc.vector.tensor_scalar(rinv2[:, 0:8].unsqueeze(2), odd, lamt[:, 4:5], None, ALU.mult))
                if t:
                    full(dve, "dt0_7")
                for hh in range(H1):
                    own.link(nc.vector.tensor_scalar(lm2[:, 2 * hh + 1, 0:W], lm2[:, 2 * hh + 1, 0:W],
                                                     rinv2[:, hh:hh + 1], None, ALU.mult))
                    nc.vector.scalar_tensor_tensor(am[:, hh, 0:W], lm2[:, 2 * hh, 0:W], rinv[:, 2 * hh:2 * hh + 1],
                                                   lm2[:, 2 * hh + 1, 0:W], ALU.mult, ALU.subtract).then_inc(S("am"), 1)
            dve_head_norm(dve, own, "nd", "subln")
            dve_idle_layer("do")
            dve_post(dve, own, "postdiff", "b_post")
            dve_ffn(dve, own, 1)

        def dve_ffn(dve, own, k):
            dve_pre(dve, own, f"ffn{k}", f"f_pre{k}", xhi, xlo)

            def conv(s0, it, j):
                u0 = pair_first[f"fu{k}"] + j
                p = s0 % 2
                dve.wait_ge(S("f_tap"), k * FT2 + j + 1 + 4 * it)
                for tap in (1, 0):
                    sh = 2 - tap
                    for t in range(2):
                        col = (t * FT2 + j) * 3 + tap + 12 * it
                        ins = nc.vector.scalar_tensor_tensor(
                            ft[:, p, t, sh:SEQ], PS[u0 % 2][:, t, 0:SEQ - sh], pdyn(f"f_conv{k}", col),
                            ft[:, p, t, sh:SEQ], ALU.mult, ALU.add)
                    if tap:
                        own.link(ins)
                ins.then_inc(pair_free[u0 % 2], 1)
                load_lo(s0 + 3, it)
            slots(dve, f"fu{k}", conv, chain=own, links=1)
            dve_idle_layer(f"fd{k}")
            dve_post(dve, own, f"postffn{k}", f"f_post{k}")


        def pe_norm(pe, name):
            src, T = norm_view(name)
            b = fill("norm_" + name)
            for kt in range(KT):
                if kt % 2 == 0:
                    pe.wait_ge(S("sq_" + name), kt // 2 + 1)
                ins = nc.tensor.matmul(b[:, 0:T], ones[:], sq[:, kt, 0:T], start=kt == 0, stop=kt == KT - 1)
            is_full(ins, "norm_" + name)

        def pe_post(pe, name, layer):
            last = pair_first[layer] + dict(STREAM)[layer] // GROUP.get(layer, 1) - 1
            for g in range(0 if layer == "down" else 3, 4):
                pe_sum_squares(name, last - 3 + g, g)

        def pe_body(pe):
            pe.wait_ge(set_up, 1)
            pe_norm(pe, "mix")
            slot_in(0, 0)
            feature_slot(0, 0, xhi, xlo, tiles=(0,), ready="xlo_mix")
            for c, (t0, m) in enumerate(CHUNKS):
                ins = token_slot(0, PS[0][0:m, 1, 32 * c:32 * c + 24], xhi, xlo, slice(P, P + 24), m, t0)
            ins.then_inc(slot_done, 1)
            pe_layer("qkv", xhi, xlo, lead=4)
            pe_layer("iq", xhi, xlo)
            s, u = FIRST["av"], pair_first["av"]
            slot_in(s, 0)
            pair_in(u, 0, 0)
            for c, (t0, m) in enumerate(CHUNKS):
                out = PS[u % 2][0:m, c, 0:NCOL] if c < 2 else PS[u % 2][0:m, 0, NCOL:2 * NCOL]
                ins = token_slot(s, out, xhi, xlo, slice(0, NCOL), m, t0)
            ins.then_inc(slot_done, 1)
            pe_layer("ak", xhi, xlo)
            pe_layer("aq", xhi, xlo)
            pe.wait_ge(c1_in, 16)
            for name, x, W, c, sn, t0 in rotations():
                turn = cst("turni" if c == "cosi" else "turna")
                if name == "rot_ik":
                    pair_done(pe, 0)
                elif name[:6] == "rot_iq":
                    pair_done(pe, pair_first["iq"] + int(name[6:]))
                elif name[:6] == "rot_ak":
                    pair_done(pe, pair_first["ak"])
                else:
                    pair_done(pe, pair_first["aq"] + int(name[6:]))
                b = fill(name)
                for n in range(x.shape[1]):
                    ins = nc.tensor.matmul(b[:, n * W:n * W + W], turn, x[:, n], start=True, stop=True)
                is_full(ins, name)
            if upto == "A":
                return
            def gate_slot(n):
                name, j = GATE_SLOTS[n]
                s, u = FIRST[name] + j, pair_first[name] + j
                slot_in(s, 0)
                pair_in(u, 0, 0)
                feature_slot(s, u % 2, xhi, xlo).then_inc(slot_done, 1)

            def index_scores(t):
                W = META + P + t * P
                for hh in range(H1):
                    b = fill(f"idx{t}_{hh}")
                    r = slice(64 * (hh % 2), 64 * (hh % 2) + 64)
                    is_full(nc.tensor.matmul(b[:, 0:W], iq[r, hh // 2, t * P:t * P + P], ik[r, 0:W], start=True,
                                             stop=True), f"idx{t}_{hh}")

            gate_slot(0)
            gate_slot(1)
            pe.wait_ge(S("rope"), 3)
            index_scores(0)
            for t in range(2):
                W = META + P + t * P
                if t == 0:
                    pe.wait_ge(S("rope"), 9)
                for hh in range(H1):
                    if hh == 4:
                        gate_slot(2 if t == 0 else 7)
                        gate_slot(3 if t == 0 else 8)
                    b = fill(f"log{t}_{hh}")
                    is_full(nc.tensor.matmul(b[:, 0:W], aq[:, hh, t * P:t * P + P], ak[:, hh // 4, 0:W], start=True,
                                             stop=True), f"log{t}_{hh}")
                if t == 0:
                    index_scores(1)
                    gate_slot(4)
                    gate_slot(5)
                else:
                    gate_slot(9)
                for hh in range(H1 + 1):
                    if hh == 4 and t == 0:
                        gate_slot(6)
                    if hh % 4 == 0 and hh < H1:
                        pe.wait_ge(S("prob"), 2 * t + hh // 4 + 1)
                    if hh < H1:
                        b = fill(f"tr{t}_{hh}")
                        for c, (t0, m) in enumerate(CHUNKS):
                            if c == 1 and t == 0:
                                continue
                            ins = nc.tensor.transpose(b[0:m, c * P:c * P + P], lm[:, hh, t0:t0 + m], ident)
                        is_full(ins, f"tr{t}_{hh}")
                    if hh:
                        g = hh - 1
                        after(pe, f"tr{t}_{g}")
                        name = f"pv{t}_{g // 4}"
                        b = fill(name) if g % 4 == 0 else AUX[USE[name][0]]
                        cs = [c for c in range(3) if t or c != 1]
                        for c in cs:
                            m = CHUNKS[c][1]
                            ins = nc.tensor.matmul(b[:, (g % 4) * P:(g % 4) * P + P],
                                                   av[0:m, c, (g // 4) * P:(g // 4) * P + P], pT[0:m, g % 2, c],
                                                   start=c == 0, stop=c == 2)
                        if g % 4 == 3:
                            is_full(ins, name)
                        else:
                            ins.then_inc(S("pv_mm"), 1)
            gate_slot(10)
            gate_slot(11)
            pe.wait_ge(S("slo"), 2)
            pe_layer("wbd", shi, slo)
            if upto == "C":
                return
            pe_gdn(pe)
            if upto == "D":
                return
            pe_layer("wbg", ghi, glo, ready="nglo")
            pe_layer("wout", xhi[:, :, 0:SEQ], xlo[:, :, 0:SEQ], ready="mlo", norm="postmix")
            pe_post(pe, "postmix", "wout")
            pe_norm(pe, "mlp")
            pe_layer("up", xhi[:, :, 0:SEQ], xlo[:, :, 0:SEQ], lead=4, ready="xlo_mlp")
            pe.wait_ge(S("ulo"), 16)
            pe_groups("down", uhi, ulo, 4, KT, 8)
            pe_post(pe, "postmlp", "down")
            if upto == "G":
                return
            pe_second(pe)

        def pe_gdn(pe):
            pe_head_sums(pe, "l2sum", ((sq, "l2sq", 1), (sqb, "l2sq", 2)), T1, 16)
            pe.wait_ge(S("l2r"), 1)
            for hh in range(16):
                b = fill(f"l2b{hh}")
                is_full(nc.tensor.matmul(b[:, 0:T1], ident[0:16, hh:hh + 1].to_broadcast([16, P]), rhead[0:16, 0:T1],
                                         start=True, stop=True), f"l2b{hh}")
            pe.wait_ge(S("bg"), 1)
            b = fill("sel")
            is_full(nc.tensor.matmul(b[:, 0:16], cst("spread", META), bg[0:META, 2, :], start=True, stop=True), "sel")
            pe.wait_ge(S("bcg"), 1)
            b = fill("cum")
            g = bcg[:, 1]
            nc.tensor.matmul(b[:, 0:16], cst("upper"), g[:, 0:16], start=True, stop=True)
            nc.tensor.matmul(b[:, 16:17], cst("upper16"), g[:, 16:17], start=True, stop=True)
            nc.tensor.matmul(b[:, 20:28], ones[:], g[:, 0:8], start=True, stop=True)
            is_full(nc.tensor.matmul(b[:, 28:29], cst("ones16"), g[:, 16:17], start=True, stop=True), "cum")
            pe.wait_ge(S("meta_kv"), 1)
            lev0 = 0
            for s, probs in enumerate(PROBLEMS):
                n, ng = len(probs), seg(probs)
                t0 = META + (s - 1) * P
                tok = slice(t0, t0 + P)

                def feat(base, q):
                    return qkv[:, base + q, tok] if s else og[:, base // 8 - 1, 0:P]
                for g in range(ng):
                    m = min(4, n - 4 * g)
                    b = fill(f"gb{s}_{g}")
                    for q in range(m):
                        j = probs[4 * g + q]
                        ins = nc.tensor.matmul(b[:, q * P:q * P + P], bcg[:, 1, j:j + 1].to_broadcast([P, P]),
                                               cst("upper" if s else "upper16"), start=True, stop=True)
                    is_full(ins, f"gb{s}_{g}")
                    b = fill(f"bb{s}_{g}")
                    for q in range(m):
                        j = probs[4 * g + q]
                        ins = nc.tensor.matmul(b[:, q * P:q * P + P], bcg[:, 0, j:j + 1].to_broadcast([P, P]), ident,
                                               start=True, stop=True)
                    is_full(ins, f"bb{s}_{g}")
                for g in range(ng):
                    m = min(4, n - 4 * g)
                    after(pe, f"bb{s}_{g}")
                    b = fill(f"kk{s}_{g}")
                    for q in range(m):
                        ins = nc.tensor.matmul(b[:, q * P:q * P + P], feat(8, 4 * g + q), kb[:, 4 * g + q], start=True,
                                               stop=True)
                    is_full(ins, f"kk{s}_{g}")
                    if s:
                        b = fill(f"qk{s}_{g}")
                        for q in range(m):
                            ins = nc.tensor.matmul(b[:, q * P:q * P + P], feat(8, 4 * g + q), feat(0, 4 * g + q),
                                                   start=True, stop=True)
                        is_full(ins, f"qk{s}_{g}")
                for g in range(ng):
                    m = min(4, n - 4 * g)
                    b = fill(f"vt{s}_{g}")
                    for q in range(m):
                        ins = nc.tensor.transpose(b[:, q * P:q * P + P], feat(16, 4 * g + q), ident)
                    is_full(ins, f"vt{s}_{g}")
                    if s < 2:
                        b = fill(f"kt{s}_{g}")
                        for q in range(m):
                            ins = nc.tensor.transpose(b[:, q * P:q * P + P], feat(8, 4 * g + q), ident)
                        is_full(ins, f"kt{s}_{g}")
                pe.wait_ge(S("at_ready"), s + 1)
                with pe.Fori(0, LEVELS[s]) as it:
                    pe.wait_ge(S("al_ready"), lev0 + 1 + it)
                    for g in range(ng):
                        m = min(4, n - 4 * g)
                        for k in range(-(-m // 2)):
                            ub = USE[f"y{s}_{2 * g + k}"]
                            pe.wait_ge(aux_free[ub[0]], ub[1] - ub[2] + it * ub[2])
                        b = fill(f"x{s}_{g}", it)
                        for q in range(m):
                            p_ = 4 * g + q
                            ins = nc.tensor.matmul(b[:, q * P:q * P + P], al[:, p_], tu[:, p_ // 2, p_ % 2], start=True,
                                                   stop=True)
                        is_full(ins, f"x{s}_{g}")
                    for g in range(-(-n // 2)):
                        m = min(2, n - 2 * g)
                        after(pe, f"x{s}_{g // 2}", it)
                        b = fill(f"y{s}_{g}", it)
                        for q in range(m):
                            p_ = 2 * g + q
                            nc.tensor.matmul(b[:, q * P:q * P + P], tu[:, g, 2 + q], xs[:, p_], start=True, stop=True)
                            ins = nc.tensor.matmul(b[:, (2 + q) * P:(3 + q) * P], xs[:, p_], tu[:, g, 2 + q], start=True,
                                                   stop=True)
                        is_full(ins, f"y{s}_{g}")
                lev0 += LEVELS[s]
                ylast = range(-(-n // 2))
                if s:
                    pe.wait_ge(S("ke"), s)
                    for g in range(2):
                        after(pe, f"s{s - 1}_{g}")
                        b = fill(f"r{s}_{g}")
                        for q in range(4):
                            ins = nc.tensor.matmul(b[:, q * P:q * P + P], kb[:, 4 * g + q], st[:, 4 * g + q], start=True,
                                                   stop=True)
                        is_full(ins, f"r{s}_{g}")
                for g in range(ng):
                    m = min(4, n - 4 * g)
                    for k in range(-(-m // 2)):
                        ub = USE[f"y{s}_{2 * g + k}"]
                        pe.wait_ge(aux_free[ub[0]], ub[1] + (LEVELS[s] - 1) * ub[2])
                    if s:
                        after(pe, f"r{s}_{g}")
                    else:
                        after(pe, "vt0_0")
                    b = fill(f"v{s}_{g}")
                    for q in range(m):
                        p_ = 4 * g + q
                        ins = nc.tensor.matmul(b[:, q * P:q * P + P], tu[:, p_ // 2, 2 + p_ % 2], vb[:, p_], start=True,
                                               stop=True)
                    is_full(ins, f"v{s}_{g}")
                if s == 0:
                    pe.wait_ge(S("ktm"), 1)
                for g in range(2):
                    after(pe, f"v{s}_{g if s else 0}")
                    if s:
                        b = fill(f"o{s}_{g}")
                        for q in range(4):
                            hh = 4 * g + q
                            nc.tensor.matmul(b[:, q * P:q * P + P], st[:, hh], feat(0, hh), start=True, stop=False)
                            ins = nc.tensor.matmul(b[:, q * P:q * P + P], vn[:, hh], att[:, hh], start=False, stop=True)
                        is_full(ins, f"o{s}_{g}")
                    if s < 2:
                        b = fill(f"s{s}_{g}")
                        for q in range(4):
                            hh = 4 * g + q
                            if s:
                                ins = nc.tensor.matmul(b[:, q * P:q * P + P], ktok[:, hh], vn[:, hh], start=True, stop=True)
                            else:
                                ins = nc.tensor.matmul(b[:, q * P:q * P + P], ktm[:, hh], vn[:, 0], start=True, stop=True)
                        is_full(ins, f"s{s}_{g}")
            pe_head_norm(pe, "ng")

        def pe_head_sums(pe, name, parts, T, heads):
            b = fill(name)
            n = 0
            for src, sem_name, count in parts:
                pe.wait_ge(S(sem_name), count)
                for hh in range(8):
                    a = CCOL["window"] + 15 - n
                    ins = nc.tensor.matmul(b[0:heads, 0:T], c1[:, a:a + heads], src[:, hh], start=n == 0,
                                           stop=n == heads - 1)
                    n += 1
            is_full(ins, name)

        def pe_head_norm(pe, tag):
            pe_head_sums(pe, tag + "sum", ((HEADS[tag][1], tag + "sq", 1),), SEQ, 8)
            pe.wait_ge(S(tag + "r"), 1)
            for n in range(4):
                b = fill(f"{tag}{n}")
                for q in range(2):
                    ins = nc.tensor.matmul(b[:, q * SEQ:(q + 1) * SEQ],
                                           ident[0:8, 2 * n + q:2 * n + q + 1].to_broadcast([8, P]), rhead[0:8, 0:SEQ],
                                           start=True, stop=True)
                is_full(ins, f"{tag}{n}")

        def pe_tokens(pe, name, hi, lo):
            def step(s0, it, j):
                u0 = pair_first[name] + j
                slot_in(s0, it)
                pair_in(u0, it, 2)
                for c in range(2):
                    ins = token_slot(s0, PS[u0 % 2][:, c, 0:NCOL], hi, lo, slice(0, NCOL), P, c * P)
                ins.then_inc(slot_done, 1)
            slots(pe, name, step)

        def pe_second(pe):
            x_hi, x_lo = xhi[:, :, 0:SEQ], xlo[:, :, 0:SEQ]
            pe_norm(pe, "ret")
            pe_layer("rq", x_hi, x_lo, ready="xlo_ret")
            pe_layer("rk", x_hi, x_lo)
            pe_tokens(pe, "rv", x_hi, x_lo)
            pe_layer("rg", x_hi, x_lo)
            pe.wait_ge(S("rqk"), 1)
            for hh in range(4):
                b = fill(f"rs{hh}")
                for e in range(2):
                    nc.tensor.matmul(b[:, 0:SEQ], rk[:, 2 * hh + e, 0:P], rq[:, 2 * hh + e], start=e == 0, stop=e == 1)
                for e in range(2):
                    ins = nc.tensor.matmul(b[:, SEQ:384], rk[:, 2 * hh + e, P:SEQ], rq[:, 2 * hh + e, P:SEQ],
                                           start=e == 0, stop=e == 1)
                is_full(ins, f"rs{hh}")
            pair_done(pe, pair_first["rv"] + 6)
            pair_done(pe, pair_first["rv"] + 7)
            for hh in range(4):
                after(pe, f"rs{hh}")
                for e in range(2):
                    b = fill(f"ro{hh}_{e}")
                    for q in range(2):
                        a = slice((4 * hh + 2 * e + q) * P, (4 * hh + 2 * e + q + 1) * P)
                        lo = slice(q * SEQ, q * SEQ + P)
                        up = slice(q * SEQ + P, (q + 1) * SEQ)
                        nc.tensor.matmul(b[:, lo], rv[:, 0, a], rp[:, hh, 0:P], start=True, stop=True)
                        nc.tensor.matmul(b[:, up], rv[:, 0, a], rp[:, hh, P:SEQ], start=True, stop=False)
                        ins = nc.tensor.matmul(b[:, up], rv[:, 1, a], rp[:, hh, SEQ:384], start=False, stop=True)
                    is_full(ins, f"ro{hh}_{e}")
                after(pe, f"ro{hh}_0")
                after(pe, f"ro{hh}_1")
                b = fill(f"rn{hh}")
                for e in range(4):
                    ins = nc.tensor.matmul(b[:, 0:SEQ], ones[:], rsq[:, hh % 2, e], start=e == 0, stop=e == 3)
                is_full(ins, f"rn{hh}")
            pe.wait_ge(S("rlo"), 4)
            pe_groups("ro", rhi, rlo, 2, KT, 8, norm="postret")
            pe_post(pe, "postret", "ro")
            pe_ffn(pe, 0)
            if upto == "I":
                return
            pe_norm(pe, "diff")
            pe_layer("dk", x_hi, x_lo, ready="xlo_diff")
            pe_tokens(pe, "dv", x_hi, x_lo)
            pe.wait_ge(S("xlo_diff"), 8)
            pe_layer("dq", x2hi, x2lo)
            pair_done(pe, pair_first["dq"] + 2)
            pair_done(pe, pair_first["dq"] + 3)
            for t in range(2):
                W = P + t * P
                for n in range(4):
                    for c in range(2):
                        b = fill(f"ds{t}_{n}_{c}")
                        r = slice(64 * c, 64 * c + 64)
                        for q in range(2):
                            ins = nc.tensor.matmul(b[:, q * SEQ:q * SEQ + W], dq[r, 2 * n + q, t * P:t * P + P],
                                                   dk[r, 2 * n + q, 0:W], start=True, stop=True)
                        is_full(ins, f"ds{t}_{n}_{c}")
                for hh in range(H1 + 1):
                    if hh < H1:
                        pe.wait_ge(S("am"), t * H1 + hh + 1)
                        b = fill(f"dt{t}_{hh}")
                        for c in range(1 + t):
                            ins = nc.tensor.transpose(b[:, c * P:c * P + P], am[:, hh, c * P:c * P + P], ident)
                        is_full(ins, f"dt{t}_{hh}")
                    if hh:
                        g = hh - 1
                        after(pe, f"dt{t}_{g}")
                        name = f"dp{t}_{g // 4}"
                        b = fill(name) if g % 4 == 0 else AUX[USE[name][0]]
                        for c in range(1 + t):
                            ins = nc.tensor.matmul(b[:, (g % 4) * P:(g % 4) * P + P], dv[:, c, g * P:g * P + P],
                                                   aT[:, g % 2, c], start=c == 0, stop=c == t)
                        if g % 4 == 3:
                            is_full(ins, name)
                        else:
                            ins.then_inc(S("dp_mm"), 1)
            pe_head_norm(pe, "nd")
            pe_layer("do", dhi, dlo, ready="ndlo", norm="postdiff")
            pe_post(pe, "postdiff", "do")
            pe_ffn(pe, 1)

        def pe_ffn(pe, k):
            pe_norm(pe, f"ffn{k}")
            pe_layer(f"fu{k}", xhi[:, :, 0:SEQ], xlo[:, :, 0:SEQ], lead=2, ready=f"xlo_ffn{k}")
            pe.wait_ge(S("f_lo"), FT2 * (k + 1))
            pe_groups(f"fd{k}", fhi, flo, 3, FT2 - 2 * KT, 12, norm=f"postffn{k}")
            pe_post(pe, f"postffn{k}", f"fd{k}")

        @block.gpsimd
        def _(pool):
            own = Chain(pool, pool_own)
            nc.gpsimd.memset(ones[:], 1.0)
            nc.gpsimd.memset(eps[:, 0:1], EPS)
            nc.gpsimd.memset(eps[:, 1:2], P * EPS)
            nc.gpsimd.memset(small[:], 0.0).then_inc(set_up, 1)
            pool_body(pool, own)
            if upto:
                pool.memset(top8[:], 0.0).then_inc(S("end_pool"), 1)

        @block.scalar
        def _(act):
            act_body(act, Chain(act, act_own))
            if upto:
                act.copy(rsum[:, 0:1], ones[:, 0:1]).then_inc(S("end_act"), 1)

        @block.vector
        def _(dve):
            dve_body(dve, Chain(dve, dve_own))
            if upto:
                nc.vector.memset(top8[:, 0:1], 0.0).then_inc(S("end_dve"), 1)

        @block.tensor
        def _(pe):
            pe_body(pe)
            if upto:
                nc.tensor.wait_ge(aux_free[3], 1) if filled[3] and upto != "A" else None
                nc.tensor.matmul(AUX[3][0:1, 0:1], ones[:, 0:1], ones[:, 0:1], start=True, stop=True)\
                    .then_inc(S("end_pe"), 1)



def tiles_of(v):
    return np.ascontiguousarray(v.reshape(-1, P).T)


def slots_of(w):
    k, n = w.shape
    if k % D:
        w = np.concatenate([w, np.zeros((-k % D, n), w.dtype)])
        k = w.shape[0]
    return w.reshape(k // D, KT, P, n // NCOL, NCOL).transpose(3, 0, 2, 1, 4).reshape(-1, P, KT, NCOL)


def pairs_of(w):
    g, u = w[:, :FF2].reshape(D, FT2, P), w[:, FF2:].reshape(D, FT2, P)
    return slots_of(np.stack([g, u], 2).reshape(D, 2 * FF2))


def constants():
    f = np.float32
    i = np.arange(P)
    same16 = (i[:, None] // 16) == (i[None, :] // 16)
    up = i[:, None] <= i[None, :]
    c = {"ident": np.eye(P), "window": np.tile(np.arange(32) == 15, (P, 1)), "upper": up, "upper16": up & same16, "ones16": same16,
         "spread": (i[:, None] == i[None, :] % 16), "head": i[:, None] // 16 == np.arange(8)[None, :]}
    lev = []
    for n in range(NLEVEL):
        b = 1 << n
        col = i[None, :] // b
        lev.append(-((col % 2 == 1) & (i[:, None] // b == col - 1)).astype(f))
    c["levels"] = np.concatenate(lev, 1)
    pos = np.arange(T1, dtype=f)
    for tag, dim in (("a", 128), ("i", 64)):
        inv = (f(10000.0) ** (-np.arange(0, dim, 2, dtype=f) / f(dim))).astype(f)
        ang = pos[None, :] * inv[i % (dim // 2)][:, None]
        c["cos" + tag], c["sin" + tag] = np.cos(ang), np.sin(ang)
        turn = np.zeros((P, P), f)
        for m in range(P):
            lo = m % dim < dim // 2
            turn[m + dim // 2 if lo else m - dim // 2, m] = -1.0 if lo else 1.0
        c["turn" + tag] = turn
    past = [np.where(pos[None, :] <= (META + t * P + i)[:, None], 0.0, -BIG) for t in range(2)]
    c["past"] = np.concatenate(past, 1)
    p2 = np.arange(SEQ, dtype=f)
    inv = (f(1.0) / (f(10000.0) ** np.linspace(0.0, 1.0, P, dtype=f))).astype(f)
    ang = inv[:, None] * p2[None, :]
    c["rcos"], c["rsin"] = np.cos(ang), np.sin(ang)
    log_gamma = np.log1p(-np.power(2.0, -5.0 - np.arange(4)))
    rel = p2[None, :] - i[:, None]
    c["decay"] = np.concatenate([np.where(rel >= 0, np.exp(lg * np.maximum(rel, 0)) / 16.0, 0.0) for lg in log_gamma], 1)
    c["past2"] = np.concatenate([np.where(p2[None, :] <= (t * P + i)[:, None], 0.0, -BIG) for t in range(2)], 1)
    return (np.concatenate([np.asarray(c[n], f) for n, _ in CONST1], 1),
            np.concatenate([np.asarray(c[n], f) for n, _ in CONST2], 1))


def laid_out(v):
    w = v["w_in"][0]
    at = np.cumsum([0, 1024, 1024, 1024, 1024, 8, 8, 1024, 256, 256, 512, 64, 8, 1024, 1024])
    gq, gk, gv, gz, gb, ga, aq, ak, av, iq, ik, iw, gate_a, gate_b = (w[:, a:b] for a, b in zip(at[:-1], at[1:]))
    small = np.concatenate([ik, ik, gb, ga, iw, np.zeros((D, NCOL - 152), w.dtype)], 1)
    ain = v["a_w_in_2"][0]
    kv = v["w_kv_2"]
    parts = {"small": small, "qkv": w[:, 0:3072], "iq": iq, "av": av, "ak": ak, "aq": aq, "z": gz, "ga": gate_a,
             "gb": gate_b, "wbd": v["w_branch_dsa"][0], "wbg": v["w_branch_gdn"][0], "wout": v["w_out"][0],
             "up": v["w_up"][0], "down": v["w_down"][0], "rq": ain[:, 0:1024], "rk": ain[:, 1024:2048],
             "rv": ain[:, 2048:4096], "rg": ain[:, 4096:6144], "ro": v["a_w_out_2"][0],
             "fd0": v["ffn_w_down_2"][0], "fd1": v["ffn_w_down_2"][1], "dk": kv[:, 0:1024], "dv": kv[:, 1024:2048],
             "dq": v["b_w_q_2"][0], "do": v["b_w_out_2"][0]}
    made = []
    for name, count in STREAM:
        if name[:2] == "fu":
            s = pairs_of(v["ffn_w_up_2"][int(name[2])])
        else:
            s = slots_of(parts[name])
        assert s.shape[0] == count, (name, s.shape, count)
        made.append(s)
    cols = {"pre_mix": tiles_of(v["pre_mix_norm"][0]),
            "conv": v["conv_w"][0].reshape(4, 24, P).transpose(2, 1, 0).reshape(P, 96),
            "gdn": tiles_of(v["gdn_norm"][0]), "post_mix": tiles_of(v["post_mix_norm"][0]),
            "pre_mlp": tiles_of(v["pre_mlp_norm"][0]), "post_mlp": tiles_of(v["post_mlp_norm"][0]),
            "a_pre": tiles_of(v["a_norm_pre_2"][0]), "a_post": tiles_of(v["a_norm_post_2"][0]),
            "kv": tiles_of(v["kv_norm_2"]), "b_pre": tiles_of(v["b_norm_pre_2"][0]),
            "b_post": tiles_of(v["b_norm_post_2"][0]), "subln": tiles_of(v["b_subln_2"][0]),
            "alog": np.tile(v["a_log"][0][None], (P, 1)), "dtb": np.tile(v["dt_bias"][0][None], (P, 1)),
            "lam": np.tile(v["b_lambda_2"][0].reshape(1, 256), (P, 1))}
    for k in range(2):
        cols[f"f_pre{k}"] = tiles_of(v["ffn_norm_pre_2"][k])
        cols[f"f_post{k}"] = tiles_of(v["ffn_norm_post_2"][k])
        cols[f"f_conv{k}"] = v["ffn_conv_w_2"][k].reshape(3, 2 * FT2, P).transpose(2, 1, 0).reshape(P, -1)
        cols[f"f_bias{k}"] = tiles_of(v["ffn_conv_b_2"][k])
    c1, c2 = constants()
    x = np.concatenate([v["meta_tokens"], v["x"][0]], 0).T.reshape(KT, P, T1).transpose(1, 0, 2)
    return {"stream": np.concatenate(made), "params": np.concatenate([cols[n] for n, _ in PARAMS], 1),
            "const1": c1, "const2": c2, "x": x}


def kernel(**inputs):
    import concourse.bacc as bacc
    from concourse.bass_utils import run_bass_kernel_spmd as run

    v = {name: np.asarray(a) for name, a in inputs.items()}
    arrays = {"in_" + n: np.ascontiguousarray(a) for n, a in laid_out(v).items()}
    nc = bacc.Bacc("TRN2", target_bir_lowering=False, num_devices=1)
    args = {n[3:]: nc.dram_tensor(n, a.shape, F32, kind="ExternalInput").ap() for n, a in arrays.items()}
    out = nc.dram_tensor("out", (P, KT, SEQ), F32, kind="ExternalOutput").ap()
    program(nc, args["stream"], args["params"], args["const1"], args["const2"], args["x"], out)
    r = run(nc, [arrays], core_ids=[0])
    y = r.results[0]["out"]
    return y.transpose(2, 1, 0).reshape(1, SEQ, D)
```

```python
import math
from contextlib import ExitStack

import numpy as np
import concourse.bass as bass
from concourse import mybir

F32 = mybir.dt.float32
F32R = mybir.dt.float32r
ALU = mybir.AluOpType
ACT = mybir.ActivationFunctionType
AX = mybir.AxisListType

P = 128
D = 1024
KT = D // P
NCOL = 256
META = 16
SEQ = 256
T1 = META + SEQ
H1 = 8
TOPK = 64
ROUNDS = TOPK // 8
IDX_SCALE = (8 * 64) ** -0.5
ATT_SCALE = 128 ** -0.5
EPS = 1e-6
FF2 = 2816
FT2 = FF2 // P
LAMBDA_INIT = 0.8 - 0.6 * math.exp(-0.3)
BIG = 1e30
TAKEN = -3e38

STREAM = [("small", 1), ("qkv", 12), ("iq", 2), ("av", 1), ("ak", 1), ("aq", 4), ("gb", 4), ("z", 4),
          ("ga", 4), ("wbd", 4), ("wbg", 4), ("wout", 4), ("up", 16), ("down", 16), ("rq", 4), ("rk", 4),
          ("rv", 8), ("rg", 8), ("ro", 8), ("fu0", 22), ("fd0", 12), ("dk", 4), ("dq", 4), ("dv", 4),
          ("do", 4), ("fu1", 22), ("fd1", 12)]
FIRST = {}
_at = 0
for _name, _count in STREAM:
    FIRST[_name] = _at
    _at += _count
NSLOT = _at

PARAMS = [("pre_mix", 8), ("conv", 96), ("gdn", 1), ("post_mix", 8), ("pre_mlp", 8), ("post_mlp", 8),
          ("a_pre", 8), ("a_post", 8), ("kv", 8), ("b_pre", 8), ("b_post", 8), ("subln", 1),
          ("f_pre0", 8), ("f_pre1", 8), ("f_post0", 8), ("f_post1", 8),
          ("f_conv0", 3 * 2 * FT2), ("f_conv1", 3 * 2 * FT2), ("f_bias0", 2 * FT2), ("f_bias1", 2 * FT2),
          ("alog", 8), ("dtb", 8), ("lam", 256)]
PCOL = {}
_at = 0
for _name, _count in PARAMS:
    PCOL[_name] = _at
    _at += _count
NPAR = _at

CONST1 = [("ident", 128), ("window", 32), ("upper", 128), ("upper16", 128), ("ones16", 128), ("spread", 128), ("head", 8),
          ("levels", 7 * 128), ("cosa", T1), ("sina", T1), ("cosi", T1), ("sini", T1), ("turna", 128),
          ("turni", 128), ("past", 2 * T1)]
CONST2 = [("rcos", SEQ), ("rsin", SEQ), ("decay", 4 * SEQ), ("past2", 2 * SEQ)]
CCOL = {}
_at = 0
for _name, _count in CONST1:
    CCOL[_name] = _at
    _at += _count
NC1 = _at
_at = 0
for _name, _count in CONST2:
    CCOL[_name] = _at
    _at += _count
NC2 = _at
NLEVEL = 7
SUMS = 508
PROJECT = [("iq", 0), ("iq", 1), 0, ("av", 0), 1, 2, ("ak", 0), ("aq", 0), 3, 4, ("aq", 1), 5, ("aq", 2), 6, ("aq", 3), 7,
           ("gb", 0), 8]
RETENTION = [("gate", 0), ("hi", 0), ("silu", 0), ("gate", 1), ("hi", 1), ("silu", 1), ("product", 0), ("readout", 0),
             ("gate", 2), ("hi", 2), ("silu", 2), ("product", 1), ("readout", 1), ("gate", 3), ("hi", 3), ("silu", 3),
             ("squares", 0), ("root", 0), ("product", 2), ("readout", 2), ("gate", 4), ("hi", 4), ("finish", 0),
             ("squares", 1), ("root", 1), ("product", 3), ("readout", 3), ("high", 0), ("gate", 5), ("hi", 5),
             ("low", 0), ("finish", 1), ("squares", 2), ("silu", 4), ("silu", 5), ("high", 1), ("gate", 6), ("hi", 6),
             ("low", 1), ("root", 2), ("squares", 3), ("finish", 2), ("gate", 7), ("hi", 7), ("root", 3), ("silu", 6),
             ("silu", 7), ("high", 2), ("finish", 3), ("low", 2), ("high", 3), ("low", 3)]
GATE_SLOTS = [(name, j) for name in ("gb", "z", "ga") for j in range(4)]
CHUNKS = [(META, P), (META + P, P), (0, META)]


class Chain:

    def __init__(self, eng, sem):
        self.eng, self.sem, self.n = eng, sem, 0

    def link(self, ins):
        ins.then_inc(self.sem, 1)
        self.n = self.n + 1
        self.eng.wait_ge(self.sem, self.n)


def slots(eng, name, step, body=4, chain=None, links=0, lead=0):
    first, count = FIRST[name], dict(STREAM)[name]
    for j in range(lead):
        step(first + j, 0, j)
    loops = (count - lead) // body if count - lead >= 2 * body else 0
    if loops:
        before = chain.n if chain else 0
        with eng.Fori(0, loops) as it:
            if chain:
                chain.n = before + it * (links * body)
            for j in range(lead, lead + body):
                step(first + j, it, j)
        if chain:
            chain.n = before + loops * links * body
    for j in range(lead + loops * body, count):
        step(first + j, 0, j)


def program(nc, stream, params, const1, const2, x_in, y_out):
    ctx = ExitStack()
    with ctx:
        base = -(-nc.sbuf_base // 64) * 64
        arena = ctx.enter_context(nc.sbuf_tensor("arena", [P, (nc.sbuf_usable_end - base) // 4 - 32], F32))
        del arena

        def at(name, off, shape, dt=F32):
            return nc.alloc_sbuf_tensor_at(name, shape, dt, offset=base + off)

        RAW_N = 4
        raw = at("raw", 0, [P, RAW_N, KT, NCOL])
        wlo = at("wlo", 0, [P, RAW_N, KT, NCOL], F32R)
        whi = at("whi", 32768, [P, RAW_N, KT, NCOL], F32R)
        par = at("par", 65536, [P, NPAR])
        cursor = [65536 + 4 * NPAR]

        def nxt(name, shape):
            cursor[0] = -(-cursor[0] // 32) * 32
            t = at(name, cursor[0], shape)
            cursor[0] += 4 * int(np.prod(shape[1:]))
            return t

        ones = nxt("ones", [P, P])
        eps = nxt("eps", [P, 2])
        small = nxt("small", [P, 3, 24])
        bg = nxt("bg", [P, 3, 16])
        gtmp = nxt("gtmp", [P, 3, 3, 8])
        bcg = nxt("bcg", [P, 2, 17])
        gcum = nxt("gcum", [P, 17])
        sel16 = nxt("sel16", [P, 16])
        ktsc = nxt("ktsc", [P, 9])
        egl = nxt("egl", [P, 8])
        lamt = nxt("lamt", [P, 8])
        aexp = nxt("aexp", [P, 8])
        wix = nxt("wix", [P, 2, 8])
        rmax = nxt("rmax", [P, 16])
        rsum = nxt("rsum", [P, 16])
        rinv = nxt("rinv", [P, 16])
        top8 = nxt("top8", [P, 8])
        rstd = nxt("rstd", [P, T1])
        rcol = nxt("rcol", [P, 2])
        rhead = rstd[0:16]
        PC = -(-cursor[0] // 64) * 64
        c1 = at("c1", PC, [P, NC1])
        c2 = at("c2", PC + 640, [P, NC2])
        HB = PC + 4 * NC1
        h = at("h", HB, [P, KT, T1])
        B = HB + 8704
        xhi = at("xhi", B, [P, KT, T1], F32R)
        xlo = at("xlo", B + 8704, [P, KT, T1], F32R)
        qkv = at("qkv", B + 17408, [P, 24, T1])
        aq = at("aq", B + 43520, [P, 8, SEQ])
        ak = at("ak", B + 51712, [P, 2, T1])
        av = at("av", B + 53888, [P, 3, NCOL])
        iq = at("iq", B + 56960, [P, 4, SEQ])
        ik = at("ik", B + 61056, [P, T1])
        ctmp = at("ctmp", B + 62144, [P, 2, 2, T1])
        lm = at("lm", B + 62144, [P, 8, T1])
        ibias = at("ibias", B + 70848, [P, T1])
        iscore = at("iscore", B + 71936, [P, T1])
        iwork = at("iwork", B + 73024, [P, T1])
        irelu = at("irelu", B + 74112, [P, 2, T1])
        zs = at("zs", B + 76288, [P, 8, SEQ])
        gas = at("gas", B + 84480, [P, 8, SEQ])
        gbs = at("gbs", B + 92672, [P, 8, SEQ])
        shi = at("shi", B + 43520, [P, 8, SEQ], F32R)
        slo = at("slo", B + 51712, [P, 8, SEQ], F32R)
        m1 = at("m1", B + 59904, [P, 8, SEQ])
        yo = at("yo", B + 101376, [P, 8, SEQ])
        pT = at("pT", B + 109568, [P, 2, 3, P])
        xf = at("xf", B + 83968, [P, KT, T1])
        sq = at("sq", B + 92672, [P, KT, T1])
        sqq = at("sqq", B, [P, 8, T1])
        sqk = at("sqk", B + 8704, [P, 8, T1])
        kb = at("kb", B + 43520, [P, 8, P])
        att = at("att", B + 47616, [P, 8, P])
        at_ = at("at_", B + 51712, [P, 8, P])
        al = at("al", B + 55808, [P, 8, P])
        eg = at("eg", B + 68096, [P, 8, P])
        dm = at("dm", B + 72192, [P, 8, P])
        tu = at("tu", B + 92672, [P, 4, 4, P])
        xs = at("xs", B + 101376, [P, 8, P])
        vb = at("vb", B + 105472, [P, 8, P])
        ktok = at("ktok", B, [P, 8, P])
        vn = at("vn", B + 4096, [P, 8, P])
        st = at("st", B + 8192, [P, 8, P])
        ktm = at("ktm", B + 12288, [P, 8, P])
        og = at("og", B + 109568, [P, 8, SEQ])
        tus = (at("tu0", B + 115712, [P, 1, 4, P]), tu, tu)
        kbs = (at("kb0", B + 16384, [P, 1, P]), kb, kb)
        dms = (at("dm0", B + 16896, [P, 1, P]), dm, dm)
        ats, als, xss, vbs = ((at(f"{n}0", B + 113664 + 512 * k, [P, 1, P]), t, t)
                              for k, (n, t) in enumerate((("at", at_), ("al", al), ("xs", xs), ("vb", vb))))
        gsq = at("gsq", B + 43520, [P, 8, SEQ])
        ghi = at("ghi", B + 92672, [P, 8, SEQ], F32R)
        glo = at("glo", B + 100864, [P, 8, SEQ], F32R)
        merged = at("merged", B + 51712, [P, 8, SEQ])
        rt = at("rt", B + 82944, [P, 2, 2, SEQ])
        ut = at("ut", B + 87040, [P, 2, 2, SEQ])
        uhi = at("uhi", B + 17408, [P, 32, SEQ], F32R)
        ulo = at("ulo", B + 50176, [P, 32, SEQ], F32R)
        rq = at("rq", B + 17408, [P, 8, SEQ])
        rk = at("rk", B + 25600, [P, 8, SEQ])
        rv = at("rv", B + 33792, [P, 2, 2048])
        rg = at("rg", B + 50176, [P, 16, SEQ])
        rp = at("rp", B + 66560, [P, 4, 384])
        ro = at("ro", B + 72704, [P, 16, SEQ])
        rsq = at("rsq", B + 89088, [P, 2, 4, SEQ])
        rrn = at("rrn", B + 97280, [P, 2, SEQ])
        rt1 = at("rt1", B + 99328, [P, 2, SEQ])
        rt2 = at("rt2", B + 101376, [P, 2, SEQ])
        rcs = at("rcs", B + 103424, [P, 2, SEQ])
        rhi = at("rhi", B + 33792, [P, 16, SEQ], F32R)
        rlo = at("rlo", B + 17408, [P, 16, SEQ], F32R)
        fhi = at("fhi", B + 17408, [P, FT2, SEQ], F32R)
        flo = at("flo", B + 39936, [P, FT2, SEQ], F32R)
        ft = at("ft", B + 62464, [P, 2, 2, SEQ])
        fy = at("fy", B + 70656, [P, 2, 2, SEQ])
        fs = at("fs", B + 66560, [P, 2, SEQ])
        fu = at("fu", B + 68608, [P, 2, SEQ])
        x2hi = at("x2hi", B + 17408, [P, 8, SEQ], F32R)
        x2lo = at("x2lo", B + 25600, [P, 8, SEQ], F32R)
        dk = at("dk", B + 33792, [P, 8, SEQ])
        dq = at("dq", B + 41984, [P, 8, SEQ])
        dv = at("dv", B + 50176, [P, 2, 1024])
        lm2 = at("lm2", B + 58368, [P, 16, SEQ])
        am = at("am", B + 74752, [P, 8, SEQ])
        aT = at("aT", B + 84992, [P, 2, 2, P])
        lm2s = (at("lm2a", B + 100864, [P, 16, P]), lm2)
        ams = (at("ama", B + 109056, [P, 8, P]), am)
        dstat = at("dstat", B + 113152, [P, 4, 2, 16])
        dmax, dsum, dinv, dinv2 = (dstat[:, n] for n in range(4))
        do = at("do", B + 17408, [P, 8, SEQ])
        dsq = at("dsq", B + 92672, [P, 8, SEQ])
        dhi = at("dhi", B + 76288, [P, 8, SEQ], F32R)
        dlo = at("dlo", B + 84480, [P, 8, SEQ], F32R)
        HEADS = {"ng": (og, gsq, ghi, glo), "nd": (do, dsq, dhi, dlo)}

        PS = [ctx.enter_context(nc.psum_tensor(f"lin{n}", [P, 2, 512], F32)) for n in range(2)]
        AUX = [ctx.enter_context(nc.psum_tensor(f"aux{n}", [P, 512], F32)) for n in range(4)]

        def sem(name):
            return ctx.enter_context(nc.semaphore(name))

        w_loaded = [sem(f"w_loaded{r}") for r in range(RAW_N)]
        hi_ready = sem("hi_ready")
        lo_ready = sem("lo_ready")
        slot_done = sem("slot_done")
        pair_free = [sem(f"pair_free{n}") for n in range(2)]
        aux_full = [sem(f"aux_full{n}") for n in range(4)]
        aux_free = [sem(f"aux_free{n}") for n in range(4)]
        par_in = sem("par_in")
        c1_in = sem("c1_in")
        ident_in = sem("ident_in")
        c2_in = sem("c2_in")
        x_loaded = [sem(f"x_loaded{c}") for c in range(2)]
        set_up = sem("set_up")
        out_done = sem("out_done")
        act_own = sem("act_own")
        dve_own = sem("dve_own")
        pool_own = sem("pool_own")
        named = {}

        def S(name):
            if name not in named:
                named[name] = sem(name)
            return named[name]

        filled = [0] * 4
        USE = {}

        def use(bank, *names):
            for name in names:
                filled[bank] += 1
                USE[name] = (bank, filled[bank], 0)

        def use_loop(count, banks_names):
            per = [0] * 4
            for bank, name in banks_names:
                per[bank] += 1
                USE[name] = (bank, filled[bank] + per[bank], 1)
            for bank, name in banks_names:
                USE[name] = (bank, USE[name][1], per[bank])
            for n in range(4):
                filled[n] += per[n] * count

        def fill(name, it=0):
            bank, n, per = USE[name]
            if n > 1 or per:
                nc.tensor.wait_ge(aux_free[bank], n - 1 + it * per)
            return AUX[bank]

        def is_full(ins, name):
            ins.then_inc(aux_full[USE[name][0]], 1)

        def full(eng, name, it=0):
            bank, n, per = USE[name]
            eng.wait_ge(aux_full[bank], n + it * per)
            return AUX[bank]

        def is_free(ins, name):
            ins.then_inc(aux_free[USE[name][0]], 1)

        def pcol(name, n=0, count=1):
            return par[:, PCOL[name] + n:PCOL[name] + n + count]

        def pdyn(name, n, count=1):
            return par[:, bass.ds(PCOL[name] + n, count)]

        def cst(name, rows=P, t=c1, lo=0, n=None):
            a = CCOL[name] + lo
            width = dict(CONST1 + CONST2)[name] - lo if n is None else n
            return t[0:rows, a:a + width]

        ident = cst("ident")

        use(2, "norm_mix")
        use(0, "rot_ik")
        use(1, "rot_iq0")
        use(2, "rot_iq1")
        use(3, "rot_ak0")
        use(0, "rot_ak1")
        for n in range(4):
            use((n + 1) % 4, f"rot_aq{n}")
        for name in ("idx0", "log0", "idx1"):
            for hh in range(H1):
                use(hh % 4, f"{name}_{hh}")
        for t in range(2):
            if t:
                for hh in range(H1):
                    use(hh % 4, f"log1_{hh}")
            for hh in range(H1):
                use(hh % 2, f"tr{t}_{hh}")
                if hh % 4 == 3:
                    use(2 + hh // 4, f"pv{t}_{hh // 4}")
        use(0, "l2sum")
        for hh in range(16):
            if hh == 4:
                use(0, "sel")
            if hh == 8:
                use(0, "cum")
            use((hh + 1) % 4, f"l2b{hh}")
        PROBLEMS = [[16], list(range(8)), list(range(8, 16))]
        TOGETHER = {1: [(1, 0), (1, 1), (0, 0)], 2: [(2, 0), (2, 1)]}
        PAIRS = {1: [(3, 1, 0), (0, 1, 1), (2, 1, 2), (1, 1, 3), (3, 0, 0)],
                 2: [(2, 2, 0), (3, 2, 1), (0, 2, 2), (1, 2, 3)]}
        MID = NLEVEL - 2

        def gdn_prepare(s):
            ng = -(-len(PROBLEMS[s]) // 4)
            for g in range(ng):
                use(2 * g % 4, f"gb{s}_{g}")
                use((2 * g + 1) % 4, f"bb{s}_{g}")
            for g in range(ng):
                use(g, f"kk{s}_{g}")
                if s:
                    use(2 + g, f"qk{s}_{g}")
            for g in range(ng):
                use(g, f"vt{s}_{g}")
                if s < 2:
                    use(2 + g, f"kt{s}_{g}")

        gdn_prepare(0)
        for s in (1, 2):
            gdn_prepare(s)
            xb = [(n, f"x{a}_{g}") for n, (a, g) in enumerate(TOGETHER[s])]
            yb = [(n, f"y{a}_{g}") for n, a, g in PAIRS[s]]
            for bank, name in xb:
                use(bank, "first_" + name)
            use_loop(MID, [(bank, "mid_" + name) for bank, name in xb + yb])
            for bank, name in xb + yb:
                use(bank, "last_" + name)
            if s == 1:
                use(2, "v0_0")
                use(2, "s0_0")
                use(3, "s0_1")
            for g in range(2):
                use(g, f"r{s}_{g}")
            for g in range(2):
                use(2 + g, f"v{s}_{g}")
            for g in range(2):
                use(g, f"o{s}_{g}")
                if s < 2:
                    use(2 + g, f"s{s}_{g}")
        use(0, "ngsum")
        for n in range(4):
            use((n + 1) % 4, f"ng{n}")
        use(0, "norm_postmix", "rstd_postmix")
        use(1, "norm_mlp")
        use(2, "norm_postmlp", "rstd_postmlp")
        use(3, "norm_ret")
        use(0, "rcol_ret")
        for hh in range(4):
            use(hh, f"rs{hh}")
        for hh in range(5):
            if hh < 4:
                use(0, f"ro{hh}_0")
                use(1, f"ro{hh}_1")
            if hh:
                use(2 + (hh - 1) % 2, f"rn{hh - 1}")
        use(0, "norm_postret", "rstd_postret")
        use(1, "norm_ffn0")
        use(2, "norm_postffn0", "rstd_postffn0")
        use(3, "norm_diff")
        use(0, "rcol_diff")
        for n in range(4):
            for t in range(2):
                for c in range(2):
                    use(2 * t + c, f"ds{t}_{n}_{c}")
        for t in range(2):
            for hh in range(H1):
                use(hh % 2, f"dt{t}_{hh}")
                if hh % 4 == 3:
                    use(2 + hh // 4, f"dp{t}_{hh // 4}")
        use(0, "ndsum")
        for n in range(4):
            use((n + 1) % 4, f"nd{n}")
        use(0, "norm_postdiff", "rstd_postdiff")
        use(1, "norm_ffn1")
        use(2, "norm_postffn1", "rstd_postffn1")

        def load_hi(s0, it):
            if s0 >= NSLOT:
                return
            nc.scalar.wait_ge(w_loaded[s0 % 4], 16 * (s0 // 4 + 1) + 16 * it)
            if s0 >= RAW_N:
                nc.scalar.wait_ge(slot_done, s0 - RAW_N + 1 + 4 * it)
            nc.scalar.copy(whi[:, s0 % 4], raw[:, s0 % 4]).then_inc(hi_ready, 1)

        def load_lo(s0, it):
            if s0 >= NSLOT:
                return
            nc.vector.wait_ge(hi_ready, s0 + 1 + 4 * it)
            nc.vector.tensor_tensor(wlo[:, s0 % 4], raw[:, s0 % 4], whi[:, s0 % 4].bitcast(F32),
                                    ALU.subtract).then_inc(lo_ready, 1)

        def slot_in(s0, it):
            nc.tensor.wait_ge(lo_ready, s0 + 1 + 4 * it)

        def pair_in(u0, it, per):
            if u0 >= 2:
                nc.tensor.wait_ge(pair_free[u0 % 2], u0 // 2 + it * per)

        def mm3(out, s0, kt, cols, hi, lo, start, stop, swap=False):
            wh, wl = whi[:, s0 % 4, kt, cols], wlo[:, s0 % 4, kt, cols]
            if swap:
                trio = ((hi, wh), (hi, wl), (lo, wh))
            else:
                trio = ((wh, hi), (wh, lo), (wl, hi))
            for n, (a, b) in enumerate(trio):
                ins = nc.tensor.matmul(out, a, b, start=start and n == 0, stop=stop and n == 2)
            return ins

        def feature_slot(s0, pair, hi, lo, tiles=(0, 1), kts=KT, ready=None, sums=None):
            T = hi.shape[-1]
            step = 2 if ready else kts
            for k1 in range(0, kts, step):
                if ready:
                    nc.tensor.wait_ge(S(ready), k1 // 2 + 1)
                    if sums and k1:
                        pe_sum_input(sums, k1 // 2 - 1)
                for t in tiles:
                    for kt in range(k1, k1 + step):
                        ins = mm3(PS[pair][:, t, 0:T], s0, kt, slice(t * P, t * P + P), hi[:, kt], lo[:, kt], kt == 0,
                                  kt == kts - 1)
                    if sums and kt == kts - 1 and t == 0:
                        pe_sum_input(sums, 3)
            return ins

        def pe_sum_input(name, c):
            b = fill("norm_" + name) if c == 0 else AUX[USE["norm_" + name][0]]
            nc.tensor.wait_ge(S("sq_" + name), c + 1)
            for kt in (2 * c, 2 * c + 1):
                ins = nc.tensor.matmul(b[:, 0:SEQ], ones[:], sq[:, kt, 0:SEQ], start=kt == 0, stop=kt == KT - 1)
            if c == 3:
                is_full(ins, "norm_" + name)

        def pe_token_scale(pe, name):
            pe.wait_ge(S("r_" + name), 1)
            b = fill("rcol_" + name)
            for c in range(2):
                ins = nc.tensor.matmul(b[:, c:c + 1], rstd[:, c * P:c * P + P], ident[:, 0:1], start=True, stop=True)
            is_full(ins, "rcol_" + name)

        def token_slot(s0, out, hi, lo, cols, m, t0):
            for kt in range(KT):
                ins = mm3(out, s0, kt, cols, hi[:, kt, t0:t0 + m], lo[:, kt, t0:t0 + m], kt == 0, kt == KT - 1,
                          swap=True)
            return ins

        POST = ("wout", "down", "ro", "do", "fd0", "fd1")
        GAIN_OF = {"postmix": "post_mix", "postmlp": "post_mlp", "postret": "a_post", "postffn0": "f_post0",
                   "postdiff": "b_post", "postffn1": "f_post1"}
        NORM_OF = {"mix": "small", "mlp": "up", "ret": "rq", "ffn0": "fu0", "diff": "dk", "ffn1": "fu1"}
        GROUP = {"down": 4, "ro": 2, "fd0": 3, "fd1": 3}
        pair_first = {}
        n = 0
        for name, count in STREAM:
            pair_first[name] = n
            n += count // GROUP.get(name, 1)

        def pe_layer(name, hi, lo, body=4, lead=0, ready=None, norm=None, sums=None):
            def step(s0, it, j):
                u0 = pair_first[name] + j
                slot_in(s0, it)
                pair_in(u0, it, body // 2)
                feature_slot(s0, u0 % 2, hi, lo, ready=ready if j == 0 else None,
                             sums=sums if j == 0 else None).then_inc(slot_done, 1)
                if norm and j:
                    pe_sum_squares(norm, j - 1)
            slots(nc.tensor, name, step, body, lead=lead)

        def pe_groups(name, hi, lo, group, kts_last, body, norm=None, ready=None):
            def step(s0, it, j):
                g = j % group
                u0 = pair_first[name] + j // group
                slot_in(s0, it * (body // 4))
                if g == 0:
                    pair_in(u0, it, body // group // 2)
                if ready:
                    nc.tensor.wait_ge(S(ready[0]), ready[1][g])
                kts = kts_last if g == group - 1 else KT
                T = hi.shape[-1]
                for t in range(2):
                    for kt in range(kts):
                        ins = mm3(PS[u0 % 2][:, t, 0:T], s0, kt, slice(t * P, t * P + P), hi[:, g * KT + kt],
                                  lo[:, g * KT + kt], g == 0 and kt == 0, g == group - 1 and kt == kts - 1)
                ins.then_inc(slot_done, 1)
                if norm and g == 0 and j:
                    pe_sum_squares(norm, j // group - 1)
            slots(nc.tensor, name, step, body)

        def pe_sum_squares(norm, g):
            b = fill("norm_" + norm) if g == 0 else AUX[USE["norm_" + norm][0]]
            nc.tensor.wait_ge(S("sq_" + norm), g + 1)
            for kt in (2 * g, 2 * g + 1):
                ins = token_sums(b, kt)
            if g == KT // 2 - 1:
                is_full(ins, "norm_" + norm)

        def token_sums(b, kt):
            for c in range(2):
                ins = nc.tensor.matmul(b[:, SUMS + c:SUMS + c + 1], sq[:, kt, c * P:c * P + P], ones[:, 0:1],
                                       start=kt == 0 and c == 0, stop=kt == KT - 1 and c == 1)
            return ins

        def pe_spread(name):
            nc.tensor.wait_ge(S("rcol_" + name), 1)
            b = fill("rstd_" + name)
            for c in range(2):
                ins = nc.tensor.matmul(b[:, c * P:c * P + P], rcol[:, c:c + 1].to_broadcast([P, P]), ident, start=True,
                                       stop=True)
            is_full(ins, "rstd_" + name)

        def keep_warm(layer, n, slot=0):
            u = pair_first[layer] + slot
            pair_in(u, 0, 0)
            for _ in range(n):
                nc.tensor.matmul(PS[u % 2][:, 0, 0:P], ones[:], ones[:], start=True, stop=True)

        def bc(a, n):
            return a.unsqueeze(1).to_broadcast([a.shape[0], n, a.shape[1]])

        def wide(a, w):
            return a.rearrange("p (n w) -> p n w", w=w)

        def after(eng, name, it=0):
            bank, n, per = USE[name]
            eng.wait_ge(aux_free[bank], n + it * per)

        def pair_done(eng, u):
            eng.wait_ge(pair_free[u % 2], u // 2 + 1)

        hx = h[:, :, META:T1]

        def seg(probs):
            return (len(probs) + 3) // 4

        block = ctx.enter_context(nc.Block())

        @block.sync
        def _(sp):
            for c in range(2):
                sp.dma_start(h[:, 4 * c:4 * c + 4], x_in[:, 4 * c:4 * c + 4]).then_inc(x_loaded[c], 16)
            head = CCOL["upper"]
            sp.dma_start(c1[:, 0:head], const1[:, 0:head]).then_inc(ident_in, 16)
            sp.dma_start(par[:], params).then_inc(par_in, 16)
            for s in range(4):
                sp.dma_start(raw[:, s], stream[s]).then_inc(w_loaded[s], 16)
            sp.dma_start(c1[:, head:NC1], const1[:, head:NC1]).then_inc(c1_in, 16)
            with sp.Fori(1, NSLOT // 4) as it:
                for r in range(4):
                    sp.wait_ge(slot_done, it * 4 + (r - 3))
                    slot = stream[bass.ds(it * 4 + r, 1)].rearrange("o p k n -> (o p) k n")
                    sp.dma_start(raw[:, r], slot).then_inc(w_loaded[r], 16)
            for s in range(NSLOT // 4 * 4, NSLOT):
                sp.wait_ge(slot_done, s - 3)
                sp.dma_start(raw[:, s % 4], stream[s]).then_inc(w_loaded[s % 4], 16)
            for c in range(4):
                sp.wait_ge(S("h_postffn1"), c + 1)
                sp.dma_start(y_out[:, 2 * c:2 * c + 2], hx[:, 2 * c:2 * c + 2]).then_inc(out_done, 16)
            sp.wait_ge(out_done, 64)


        def pool_low(pool, first, end):
            for s in range(first, end):
                pool.wait_ge(lo_ready, s)
                pool.wait_ge(hi_ready, s + 1)
                nc.gpsimd.tensor_tensor(wlo[:, s % 4], raw[:, s % 4], whi[:, s % 4].bitcast(F32), ALU.subtract)\
                    .then_inc(lo_ready, 1)

        def pool_body(pool, own):
            pool_low(pool, FIRST["gb"] + 3, FIRST["wbd"] + 3)
            for s in (1, 2):
                sets = sorted({a for a, _ in TOGETHER[s]}, reverse=True)
                x_last = "x%d_%d" % TOGETHER[s][-1]
                bank, n, per = USE["mid_" + x_last]

                def level(lev):
                    for a in sets:
                        m = len(PROBLEMS[a])
                        ins = nc.gpsimd.tensor_tensor(als[a][:, 0:m], ats[a][:, 0:m], bc(lev, m), ALU.mult)
                    ins.then_inc(S("al_ready"), 1)

                for a, g in TOGETHER[s]:
                    after(pool, f"kk{a}_{g}")
                level(cst("levels", n=P))
                pool.wait_ge(S("first_level"), s)
                level(cst("levels", lo=P, n=P))
                with pool.Fori(0, MID) as it:
                    pool.wait_ge(aux_full[bank], n + it * per)
                    level(c1[:, bass.ds(it * P + (CCOL["levels"] + 2 * P), P)])
            pool.wait_ge(S("nglo"), 4)
            pool.dma_start(c2[:], const2).then_inc(c2_in, 16)
            pool_low(pool, FIRST["rg"] + 6, FIRST["ro"] + 3)
            for k in range(2):
                def tail(s0, it, j):
                    n0 = k * FT2 + j
                    pool.wait_ge(S("f_silu"), n0 + 1 + 4 * it)
                    if n0 >= 2:
                        pool.wait_ge(S("f_hi"), n0 - 1 + 4 * it)
                    nc.gpsimd.tensor_tensor(fu[:, s0 % 2], fs[:, s0 % 2], ft[:, s0 % 2, 1], ALU.mult)\
                        .then_inc(S("f_prod"), 1)
                    pool.wait_ge(S("f_prod"), n0 + 1 + 4 * it)
                    pool.wait_ge(S("f_hi"), n0 + 1 + 4 * it)
                    nc.gpsimd.tensor_tensor(flo[:, bass.ds(j + 4 * it, 1)], fu[:, s0 % 2].unsqueeze(1),
                                            fhi[:, bass.ds(j + 4 * it, 1)].bitcast(F32), ALU.subtract).then_inc(S("f_lo"), 1)
                slots(pool, f"fu{k}", tail)


        def act_pre(act, name, hi, gain, after_h, until=0):
            if until:
                act.wait_ge(slot_done, until)
            for c in range(4):
                act.wait_ge(S(after_h), c + 1)
                a = slice(2 * c, 2 * c + 2)
                for kt in (2 * c, 2 * c + 1):
                    ins = nc.scalar.activation(hi[:, kt, 0:SEQ], hx[:, kt], ACT.Copy, scale=pcol(gain, kt))
                ins.then_inc(S("xhi_" + name), 1)
                nc.scalar.activation(sq[:, a, 0:SEQ], hx[:, a], ACT.Square).then_inc(S("sq_" + name), 1)
            act_root(act, name, SEQ)
            load_hi(FIRST[NORM_OF[name]] + 2, 0)

        def act_token_scale(act, name):
            b = full(act, "rcol_" + name)
            is_free(nc.scalar.copy(rcol[:], b[:, 0:2]), "rcol_" + name)
            after(act, "rcol_" + name)

        def act_root(act, name, T):
            b = full(act, "norm_" + name)
            if name in NORM_OF:
                is_free(nc.scalar.activation(rstd[:, 0:T], b[:, 0:T], ACT.Sqrt, scale=1.0 / D, bias=eps[:, 0:1]),
                        "norm_" + name)
                return
            is_free(nc.scalar.activation(rcol[:], b[:, SUMS:SUMS + 2], ACT.Sqrt, scale=1.0 / D, bias=eps[:, 0:1]),
                    "norm_" + name)

        def act_high_mix(act):
            for c in range(4):
                act.wait_ge(S("xf_mix"), c + 1)
                a = slice(2 * c, 2 * c + 2)
                nc.scalar.copy(xhi[:, a], xf[:, a]).then_inc(S("xhi_mix"), 1)

        def act_layer_out(act, name, norm):
            group = GROUP.get(name, 1)
            for j in range(dict(STREAM)[name]):
                s = FIRST[name] + j
                act.wait_ge(slot_done, s + 1)
                if j % group == group - 1:
                    g = j // group
                    u = pair_first[name] + g
                    nc.scalar.activation(sq[:, 2 * g:2 * g + 2, 0:SEQ], PS[u % 2][:, :, 0:SEQ], ACT.Square)\
                        .then_inc(S("sq_" + norm), 1)
                    for t in range(2):
                        ins = nc.scalar.activation(yo[:, 2 * g + t], PS[u % 2][:, t, 0:SEQ], ACT.Copy,
                                                   scale=pcol(GAIN_OF[norm], 2 * g + t))
                    ins.then_inc(pair_free[u % 2], 1)
                if j < dict(STREAM)[name] - 1:
                    load_hi(s + 3, 0)
            act_root(act, norm, SEQ)

        def act_body(act, own):
            act.wait_ge(set_up, 1)
            for c in range(4):
                if c % 2 == 0:
                    act.wait_ge(x_loaded[c // 2], 16)
                a = slice(2 * c, 2 * c + 2)
                nc.scalar.activation(sq[:, a], h[:, a], ACT.Square).then_inc(S("sq_mix"), 1)
            load_hi(0, 0)
            act_root(act, "mix", T1)
            act_high_mix(act)
            load_hi(1, 0)
            load_hi(2, 0)
            act.wait_ge(slot_done, 1)
            nc.scalar.copy(ik[:], PS[0][:, 0, 0:T1])
            nc.scalar.copy(small[:, 0:2, :], wide(PS[0][:, 1, 0:64], 32)[:, :, 0:24])
            nc.scalar.copy(small[0:META, 2, :], PS[0][0:META, 1, 64:88]).then_inc(pair_free[0], 1)
            load_hi(3, 0)
            act.wait_ge(par_in, 16)

            def conv(s0, it, j):
                u0 = pair_first["qkv"] + j
                if j % 4 == 0:
                    nc.scalar.activation(gtmp[:, 2, 0, 1:2], eps[:, 0:1], ACT.Silu)
                act.wait_ge(slot_done, s0 + 1 + 4 * it)
                for t in range(2):
                    col = (2 * j + t) * 4 + 3 + it * 32
                    ins = nc.scalar.activation(ctmp[:, u0 % 2, t], PS[u0 % 2][:, t, 0:T1], ACT.Copy,
                                               scale=pdyn("conv", col))
                ins.then_inc(S("conv_tap"), 1)
                load_hi(s0 + 3, it)
                act.wait_ge(pair_free[u0 % 2], u0 // 2 + 1 + 2 * it)
                nc.scalar.activation(qkv[:, bass.ds(2 * j + 8 * it, 2)], ctmp[:, u0 % 2], ACT.Silu)\
                    .then_inc(S("conv_silu"), 1)
            slots(act, "qkv", conv)
            for name, dst in (("iq", iq[:]), ("av", av[:]), ("ak", ak[:]), ("aq", aq[:])):
                for j in range(dict(STREAM)[name]):
                    s = FIRST[name] + j
                    u = pair_first[name] + j
                    act.wait_ge(slot_done, s + 1)
                    if name == "av":
                        nc.scalar.copy(av[:, 0:2], PS[u % 2][:, :, 0:NCOL])
                        nc.scalar.copy(av[0:META, 2], PS[u % 2][0:META, 0, NCOL:2 * NCOL]).then_inc(pair_free[u % 2], 1)
                    elif name == "ak":
                        nc.scalar.copy(ak[:], PS[u % 2][:, :, 0:T1]).then_inc(pair_free[u % 2], 1)
                    else:
                        nc.scalar.copy(dst[:, 2 * j:2 * j + 2], PS[u % 2][:, :, META:T1]).then_inc(pair_free[u % 2], 1)
                    load_hi(s + 3, 0)
            gates = {"gb": (gbs, ACT.Sigmoid), "z": (zs, ACT.Silu), "ga": (gas, ACT.Sigmoid)}

            def gate_out(n):
                name, j = GATE_SLOTS[n]
                dst, func = gates[name]
                s, u = FIRST[name] + j, pair_first[name] + j
                act.wait_ge(slot_done, s + 1)
                nc.scalar.activation(dst[:, 2 * j:2 * j + 2], PS[u % 2][:, :, META:T1], func)\
                    .then_inc(pair_free[u % 2], 1)
                load_hi(s + 3, 0)

            def relus(t):
                W = META + P + t * P
                for hh in range(H1):
                    b = full(act, f"idx{t}_{hh}")
                    n = t * H1 + hh
                    if n >= 2:
                        act.wait_ge(S("relu_used"), n - 1)
                    is_free(nc.scalar.activation(irelu[:, hh % 2, 0:W], b[:, 0:W], ACT.Relu), f"idx{t}_{hh}")

            gate_out(0)
            relus(0)
            gate_out(1)
            gate_out(2)
            gate_out(3)
            for t in range(2):
                W = META + P + t * P
                nc.scalar.activation(gtmp[:, 2, 0, 0:1], eps[:, 0:1], ACT.Exp)
                act.wait_ge(S("rmax"), t + 1)
                for hh in range(H1):
                    ins = nc.scalar.activation(lm[:, hh, 0:W], lm[:, hh, 0:W], ACT.Exp, bias=rmax[:, hh:hh + 1],
                                               accum_out=rsum[:, hh:hh + 1])
                ins.then_inc(S("exp"), 1)
                if t == 0:
                    relus(1)
                    gate_out(4)
                    gate_out(5)
                else:
                    gate_out(9)
                for hh in range(H1 + 1):
                    if hh == 4 and t == 0:
                        gate_out(6)
                    if hh < H1:
                        b = full(act, f"tr{t}_{hh}")
                        if hh >= 2 or t:
                            done = hh - 2 if hh >= 2 else hh + 6
                            if done % 4 == 3:
                                full(act, f"pv{t if hh >= 2 else t - 1}_{done // 4}")
                            else:
                                act.wait_ge(S("pv_mm"), pv_count(t if hh >= 2 else t - 1, done))
                        if t:
                            nc.scalar.copy(pT[:, hh % 2, 0:2], wide(b[:, 0:2 * P], P))
                        else:
                            nc.scalar.copy(pT[:, hh % 2, 0], b[:, 0:P])
                        is_free(nc.scalar.copy(pT[0:META, hh % 2, 2], b[0:META, 2 * P:3 * P]), f"tr{t}_{hh}")
                    if hh % 4 == 0 and hh:
                        g = hh // 4 - 1
                        b = full(act, f"pv{t}_{g}")
                        is_free(nc.scalar.copy(yo[:, 4 * g:4 * g + 4, t * P:t * P + P], wide(b[:], P)), f"pv{t}_{g}")
                if t == 0:
                    gate_out(7)
                    gate_out(8)
            for g in range(2):
                after(act, f"pv1_{g}")
                nc.scalar.copy(shi[:, 4 * g:4 * g + 4], yo[:, 4 * g:4 * g + 4]).then_inc(S("shi"), 1)
            gate_out(10)
            gate_out(11)
            act_gdn(act, own)
            for name in ("wbg",):
                for j in range(4):
                    act.wait_ge(S("merged"), j + 1)
                    nc.scalar.copy(xhi[:, 2 * j:2 * j + 2, 0:SEQ], merged[:, 2 * j:2 * j + 2]).then_inc(S("mhi"), 1)
                    load_hi(FIRST[name] + j + 3, 0)
            act_layer_out(act, "wout", "postmix")
            act_pre(act, "mlp", xhi, "pre_mlp", "h_postmix", FIRST["up"])

            def up(s0, it, j):
                u0 = pair_first["up"] + j
                load_hi(s0 + 3, it)
                act.wait_ge(pair_free[u0 % 2], u0 // 2 + 1 + 2 * it)
                nc.scalar.activation(uhi[:, bass.ds(2 * j + 8 * it, 2)], rt[:, u0 % 2], ACT.Square)\
                    .then_inc(S("uhi"), 1)
            slots(act, "up", up, lead=4)
            act_layer_out(act, "down", "postmlp")
            act_second(act, own)

        def pv_count(t, hh):
            return t * 6 + (hh // 4) * 3 + hh % 4 + 1

        def act_gdn(act, own):
            for w, dst in enumerate((sqq, sqk)):
                nc.scalar.activation(dst[:], qkv[:, 8 * w:8 * w + 8], ACT.Square).then_inc(S("l2sq"), 1)
            load_hi(FIRST["wbd"] + 3, 0)
            act_head_root(act, "l2sum", 16, T1, 1.0)
            load_hi(FIRST["wbd"] + 4, 0)
            nc.scalar.activation(bg[:, :, 0:8], small[:, :, 0:8], ACT.Sigmoid)
            nc.scalar.activation(aexp[:], pcol("alog", 0, 8), ACT.Exp)
            act.wait_ge(S("g_arg"), 1)
            own.link(nc.scalar.activation(gtmp[:, 1], gtmp[:, 0], ACT.Abs))
            own.link(nc.scalar.activation(gtmp[:, 1], gtmp[:, 1], ACT.Exp, scale=-1.0))
            nc.scalar.activation(gtmp[:, 1], gtmp[:, 1], ACT.Ln, bias=ones[:, 0:1]).then_inc(S("g_ln"), 1)
            load_hi(FIRST["wbd"] + 5, 0)
            load_hi(FIRST["wbd"] + 6, 0)
            act.wait_ge(S("ktsc"), 1)
            nc.scalar.activation(ktsc[:], ktsc[:], ACT.Exp)
            is_free(nc.scalar.activation(egl[:], AUX[USE["cum"][0]][:, 20:28], ACT.Exp), "cum")
            ndm = 0
            for s, probs in enumerate(PROBLEMS):
                n = len(probs)
                for g in range(seg(probs)):
                    m = min(4, n - 4 * g)
                    ndm += 1
                    act.wait_ge(S("dm_arg"), ndm)
                    name = f"gb{s}_{g}"
                    is_free(nc.scalar.activation(eg[:, 4 * g:4 * g + m], wide(AUX[USE[name][0]][:, 0:m * P], P), ACT.Exp),
                            name)
                    nc.scalar.activation(dms[s][:, 4 * g:4 * g + m], dms[s][:, 4 * g:4 * g + m], ACT.Exp)\
                        .then_inc(S("dm_exp"), 1)
                for g in range(seg(probs)):
                    m = min(4, n - 4 * g)
                    b = full(act, f"vt{s}_{g}")
                    for q in range(m):
                        p_ = probs[4 * g + q]
                        ins = nc.scalar.activation(vbs[s][:, 4 * g + q], b[:, q * P:q * P + P], ACT.Copy,
                                                   scale=bcg[:, 0, p_:p_ + 1])
                    is_free(ins, f"vt{s}_{g}")
                if s == 0:
                    continue

                def level(kind, it=0):
                    for a, g in TOGETHER[s]:
                        m = min(4, len(PROBLEMS[a]) - 4 * g)
                        name = f"{kind}_x{a}_{g}"
                        b = full(act, name, it)
                        is_free(nc.scalar.copy(xss[a][:, 4 * g:4 * g + m], wide(b[:, 0:m * P], P)), name)

                with act.Fori(0, MID) as it:
                    level("mid", it)
                level("last")
                if s == 1:
                    b = full(act, "v0_0")
                    is_free(nc.scalar.copy(vn[:, 0:1], wide(b[:, 0:P], P)), "v0_0")
                for g in range(2):
                    b = full(act, f"v{s}_{g}")
                    is_free(nc.scalar.copy(vn[:, 4 * g:4 * g + 4], wide(b[:], P)), f"v{s}_{g}")
                for g in range(2):
                    b = full(act, f"o{s}_{g}")
                    is_free(nc.scalar.copy(og[:, 4 * g:4 * g + 4, (s - 1) * P:s * P], wide(b[:], P)), f"o{s}_{g}")
                    if s == 2:
                        act_head_squares(act, "ng", g)
            head_norm_act(act, "ng")

        def act_head_root(act, name, heads, T, scale):
            b = full(act, name)
            is_free(nc.scalar.activation(rhead[0:heads, 0:T], b[0:heads, 0:T], ACT.Sqrt, scale=scale,
                                         bias=eps[0:heads, 0:1]), name)

        def act_head_squares(act, tag, g):
            after(act, f"o2_{g}" if tag == "ng" else f"dp1_{g}")
            src, squares, _, _ = HEADS[tag]
            a = slice(4 * g, 4 * g + 4)
            nc.scalar.activation(squares[:, a], src[:, a], ACT.Square).then_inc(S(tag + "sq"), 1)

        def head_norm_act(act, tag):
            src, _, hi, _ = HEADS[tag]
            act_head_root(act, tag + "sum", 8, SEQ, 1.0 / P)
            for n in range(4):
                after(act, f"{tag}{n}")
                a = slice(2 * n, 2 * n + 2)
                nc.scalar.copy(hi[:, a], src[:, a]).then_inc(S(tag + "hi"), 1)

        def act_second(act, own):
            act_pre(act, "ret", xhi, "a_pre", "h_postmlp")
            for name in ("rq", "rk"):
                for j in range(4):
                    s = FIRST[name] + j
                    act.wait_ge(slot_done, s + 1)
                    load_hi(s + 3, 0)

            act_token_scale(act, "ret")

            def values(s0, it, j):
                u0 = pair_first["rv"] + j
                act.wait_ge(slot_done, s0 + 1 + 4 * it)
                for c in range(2):
                    ins = nc.scalar.activation(rv[:, c, bass.ds(j * NCOL + 4 * NCOL * it, NCOL)],
                                               PS[u0 % 2][:, c, 0:NCOL], ACT.Copy, scale=rcol[:, c:c + 1])
                ins.then_inc(pair_free[u0 % 2], 1)
                load_hi(s0 + 3, it)
            slots(act, "rv", values)

            def slot_hi(j):
                load_hi(FIRST["rg"] + j + 3, 0)

            def silu(j):
                pair_done(act, pair_first["rg"] + j)
                g = rg[:, 2 * j:2 * j + 2]
                nc.scalar.activation(g, g, ACT.Silu).then_inc(S("rg"), 1)

            def readout(hh):
                if hh >= 2:
                    full(act, f"rn{hh - 2}")
                for e in range(2):
                    b = full(act, f"ro{hh}_{e}")
                    nc.scalar.copy(ro[:, 4 * hh + 2 * e:4 * hh + 2 * e + 2], wide(b[:], SEQ))
                    is_free(nc.scalar.activation(rsq[:, hh % 2, 2 * e:2 * e + 2], wide(b[:], SEQ), ACT.Square),
                            f"ro{hh}_{e}")

            def root(hh):
                b = full(act, f"rn{hh}")
                if hh >= 2:
                    act.wait_ge(S("ro_done"), hh - 1)
                is_free(nc.scalar.activation(rrn[:, hh % 2], b[:, 0:SEQ], ACT.Sqrt, scale=1.0 / 512, bias=eps[:, 0:1]),
                        f"rn{hh}")

            def high(hh):
                a = slice(4 * hh, 4 * hh + 4)
                act.wait_ge(S("ro_done"), hh + 1)
                nc.scalar.copy(rhi[:, a], ro[:, a]).then_inc(S("rhi"), 1)

            todo = {"hi": slot_hi, "silu": silu, "readout": readout, "root": root, "high": high}
            for name, n in RETENTION:
                if name in todo:
                    todo[name](n)
            act_layer_out(act, "ro", "postret")
            act_ffn(act, own, 0)
            act_pre(act, "diff", xhi, "kv", "h_postffn0")
            for j in range(4):
                s = FIRST["dk"] + j
                if j == 2:
                    for kt in range(KT):
                        ins = nc.scalar.activation(x2hi[:, kt], hx[:, kt], ACT.Copy, scale=pcol("b_pre", kt))
                    ins.then_inc(S("x2hi"), 1)
                load_hi(s + 3, 0)
            act.wait_ge(S("lam"), 1)
            nc.scalar.activation(lamt[:, 2:4], lamt[:, 0:2], ACT.Exp).then_inc(S("lam_exp"), 1)
            for j in range(4):
                load_hi(FIRST["dq"] + j + 3, 0)
            act_token_scale(act, "diff")

            def exponentials(n):
                for t in range(2):
                    W = P + t * P
                    act.wait_ge(S("rmax2"), 2 * n + t + 1)
                    for q in range(4 * n, 4 * n + 4):
                        ins = nc.scalar.activation(lm2s[t][:, q, 0:W], lm2s[t][:, q, 0:W], ACT.Exp,
                                                   bias=dmax[:, t, q:q + 1], accum_out=dsum[:, t, q:q + 1])
                    ins.then_inc(S("exp2"), 1)

            for j in range(4):
                s, u = FIRST["dv"] + j, pair_first["dv"] + j
                act.wait_ge(slot_done, s + 1)
                for c in range(2):
                    ins = nc.scalar.activation(dv[:, c, j * NCOL:(j + 1) * NCOL], PS[u % 2][:, c, 0:NCOL], ACT.Copy,
                                               scale=rcol[:, c:c + 1])
                ins.then_inc(pair_free[u % 2], 1)
                if j < 3:
                    load_hi(s + 3, 0)
                if j:
                    exponentials(j - 1)
            exponentials(3)
            for t in range(2):
                W = P + t * P
                for hh in range(H1 + 1):
                    if hh < H1:
                        b = full(act, f"dt{t}_{hh}")
                        if hh >= 2 or t:
                            done = hh - 2 if hh >= 2 else hh + 6
                            if done % 4 == 3:
                                full(act, f"dp{t if hh >= 2 else t - 1}_{done // 4}")
                            else:
                                act.wait_ge(S("dp_mm"), pv_count(t if hh >= 2 else t - 1, done))
                        is_free(nc.scalar.copy(aT[:, hh % 2, 0:1 + t], wide(b[:, 0:W], P)), f"dt{t}_{hh}")
                    if hh % 4 == 0 and hh:
                        g = hh // 4 - 1
                        b = full(act, f"dp{t}_{g}")
                        is_free(nc.scalar.copy(do[:, 4 * g:4 * g + 4, t * P:t * P + P], wide(b[:], P)), f"dp{t}_{g}")
                        if t:
                            act_head_squares(act, "nd", g)
                if t == 0:
                    load_hi(FIRST["dv"] + 6, 0)
            head_norm_act(act, "nd")
            act_layer_out(act, "do", "postdiff")
            act_ffn(act, own, 1)

        def act_ffn(act, own, k):
            act_pre(act, f"ffn{k}", xhi, f"f_pre{k}", ["h_postret", "h_postdiff"][k], FIRST[f"fu{k}"])

            def conv(s0, it, j):
                u0 = pair_first[f"fu{k}"] + j
                n0 = k * FT2 + j
                p = s0 % 2
                if j % 4 == 0:
                    nc.scalar.activation(gtmp[:, 2, 0, 1:2], eps[:, 0:1], ACT.Silu)
                act.wait_ge(pair_free[u0 % 2], u0 // 2 + 1 + 2 * it)
                if n0 >= 2:
                    act.wait_ge(S("f_prod"), n0 - 1 + 4 * it)
                for t in range(2):
                    ins = nc.scalar.activation(ft[:, p, t], fy[:, p, t], ACT.Identity,
                                               scale=pdyn(f"f_conv{k}", (t * FT2 + j) * 3 + 2 + 12 * it),
                                               bias=pdyn(f"f_bias{k}", t * FT2 + j + 4 * it))
                ins.then_inc(S("f_tap"), 1)
                load_hi(s0 + 3, it)
                act.wait_ge(S("f_conv"), n0 + 1 + 4 * it)
                nc.scalar.activation(fs[:, p], ft[:, p, 0], ACT.Silu).then_inc(S("f_silu"), 1)
                act.wait_ge(S("f_prod"), n0 + 1 + 4 * it)
                nc.scalar.copy(fhi[:, bass.ds(j + 4 * it, 1)], fu[:, p].unsqueeze(1)).then_inc(S("f_hi"), 1)
            slots(act, f"fu{k}", conv)
            act_layer_out(act, f"fd{k}", f"postffn{k}")


        def dve_mix(dve, own):
            after(dve, "norm_mix")
            own.link(nc.vector.reciprocal(rstd[:], rstd[:]))

            def low(c):
                dve.wait_ge(S("xhi_mix"), c + 1)
                a = slice(2 * c, 2 * c + 2)
                nc.vector.tensor_tensor(xlo[:, a], xf[:, a], xhi[:, a].bitcast(F32), ALU.subtract)\
                    .then_inc(S("xlo_mix"), 1)

            for c in range(4):
                for kt in (2 * c, 2 * c + 1):
                    ins = nc.vector.scalar_tensor_tensor(xf[:, kt], h[:, kt], pcol("pre_mix", kt), rstd[:], ALU.mult,
                                                         ALU.mult)
                ins.then_inc(S("xf_mix"), 1)
                if c:
                    low(c - 1)
            low(3)

        def dve_root(dve, name):
            after(dve, "norm_" + name)
            nc.vector.reciprocal(rcol[:], rcol[:]).then_inc(S("rcol_" + name), 1)
            full(dve, "rstd_" + name)

        def dve_post(dve, own, name, layer, follow=None):
            dve_root(dve, name)
            b = AUX[USE["rstd_" + name][0]]

            def low(c):
                nxt_name, nxt_gain, lo, hi = follow
                dve.wait_ge(S("xhi_" + nxt_name), c + 1)
                for kt in (2 * c, 2 * c + 1):
                    ins = nc.vector.scalar_tensor_tensor(lo[:, kt, 0:SEQ], hx[:, kt], pcol(nxt_gain, kt),
                                                         hi[:, kt, 0:SEQ].bitcast(F32), ALU.mult, ALU.subtract)
                ins.then_inc(S("xlo_" + nxt_name), 1)

            for c in range(4):
                a = slice(2 * c, 2 * c + 2)
                own.link(nc.vector.tensor_tensor(xf[:, a, 0:SEQ], yo[:, a], bc(b[:, 0:SEQ], 2), ALU.mult))
                nc.vector.tensor_tensor(hx[:, a], hx[:, a], xf[:, a, 0:SEQ], ALU.add).then_inc(S("h_" + name), 1)
                if follow and c:
                    low(c - 1)
            dve.wait_ge(S("h_" + name), 4)
            is_free(nc.vector.tensor_scalar(top8[:, 0:1], ones[:, 0:1], 1.0, None, ALU.mult), "rstd_" + name)
            if follow:
                low(3)
                after(dve, "norm_" + follow[0])
                nc.vector.reciprocal(rstd[:, 0:SEQ], rstd[:, 0:SEQ]).then_inc(S("r_" + follow[0]), 1)
                if follow[0][:3] != "ffn":
                    load_lo(FIRST[layer] + dict(STREAM)[layer] + 2, 0)
                dve.wait_ge(S("r_" + follow[0]), 1)

        def dve_idle_layer(name):
            def step(s0, it, j):
                if j < last:
                    load_lo(s0 + 3, it)
            last = dict(STREAM)[name] - (1 if name in POST else 0)
            slots(nc.vector, name, step, NSLOT if name in POST else 4)

        def dve_body(dve, own):
            dve.wait_ge(par_in, 16)
            load_lo(0, 0)
            dve_mix(dve, own)
            load_lo(1, 0)
            load_lo(2, 0)
            load_lo(3, 0)

            def conv(s0, it, j):
                u0 = pair_first["qkv"] + j
                dve.wait_ge(S("conv_tap"), j + 1 + 4 * it)
                for tap in (2, 1, 0):
                    sh = 3 - tap
                    for t in range(2):
                        col = (2 * j + t) * 4 + tap + it * 32
                        ins = nc.vector.scalar_tensor_tensor(
                            ctmp[:, u0 % 2, t, sh:T1], PS[u0 % 2][:, t, 0:T1 - sh], pdyn("conv", col),
                            ctmp[:, u0 % 2, t, sh:T1], ALU.mult, ALU.add)
                    if tap:
                        own.link(ins)
                ins.then_inc(pair_free[u0 % 2], 1)
                load_lo(s0 + 3, it)
            slots(dve, "qkv", conv, chain=own, links=2)
            dve.wait_ge(c1_in, 16)
            dve.wait_ge(S("conv_silu"), 12)
            todo = list(rotations())
            for step in PROJECT:
                if isinstance(step, tuple):
                    if step[0] != "gb":
                        load_lo(FIRST[step[0]] + step[1] + 3, 0)
                    continue
                name, x, W, c, sn, t0 = todo[step]
                n = x.shape[1]
                b = full(dve, name)
                is_free(nc.vector.tensor_tensor(ctmp[:, 0, 0:n, 0:W], wide(b[:, 0:n * W], W),
                                                bc(cst(sn, lo=t0, n=W), n), ALU.mult), name)
                after(dve, name)
                own.link(nc.vector.tensor_tensor(x, x, bc(cst(c, lo=t0, n=W), n), ALU.mult))
                nc.vector.tensor_tensor(x, x, ctmp[:, 0, 0:n, 0:W], ALU.add).then_inc(S("rope"), 1)
                dve.wait_ge(S("rope"), step + 1)
            own.link(nc.vector.tensor_scalar(wix[:], small[:, 0:2, 16:24], IDX_SCALE, None, ALU.mult))
            def top_bias(t):
                W = META + P + t * P
                past = cst("past", lo=t * T1, n=W)
                for hh in range(H1):
                    after(dve, f"idx{t}_{hh}")
                    w = wix[:, t, hh:hh + 1]
                    n = t * H1 + hh
                    if n:
                        dve.wait_ge(S("relu_used"), n)
                    if hh == 0:
                        ins = nc.vector.tensor_scalar(iscore[:, 0:W], irelu[:, hh % 2, 0:W], w, None, ALU.mult)
                    else:
                        ins = nc.vector.scalar_tensor_tensor(iscore[:, 0:W], irelu[:, hh % 2, 0:W], w, iscore[:, 0:W],
                                                             ALU.mult, ALU.add)
                    ins.then_inc(S("relu_used"), 1)
                dve.wait_ge(S("relu_used"), t * H1 + H1)
                own.link(nc.vector.tensor_tensor(iwork[:, 0:W], iscore[:, 0:W], past, ALU.add))
                for _ in range(ROUNDS):
                    own.link(nc.vector.max(top8[:], iwork[:, 0:W]))
                    own.link(nc.vector.match_replace(iwork[:, 0:W], top8[:], iwork[:, 0:W], TAKEN))
                if t:
                    for hh in range(4, 8):
                        after(dve, f"log0_{hh}")
                own.link(nc.vector.tensor_scalar(ibias[:, 0:W], iwork[:, 0:W], TAKEN, BIG, ALU.is_equal, ALU.mult))
                own.link(nc.vector.scalar_tensor_tensor(ibias[:, 0:W], ibias[:, 0:W], -BIG, past, ALU.add, ALU.add))

            for t in range(2):
                W = META + P + t * P
                top_bias(t)
                if t:
                    full(dve, "tr0_7")
                for hh in range(H1):
                    b = full(dve, f"log{t}_{hh}")
                    is_free(nc.vector.scalar_tensor_tensor(lm[:, hh, 0:W], b[:, 0:W], ATT_SCALE, ibias[:, 0:W],
                                                           ALU.mult, ALU.add), f"log{t}_{hh}")
                for hh in range(4, 8):
                    after(dve, f"log{t}_{hh}")
                nc.vector.tensor_reduce(rmax[:, 0:8], lm[:, :, 0:W], AX.X, ALU.max, negate=True)\
                    .then_inc(S("rmax"), 1)
                dve.wait_ge(S("exp"), t + 1)
                own.link(nc.vector.reciprocal(rinv[:, 0:8], rsum[:, 0:8]))
                for g in range(2):
                    nc.vector.tensor_tensor(lm[:, 4 * g:4 * g + 4, 0:W], lm[:, 4 * g:4 * g + 4, 0:W],
                                            rinv[:, 4 * g:4 * g + 4].unsqueeze(2).to_broadcast([P, 4, W]), ALU.mult)\
                        .then_inc(S("prob"), 1)
            for g in range(2):
                dve.wait_ge(S("shi"), g + 1)
                nc.vector.tensor_tensor(slo[:, 4 * g:4 * g + 4], yo[:, 4 * g:4 * g + 4],
                                        shi[:, 4 * g:4 * g + 4].bitcast(F32), ALU.subtract).then_inc(S("slo"), 1)
            dve.wait_ge(lo_ready, FIRST["wbd"] + 3)
            dve_gdn(dve, own)
            for j in range(4):
                s, u = FIRST["wbg"] + j, pair_first["wbg"] + j
                a = slice(2 * j, 2 * j + 2)
                dve.wait_ge(slot_done, s + 1)
                nc.vector.tensor_tensor(merged[:, a], PS[u % 2][:, :, 0:SEQ], gas[:, a], ALU.mult)\
                    .then_inc(pair_free[u % 2], 1)
                pair_done(dve, u)
                nc.vector.tensor_tensor(merged[:, a], merged[:, a], m1[:, a], ALU.add).then_inc(S("merged"), 1)
                dve.wait_ge(S("mhi"), j + 1)
                nc.vector.tensor_tensor(xlo[:, a, 0:SEQ], merged[:, a], xhi[:, a, 0:SEQ].bitcast(F32), ALU.subtract)\
                    .then_inc(S("mlo"), 1)
                load_lo(s + 3, 0)
            dve_idle_layer("wout")
            dve_post(dve, own, "postmix", "wout", ("mlp", "pre_mlp", xlo, xhi))

            def up(s0, it, j):
                u0 = pair_first["up"] + j
                p = u0 % 2
                dve.wait_ge(slot_done, s0 + 1 + 4 * it)
                if j >= 2:
                    dve.wait_ge(S("uhi"), j - 1 + 4 * it)
                nc.vector.scalar_tensor_tensor(rt[:, p], PS[p][:, :, 0:SEQ], 0.0, bc(rstd[:, 0:SEQ], 2), ALU.max,
                                               ALU.mult).then_inc(pair_free[p], 1)
                load_lo(s0 + 3, it)
                dve.wait_ge(pair_free[p], u0 // 2 + 1 + 2 * it)
                own.link(nc.vector.tensor_tensor(ut[:, p], rt[:, p], rt[:, p], ALU.mult))
                dve.wait_ge(S("uhi"), j + 1 + 4 * it)
                nc.vector.tensor_tensor(ulo[:, bass.ds(2 * j + 8 * it, 2)], ut[:, p],
                                        uhi[:, bass.ds(2 * j + 8 * it, 2)].bitcast(F32), ALU.subtract)\
                    .then_inc(S("ulo"), 1)
            slots(dve, "up", up, chain=own, links=1, lead=4)
            dve_idle_layer("down")
            dve_post(dve, own, "postmlp", "down", ("ret", "a_pre", xlo, xhi))
            dve_second(dve, own)

        def dve_gdn(dve, own):
            own.link(nc.vector.tensor_tensor(gtmp[:, 0], small[:, :, 8:16], bc(pcol("dtb", 0, 8), 3), ALU.add))
            nc.vector.tensor_scalar(top8[:, 0:1], ones[:, 0:1], 1.0, None, ALU.mult).then_inc(S("g_arg"), 1)

            def branch(j):
                s, u = FIRST["wbd"] + j, pair_first["wbd"] + j
                dve.wait_ge(slot_done, s + 1)
                if j == 0:
                    for u_ in (2, 3):
                        pair_done(dve, pair_first["ga"] + u_)
                nc.vector.tensor_tensor(m1[:, 2 * j:2 * j + 2], PS[u % 2][:, :, 0:SEQ], gbs[:, 2 * j:2 * j + 2],
                                        ALU.mult).then_inc(pair_free[u % 2], 1)
                load_lo(s + 3, 0)

            def unit(heads):
                for hh in heads:
                    b = full(dve, f"l2b{hh}")
                    is_free(nc.vector.scalar_tensor_tensor(qkv[:, hh], qkv[:, hh], P ** -0.5 if hh < 8 else 1.0,
                                                           b[:, 0:T1], ALU.mult, ALU.mult), f"l2b{hh}")

            branch(0)
            after(dve, "l2sum")
            nc.vector.reciprocal(rhead[:, 0:T1], rhead[:, 0:T1]).then_inc(S("l2r"), 1)
            branch(1)
            unit(range(4))
            dve.wait_ge(S("g_ln"), 1)
            own.link(nc.vector.scalar_tensor_tensor(gtmp[:, 0], gtmp[:, 0], 0.0, gtmp[:, 1], ALU.max, ALU.add))
            nc.vector.scalar_tensor_tensor(bg[:, :, 8:16], gtmp[:, 0], -1.0, bc(aexp[:], 3), ALU.mult, ALU.mult)\
                .then_inc(S("bg"), 1)
            dve.wait_ge(S("bg"), 1)
            nc.vector.tensor_copy(bcg[:, 0, 0:16].rearrange("p (c n) -> p c n", n=8), bg[:, 0:2, 0:8])
            nc.vector.tensor_copy(bcg[:, 1, 0:16].rearrange("p (c n) -> p c n", n=8), bg[:, 0:2, 8:16])
            branch(2)
            b = full(dve, "sel")
            is_free(nc.vector.tensor_tensor(wide(sel16[:], 8), wide(b[:, 0:16], 8), bc(cst("head"), 2), ALU.mult), "sel")
            after(dve, "sel")
            nc.vector.tensor_reduce(bcg[:, :, 16:17], wide(sel16[:], 8), AX.X, ALU.add).then_inc(S("bcg"), 1)
            dve.wait_ge(S("bcg"), 1)
            unit(range(4, 8))
            branch(3)
            b = full(dve, "cum")
            own.link(nc.vector.tensor_copy(gcum[:], b[:, 0:17]))
            nc.vector.tensor_tensor(ktsc[:, 0:8], b[:, 20:28], gcum[:, 0:8], ALU.subtract)
            nc.vector.tensor_tensor(ktsc[:, 8:9], b[:, 28:29], gcum[:, 16:17], ALU.subtract).then_inc(S("ktsc"), 1)
            unit(range(8, 16))
            for hh in range(12, 16):
                after(dve, f"l2b{hh}")
            for n in range(2):
                ins = nc.vector.tensor_copy(wide(og[:, n, 0:P], META), qkv[:, 8 + 8 * n:16 + 8 * n, 0:META])
            ins.then_inc(S("meta_kv"), 1)
            dve.wait_ge(S("meta_kv"), 1)
            nexp = 0
            for s, probs in enumerate(PROBLEMS):
                n = len(probs)
                ng = seg(probs)
                upper = cst("upper") if s else cst("upper16")
                for g in range(ng):
                    m = min(4, n - 4 * g)
                    b = full(dve, f"gb{s}_{g}")
                    for q in range(m):
                        ins = nc.vector.tensor_scalar(dms[s][:, 4 * g + q], b[:, q * P:q * P + P],
                                                      gcum[:, probs[4 * g + q]:probs[4 * g + q] + 1], 0.0,
                                                      ALU.subtract, ALU.min)
                    ins.then_inc(S("dm_arg"), 1)
                    b = full(dve, f"bb{s}_{g}")
                    is_free(nc.vector.tensor_tensor(kbs[s][:, 4 * g:4 * g + m], wide(b[:, 0:m * P], P), kview(s, g, m),
                                                    ALU.mult), f"bb{s}_{g}")
                for g in range(ng):
                    m = min(4, n - 4 * g)
                    nexp += 1
                    dve.wait_ge(S("dm_exp"), nexp)
                    a = slice(4 * g, 4 * g + m)
                    own.link(nc.vector.tensor_tensor(dms[s][:, a], dms[s][:, a], bc(upper, m), ALU.mult))
                    b = full(dve, f"kk{s}_{g}")
                    is_free(nc.vector.tensor_tensor(ats[s][:, a], wide(b[:, 0:m * P], P), dms[s][:, a], ALU.mult),
                            f"kk{s}_{g}")
                    if s:
                        b = full(dve, f"qk{s}_{g}")
                        is_free(nc.vector.tensor_tensor(att[:, a], wide(b[:, 0:m * P], P), dm[:, a], ALU.mult),
                                f"qk{s}_{g}")
                if s < 2:
                    for g in range(ng):
                        m = min(4, n - 4 * g)
                        if s == 0:
                            after(dve, "cum")
                        b = full(dve, f"kt{s}_{g}")
                        for q in range(m):
                            c = 8 if s == 0 else 4 * g + q
                            ins = nc.vector.tensor_scalar(ktok[:, 4 * g + q], b[:, q * P:q * P + P], ktsc[:, c:c + 1],
                                                          None, ALU.mult)
                        is_free(ins, f"kt{s}_{g}")
                if s == 0:
                    after(dve, "kt0_0")
                    for hh in range(H1):
                        ins = nc.vector.tensor_scalar(ktm[:, hh], ktok[:, 0], cst("head", lo=hh, n=1), None, ALU.mult)
                    ins.then_inc(S("ktm"), 1)
                    dve.wait_ge(S("ktm"), 1)
                    continue
                for k, (a, g) in enumerate(TOGETHER[s]):
                    m = min(4, len(PROBLEMS[a]) - 4 * g)
                    name = f"first_x{a}_{g}"
                    b = full(dve, name)
                    w = min(2, m)
                    t = tus[a][:, 2 * g:2 * g + -(-m // 2)]
                    eye = ident.unsqueeze(1).unsqueeze(1).to_broadcast([P, -(-m // 2), w, P])
                    four = lambda v: v.rearrange("p (a b w) -> p a b w", b=w, w=P)
                    is_free(nc.vector.tensor_tensor(t[:, :, 0:w], four(b[:, 0:m * P]), eye, ALU.add), name)
                    ins = nc.vector.tensor_tensor(t[:, :, 2:2 + w],
                                                  als[a][:, 4 * g:4 * g + m].rearrange("p (a b) w -> p a b w", b=w), eye,
                                                  ALU.add)
                ins.then_inc(S("first_level"), 1)
                own.link(nc.vector.tensor_tensor(kb[:, 0:n], kb[:, 0:n], eg[:, 0:n], ALU.mult))
                q = qkv[:, 0:8, META + (s - 1) * P:META + s * P]
                nc.vector.tensor_tensor(q, q, eg[:, 0:n], ALU.mult).then_inc(S("ke"), 1)

                def level(kind, it=0):
                    for _, a, g in PAIRS[s]:
                        m = min(2, len(PROBLEMS[a]) - 2 * g)
                        name = f"{kind}_y{a}_{g}"
                        b = full(dve, name, it)
                        v, t = wide(b[:], P), tus[a][:, g]
                        if kind == "last":
                            v, t = v[:, 2:2 + m], t[:, 2:2 + m]
                        elif m == 1:
                            v, t = v[:, 0:4:2], t[:, 0:4:2]
                        is_free(nc.vector.tensor_tensor(t, v, t, ALU.add), name)

                with dve.Fori(0, MID) as it:
                    level("mid", it)
                level("last")
                if s == 1:
                    for g in range(2):
                        b = full(dve, f"s0_{g}")
                        is_free(nc.vector.tensor_copy(st[:, 4 * g:4 * g + 4], wide(b[:], P)), f"s0_{g}")
                for g in range(ng):
                    a = slice(4 * g, 4 * g + 4)
                    b = full(dve, f"r{s}_{g}")
                    after(dve, f"vt{s}_{g}")
                    is_free(nc.vector.tensor_tensor(vb[:, a], vb[:, a], wide(b[:], P), ALU.subtract), f"r{s}_{g}")
                if s == 1:
                    for g in range(2):
                        b = full(dve, f"s{s}_{g}")
                        full(dve, f"o{s}_{g}")
                        for q in range(4):
                            hh = 4 * g + q
                            ins = nc.vector.scalar_tensor_tensor(st[:, hh], st[:, hh], egl[:, hh:hh + 1],
                                                                 b[:, q * P:q * P + P], ALU.mult, ALU.add)
                        is_free(ins, f"s{s}_{g}")
            dve_head_norm(dve, own, "ng", "gdn")

        def dve_head_norm(dve, own, tag, gain):
            x, _, hi, lo = HEADS[tag]

            def low(n):
                a = slice(2 * n, 2 * n + 2)
                dve.wait_ge(S(tag + "hi"), n + 1)
                nc.vector.tensor_tensor(lo[:, a], x[:, a], hi[:, a].bitcast(F32), ALU.subtract)\
                    .then_inc(S(tag + "lo"), 1)

            for g in range(2):
                a = slice(4 * g, 4 * g + 4)
                dve.wait_ge(S(tag + "sq"), g + 1)
                if tag == "ng":
                    ins = nc.vector.scalar_tensor_tensor(x[:, a], x[:, a], pcol(gain), zs[:, a], ALU.mult, ALU.mult)
                else:
                    ins = nc.vector.tensor_scalar(x[:, a], x[:, a], pcol(gain), 1.0 - LAMBDA_INIT, ALU.mult, ALU.mult)
            own.link(ins)
            after(dve, tag + "sum")
            nc.vector.reciprocal(rhead[0:8, 0:SEQ], rhead[0:8, 0:SEQ]).then_inc(S(tag + "r"), 1)
            for n in range(4):
                a = slice(2 * n, 2 * n + 2)
                b = full(dve, f"{tag}{n}")
                is_free(nc.vector.tensor_tensor(x[:, a], x[:, a], wide(b[:], SEQ), ALU.mult), f"{tag}{n}")
                if n:
                    low(n - 1)
            low(3)

        def kview(s, g, m):
            if s == 0:
                return og[:, 0:1, 0:P]
            t0 = META + (s - 1) * P
            return qkv[:, 8 + 4 * g:8 + 4 * g + m, t0:t0 + P]

        def rotations():
            yield "rot_ik", ik[:].unsqueeze(1), T1, "cosi", "sini", 0
            for n in range(2):
                yield f"rot_iq{n}", iq[:, 2 * n:2 * n + 2], SEQ, "cosi", "sini", META
            for n in range(2):
                yield f"rot_ak{n}", ak[:, n:n + 1], T1, "cosa", "sina", 0
            for n in range(4):
                yield f"rot_aq{n}", aq[:, 2 * n:2 * n + 2], SEQ, "cosa", "sina", META

        def dve_second(dve, own):
            dve.wait_ge(c2_in, 16)
            nc.vector.tensor_tensor(rcs[:, 0], cst("rcos", t=c2), rstd[:, 0:SEQ], ALU.mult)
            own.link(nc.vector.tensor_tensor(rcs[:, 1], cst("rsin", t=c2), rstd[:, 0:SEQ], ALU.mult))
            cos, sin = rcs[:, 0], rcs[:, 1]
            for name, dst in (("rq", rq), ("rk", rk)):
                for j in range(4):
                    s, u = FIRST[name] + j, pair_first[name] + j
                    dve.wait_ge(slot_done, s + 1)
                    x = PS[u % 2][:, :, 0:SEQ]
                    nc.vector.tensor_tensor(rt1[:], x, bc(cos, 2), ALU.mult)
                    nc.vector.tensor_tensor(rt2[:], x, bc(sin, 2), ALU.mult).then_inc(pair_free[u % 2], 1)
                    pair_done(dve, u)
                    nc.vector.tensor_tensor(dst[:, 2 * j], rt1[:, 0], rt2[:, 1], ALU.subtract)
                    own.link(nc.vector.tensor_tensor(dst[:, 2 * j + 1], rt1[:, 1], rt2[:, 0], ALU.add))
                    load_lo(s + 3, 0)
            nc.vector.tensor_scalar(top8[:, 0:1], ones[:, 0:1], 1.0, None, ALU.mult).then_inc(S("rqk"), 1)
            dve_idle_layer("rv")
            for hh in range(4):
                b = full(dve, f"rs{hh}")
                dec = cst("decay", t=c2, lo=hh * SEQ, n=SEQ)
                nc.vector.tensor_tensor(rp[:, hh, 0:SEQ], b[:, 0:SEQ], dec, ALU.mult)
                is_free(nc.vector.tensor_tensor(rp[:, hh, SEQ:384], b[:, SEQ:384], dec[:, 0:P], ALU.mult), f"rs{hh}")

            def gate(j):
                s, u = FIRST["rg"] + j, pair_first["rg"] + j
                dve.wait_ge(slot_done, s + 1)
                nc.vector.tensor_tensor(rg[:, 2 * j:2 * j + 2], PS[u % 2][:, :, 0:SEQ], bc(rstd[:, 0:SEQ], 2),
                                        ALU.mult).then_inc(pair_free[u % 2], 1)
                if j < 3:
                    load_lo(s + 3, 0)

            def finish(hh):
                a = slice(4 * hh, 4 * hh + 4)
                after(dve, f"rn{hh}")
                own.link(nc.vector.reciprocal(rrn[:, hh % 2], rrn[:, hh % 2]))
                own.link(nc.vector.tensor_tensor(ro[:, a], ro[:, a], bc(rrn[:, hh % 2], 4), ALU.mult))
                dve.wait_ge(S("rg"), 2 * hh + 2)
                nc.vector.tensor_tensor(ro[:, a], ro[:, a], rg[:, a], ALU.mult).then_inc(S("ro_done"), 1)

            def low(hh):
                a = slice(4 * hh, 4 * hh + 4)
                dve.wait_ge(S("rhi"), hh + 1)
                nc.vector.tensor_tensor(rlo[:, a], ro[:, a], rhi[:, a].bitcast(F32), ALU.subtract)\
                    .then_inc(S("rlo"), 1)

            todo = {"gate": gate, "finish": finish, "low": low}
            for name, n in RETENTION:
                if name in todo:
                    todo[name](n)
            dve.wait_ge(lo_ready, FIRST["ro"] + 3)
            dve_idle_layer("ro")
            dve_post(dve, own, "postret", "ro", ("ffn0", "f_pre0", xlo, xhi))
            dve_ffn(dve, own, 0, ("diff", "kv", xlo, xhi))
            for name, dst in (("dk", dk), ("dq", dq)):
                for j in range(4):
                    s, u = FIRST[name] + j, pair_first[name] + j
                    if name == "dk" and j == 2:
                        dve.wait_ge(S("x2hi"), 1)
                        for kt in range(KT):
                            ins = nc.vector.scalar_tensor_tensor(x2lo[:, kt], hx[:, kt], pcol("b_pre", kt),
                                                                 x2hi[:, kt].bitcast(F32), ALU.mult, ALU.subtract)
                        ins.then_inc(S("x2lo"), 1)
                    dve.wait_ge(slot_done, s + 1)
                    nc.vector.tensor_tensor(dst[:, 2 * j:2 * j + 2], PS[u % 2][:, :, 0:SEQ], bc(rstd[:, 0:SEQ], 2),
                                            ALU.mult).then_inc(pair_free[u % 2], 1)
                    load_lo(s + 3, 0)
                if name == "dk":
                    for n in range(2):
                        own.link(nc.vector.tensor_tensor(am[:, n, 0:64], pcol("lam", 128 * n, 64),
                                                         pcol("lam", 128 * n + 64, 64), ALU.mult))
                    nc.vector.tensor_reduce(lamt[:, 0:2].unsqueeze(2), am[:, 0:2, 0:64], AX.X, ALU.add)\
                        .then_inc(S("lam"), 1)
            dve.wait_ge(S("lam_exp"), 1)
            own.link(nc.vector.scalar_tensor_tensor(lamt[:, 4:5], lamt[:, 2:3], LAMBDA_INIT, lamt[:, 3:4], ALU.add,
                                                    ALU.subtract))
            for n in range(4):
                for t in range(2):
                    W = P + t * P
                    past = cst("past2", t=c2, lo=t * SEQ, n=W)
                    for c in range(2):
                        name = f"ds{t}_{n}_{c}"
                        b = full(dve, name)
                        is_free(nc.vector.scalar_tensor_tensor(lm2s[t][:, 4 * n + c:4 * n + c + 3:2, 0:W],
                                                               wide(b[:], SEQ)[:, :, 0:W], 64 ** -0.5, bc(past, 2),
                                                               ALU.mult, ALU.add), name)
                    for c in range(2):
                        after(dve, f"ds{t}_{n}_{c}")
                    nc.vector.tensor_reduce(dmax[:, t, 4 * n:4 * n + 4].unsqueeze(2), lm2s[t][:, 4 * n:4 * n + 4, 0:W],
                                            AX.X, ALU.max, negate=True).then_inc(S("rmax2"), 1)
                if n < 3:
                    load_lo(FIRST["dv"] + n + 3, 0)
            for t in range(2):
                W = P + t * P
                for n in range(4):
                    dve.wait_ge(S("exp2"), 2 * n + t + 1)
                    own.link(nc.vector.reciprocal(dinv[:, t, 4 * n:4 * n + 4], dsum[:, t, 4 * n:4 * n + 4]))
                    own.link(nc.vector.tensor_scalar(dinv2[:, t, 2 * n:2 * n + 2], dinv[:, t, 4 * n + 1:4 * n + 4:2],
                                                     lamt[:, 4:5], None, ALU.mult))
                    for hh in (2 * n, 2 * n + 1):
                        ins = nc.vector.tensor_scalar(lm2s[t][:, 2 * hh + 1, 0:W], lm2s[t][:, 2 * hh + 1, 0:W],
                                                      dinv2[:, t, hh:hh + 1], None, ALU.mult)
                    own.link(ins)
                    for hh in (2 * n, 2 * n + 1):
                        nc.vector.scalar_tensor_tensor(ams[t][:, hh, 0:W], lm2s[t][:, 2 * hh, 0:W],
                                                       dinv[:, t, 2 * hh:2 * hh + 1], lm2s[t][:, 2 * hh + 1, 0:W],
                                                       ALU.mult, ALU.subtract).then_inc(S("am"), 1)
            load_lo(FIRST["dv"] + 6, 0)
            dve_head_norm(dve, own, "nd", "subln")
            dve_idle_layer("do")
            dve_post(dve, own, "postdiff", "do", ("ffn1", "f_pre1", xlo, xhi))
            dve_ffn(dve, own, 1)

        def dve_ffn(dve, own, k, follow=None):
            def conv(s0, it, j):
                u0 = pair_first[f"fu{k}"] + j
                p = s0 % 2
                dve.wait_ge(slot_done, s0 + 1 + 4 * it)
                nc.vector.tensor_tensor(fy[:, p], PS[u0 % 2][:, :, 0:SEQ], bc(rstd[:, 0:SEQ], 2), ALU.mult)\
                    .then_inc(pair_free[u0 % 2], 1)
                load_lo(s0 + 2, it)
                dve.wait_ge(S("f_tap"), k * FT2 + j + 1 + 4 * it)
                for tap in (1, 0):
                    sh = 2 - tap
                    for t in range(2):
                        col = (t * FT2 + j) * 3 + tap + 12 * it
                        ins = nc.vector.scalar_tensor_tensor(
                            ft[:, p, t, sh:SEQ], fy[:, p, t, 0:SEQ - sh], pdyn(f"f_conv{k}", col),
                            ft[:, p, t, sh:SEQ], ALU.mult, ALU.add)
                    if tap:
                        own.link(ins)
                ins.then_inc(S("f_conv"), 1)
            slots(dve, f"fu{k}", conv, chain=own, links=1)
            load_lo(FIRST[f"fd{k}"] + 2, 0)
            dve_idle_layer(f"fd{k}")
            dve_post(dve, own, f"postffn{k}", f"fd{k}", follow)


        def pe_norm_mix(pe):
            b = fill("norm_mix")
            keep_warm("small", 20)
            for kt in range(KT):
                if kt % 2 == 0:
                    pe.wait_ge(S("sq_mix"), kt // 2 + 1)
                ins = nc.tensor.matmul(b[:, 0:T1], ones[:], sq[:, kt], start=kt == 0, stop=kt == KT - 1)
            is_full(ins, "norm_mix")
            keep_warm("small", 14)

        def pe_post(pe, name, layer):
            n = list(FIRST).index(layer) + 1
            after_layer = STREAM[n][0] if n < len(STREAM) else None
            pe_sum_squares(name, 3)
            pe_spread(name)
            if after_layer:
                keep_warm(after_layer, 10)

        def pe_body(pe):
            pe.wait_ge(set_up, 1)
            pe.wait_ge(ident_in, 16)
            pe_norm_mix(pe)
            slot_in(0, 0)
            feature_slot(0, 0, xhi, xlo, tiles=(0,), ready="xlo_mix")
            for c, (t0, m) in enumerate(CHUNKS):
                ins = token_slot(0, PS[0][0:m, 1, 32 * c:32 * c + 24], xhi, xlo, slice(P, P + 24), m, t0)
            ins.then_inc(slot_done, 1)
            pe_layer("qkv", xhi, xlo, lead=4)
            pe.wait_ge(c1_in, 16)
            todo = list(rotations())
            for step in PROJECT:
                if isinstance(step, tuple):
                    name, j = step
                    s, u = FIRST[name] + j, pair_first[name] + j
                    slot_in(s, 0)
                    pair_in(u, 0, 0)
                    if name == "av":
                        for c, (t0, m) in enumerate(CHUNKS):
                            out = PS[u % 2][0:m, c, 0:NCOL] if c < 2 else PS[u % 2][0:m, 0, NCOL:2 * NCOL]
                            ins = token_slot(s, out, xhi, xlo, slice(0, NCOL), m, t0)
                    else:
                        ins = feature_slot(s, u % 2, xhi, xlo)
                    ins.then_inc(slot_done, 1)
                    continue
                name, x, W, c, sn, t0 = todo[step]
                turn = cst("turni" if c == "cosi" else "turna")
                if name == "rot_ik":
                    pair_done(pe, 0)
                elif name[:6] == "rot_iq":
                    pair_done(pe, pair_first["iq"] + int(name[6:]))
                elif name[:6] == "rot_ak":
                    pair_done(pe, pair_first["ak"])
                else:
                    pair_done(pe, pair_first["aq"] + int(name[6:]))
                b = fill(name)
                for n in range(x.shape[1]):
                    ins = nc.tensor.matmul(b[:, n * W:n * W + W], turn, x[:, n], start=True, stop=True)
                is_full(ins, name)
            def gate_slot(n):
                name, j = GATE_SLOTS[n]
                s, u = FIRST[name] + j, pair_first[name] + j
                slot_in(s, 0)
                pair_in(u, 0, 0)
                feature_slot(s, u % 2, xhi, xlo).then_inc(slot_done, 1)

            def index_scores(t):
                W = META + P + t * P
                for hh in range(H1):
                    if t and hh == 4:
                        gate_slot(4)
                    b = fill(f"idx{t}_{hh}")
                    r = slice(64 * (hh % 2), 64 * (hh % 2) + 64)
                    is_full(nc.tensor.matmul(b[:, 0:W], iq[r, hh // 2, t * P:t * P + P], ik[r, 0:W], start=True,
                                             stop=True), f"idx{t}_{hh}")

            pe.wait_ge(S("rope"), 3)
            index_scores(0)
            gate_slot(1)
            for t in range(2):
                W = META + P + t * P
                if t == 0:
                    pe.wait_ge(S("rope"), 9)
                for hh in range(H1):
                    if hh == 4:
                        gate_slot(2 if t == 0 else 7)
                        gate_slot(3 if t == 0 else 8)
                    b = fill(f"log{t}_{hh}")
                    is_full(nc.tensor.matmul(b[:, 0:W], aq[:, hh, t * P:t * P + P], ak[:, hh // 4, 0:W], start=True,
                                             stop=True), f"log{t}_{hh}")
                if t == 0:
                    index_scores(1)
                    gate_slot(5)
                else:
                    gate_slot(9)
                for hh in range(H1 + 1):
                    if hh == 4 and t == 0:
                        gate_slot(6)
                    if hh == 0:
                        name, j = GATE_SLOTS[6 if t == 0 else 10]
                        keep_warm(name, 8, j)
                    if hh % 4 == 0 and hh < H1:
                        pe.wait_ge(S("prob"), 2 * t + hh // 4 + 1)
                    if hh < H1:
                        b = fill(f"tr{t}_{hh}")
                        for c, (t0, m) in enumerate(CHUNKS):
                            if c == 1 and t == 0:
                                continue
                            ins = nc.tensor.transpose(b[0:m, c * P:c * P + P], lm[:, hh, t0:t0 + m], ident)
                        is_full(ins, f"tr{t}_{hh}")
                    if hh:
                        g = hh - 1
                        after(pe, f"tr{t}_{g}")
                        name = f"pv{t}_{g // 4}"
                        b = fill(name) if g % 4 == 0 else AUX[USE[name][0]]
                        cs = [c for c in range(3) if t or c != 1]
                        for c in cs:
                            m = CHUNKS[c][1]
                            ins = nc.tensor.matmul(b[:, (g % 4) * P:(g % 4) * P + P],
                                                   av[0:m, c, (g // 4) * P:(g // 4) * P + P], pT[0:m, g % 2, c],
                                                   start=c == 0, stop=c == 2)
                        if g % 4 == 3:
                            is_full(ins, name)
                        else:
                            ins.then_inc(S("pv_mm"), 1)
            gate_slot(10)
            gate_slot(11)
            pe_gdn(pe)
            pe_layer("wbg", ghi, glo, ready="nglo")
            keep_warm("wout", 10)
            pe_layer("wout", xhi[:, :, 0:SEQ], xlo[:, :, 0:SEQ], ready="mlo", norm="postmix")
            pe_post(pe, "postmix", "wout")
            pe_layer("up", xhi[:, :, 0:SEQ], xlo[:, :, 0:SEQ], lead=4, ready="xlo_mlp", sums="mlp")
            pe_groups("down", uhi, ulo, 4, KT, 16, norm="postmlp", ready=("ulo", [4, 8, 12, 16]))
            pe_post(pe, "postmlp", "down")
            pe_second(pe)

        def pe_gdn(pe):
            def branch(j):
                s, u = FIRST["wbd"] + j, pair_first["wbd"] + j
                slot_in(s, 0)
                pair_in(u, 0, 0)
                feature_slot(s, u % 2, shi, slo).then_inc(slot_done, 1)

            def spread(heads):
                for hh in heads:
                    b = fill(f"l2b{hh}")
                    is_full(nc.tensor.matmul(b[:, 0:T1], ident[0:16, hh:hh + 1].to_broadcast([16, P]),
                                             rhead[0:16, 0:T1], start=True, stop=True), f"l2b{hh}")

            keep_warm("wbd", 8)
            pe.wait_ge(S("slo"), 2)
            branch(0)
            pe_head_sums(pe, "l2sum", ((sqq, "l2sq", 1), (sqk, "l2sq", 2)), T1, 16)
            branch(1)
            pe.wait_ge(S("l2r"), 1)
            spread(range(4))
            branch(2)
            pe.wait_ge(S("bg"), 1)
            b = fill("sel")
            is_full(nc.tensor.matmul(b[:, 0:16], cst("spread", META), bg[0:META, 2, :], start=True, stop=True), "sel")
            spread(range(4, 8))
            branch(3)
            pe.wait_ge(S("bcg"), 1)
            b = fill("cum")
            g = bcg[:, 1]
            nc.tensor.matmul(b[:, 0:16], cst("upper"), g[:, 0:16], start=True, stop=True)
            nc.tensor.matmul(b[:, 16:17], cst("upper16"), g[:, 16:17], start=True, stop=True)
            nc.tensor.matmul(b[:, 20:28], ones[:], g[:, 0:8], start=True, stop=True)
            is_full(nc.tensor.matmul(b[:, 28:29], cst("ones16"), g[:, 16:17], start=True, stop=True), "cum")
            spread(range(8, 16))
            pe.wait_ge(S("meta_kv"), 1)
            for s, probs in enumerate(PROBLEMS):
                n, ng = len(probs), seg(probs)
                t0 = META + (s - 1) * P
                tok = slice(t0, t0 + P)

                def feat(base, q):
                    return qkv[:, base + q, tok] if s else og[:, base // 8 - 1, 0:P]
                for g in range(ng):
                    m = min(4, n - 4 * g)
                    b = fill(f"gb{s}_{g}")
                    for q in range(m):
                        j = probs[4 * g + q]
                        ins = nc.tensor.matmul(b[:, q * P:q * P + P], bcg[:, 1, j:j + 1].to_broadcast([P, P]),
                                               cst("upper" if s else "upper16"), start=True, stop=True)
                    is_full(ins, f"gb{s}_{g}")
                    b = fill(f"bb{s}_{g}")
                    for q in range(m):
                        j = probs[4 * g + q]
                        ins = nc.tensor.matmul(b[:, q * P:q * P + P], bcg[:, 0, j:j + 1].to_broadcast([P, P]), ident,
                                               start=True, stop=True)
                    is_full(ins, f"bb{s}_{g}")
                keep_warm("wbg", 3)
                for g in range(ng):
                    m = min(4, n - 4 * g)
                    after(pe, f"bb{s}_{g}")
                    b = fill(f"kk{s}_{g}")
                    for q in range(m):
                        ins = nc.tensor.matmul(b[:, q * P:q * P + P], feat(8, 4 * g + q), kbs[s][:, 4 * g + q], start=True,
                                               stop=True)
                    is_full(ins, f"kk{s}_{g}")
                    if s:
                        b = fill(f"qk{s}_{g}")
                        for q in range(m):
                            ins = nc.tensor.matmul(b[:, q * P:q * P + P], feat(8, 4 * g + q), feat(0, 4 * g + q),
                                                   start=True, stop=True)
                        is_full(ins, f"qk{s}_{g}")
                for g in range(ng):
                    m = min(4, n - 4 * g)
                    b = fill(f"vt{s}_{g}")
                    for q in range(m):
                        ins = nc.tensor.transpose(b[:, q * P:q * P + P], feat(16, 4 * g + q), ident)
                    is_full(ins, f"vt{s}_{g}")
                    if s < 2:
                        b = fill(f"kt{s}_{g}")
                        for q in range(m):
                            ins = nc.tensor.transpose(b[:, q * P:q * P + P], feat(8, 4 * g + q), ident)
                        is_full(ins, f"kt{s}_{g}")
                if s == 0:
                    continue
                keep_warm("wbg", 6)
                pe.wait_ge(S("al_ready"), (s - 1) * NLEVEL + 1)
                for a, g in TOGETHER[s]:
                    m = min(4, len(PROBLEMS[a]) - 4 * g)
                    b = fill(f"first_x{a}_{g}")
                    for q in range(m):
                        ins = nc.tensor.matmul(b[:, q * P:q * P + P], als[a][:, 4 * g + q], ident, start=True, stop=True)
                    is_full(ins, f"first_x{a}_{g}")

                def level(kind, it=0):
                    for a, g in TOGETHER[s]:
                        m = min(4, len(PROBLEMS[a]) - 4 * g)
                        b = fill(f"{kind}_x{a}_{g}", it)
                        for k in range(-(-m // 2)):
                            bank, u, per = USE[f"mid_y{a}_{2 * g + k}"]
                            pe.wait_ge(aux_free[bank], u - per + (MID if kind == "last" else it) * per)
                        for q in range(m):
                            p_ = 4 * g + q
                            ins = nc.tensor.matmul(b[:, q * P:q * P + P], als[a][:, p_], tus[a][:, p_ // 2, p_ % 2],
                                                   start=True, stop=True)
                        is_full(ins, f"{kind}_x{a}_{g}")
                    for _, a, g in PAIRS[s]:
                        m = min(2, len(PROBLEMS[a]) - 2 * g)
                        after(pe, f"{kind}_x{a}_{g // 2}", it)
                        b = fill(f"{kind}_y{a}_{g}", it)
                        for q in range(m):
                            p_ = 2 * g + q
                            if kind != "last":
                                nc.tensor.matmul(b[:, q * P:q * P + P], tus[a][:, g, 2 + q], xss[a][:, p_], start=True,
                                                 stop=True)
                            ins = nc.tensor.matmul(b[:, (2 + q) * P:(3 + q) * P], xss[a][:, p_], tus[a][:, g, 2 + q],
                                                   start=True, stop=True)
                        is_full(ins, f"{kind}_y{a}_{g}")

                keep_warm("wbg", 16)
                pe.wait_ge(S("first_level"), s)
                with pe.Fori(0, MID) as it:
                    pe.wait_ge(S("al_ready"), (s - 1) * NLEVEL + 2 + it)
                    level("mid", it)
                pe.wait_ge(S("al_ready"), s * NLEVEL)
                level("last")
                if s == 1:
                    after(pe, "last_y0_0")
                    after(pe, "vt0_0")
                    is_full(nc.tensor.matmul(fill("v0_0")[:, 0:P], tus[0][:, 0, 2], vbs[0][:, 0], start=True, stop=True),
                            "v0_0")
                    after(pe, "v0_0")
                    pe.wait_ge(S("ktm"), 1)
                    for g in range(2):
                        b = fill(f"s0_{g}")
                        for q in range(4):
                            ins = nc.tensor.matmul(b[:, q * P:q * P + P], ktm[:, 4 * g + q], vn[:, 0], start=True, stop=True)
                        is_full(ins, f"s0_{g}")
                pe.wait_ge(S("ke"), s)
                for g in range(2):
                    after(pe, f"s{s - 1}_{g}")
                    b = fill(f"r{s}_{g}")
                    for q in range(4):
                        ins = nc.tensor.matmul(b[:, q * P:q * P + P], kb[:, 4 * g + q], st[:, 4 * g + q], start=True,
                                               stop=True)
                    is_full(ins, f"r{s}_{g}")
                for g in range(2):
                    after(pe, f"last_y{s}_{2 * g}")
                    after(pe, f"last_y{s}_{2 * g + 1}")
                    after(pe, f"r{s}_{g}")
                    b = fill(f"v{s}_{g}")
                    for q in range(4):
                        p_ = 4 * g + q
                        ins = nc.tensor.matmul(b[:, q * P:q * P + P], tu[:, p_ // 2, 2 + p_ % 2], vb[:, p_], start=True,
                                               stop=True)
                    is_full(ins, f"v{s}_{g}")
                for g in range(2):
                    after(pe, f"v{s}_{g}")
                    b = fill(f"o{s}_{g}")
                    for q in range(4):
                        hh = 4 * g + q
                        nc.tensor.matmul(b[:, q * P:q * P + P], st[:, hh], feat(0, hh), start=True, stop=False)
                        ins = nc.tensor.matmul(b[:, q * P:q * P + P], vn[:, hh], att[:, hh], start=False, stop=True)
                    is_full(ins, f"o{s}_{g}")
                    if s < 2:
                        b = fill(f"s{s}_{g}")
                        for q in range(4):
                            hh = 4 * g + q
                            ins = nc.tensor.matmul(b[:, q * P:q * P + P], ktok[:, hh], vn[:, hh], start=True, stop=True)
                        is_full(ins, f"s{s}_{g}")
            pe_head_norm(pe, "ng", "wbg")

        def pe_head_sums(pe, name, parts, T, heads):
            b = fill(name)
            n = 0
            for src, sem_name, count in parts:
                for hh in range(8):
                    if count:
                        pe.wait_ge(S(sem_name), count)
                    elif hh % 4 == 0:
                        pe.wait_ge(S(sem_name), hh // 4 + 1)
                    a = CCOL["window"] + 15 - n
                    ins = nc.tensor.matmul(b[0:heads, 0:T], c1[:, a:a + heads], src[:, hh], start=n == 0,
                                           stop=n == heads - 1)
                    n += 1
            is_full(ins, name)

        def pe_head_norm(pe, tag, layer):
            pe_head_sums(pe, tag + "sum", ((HEADS[tag][1], tag + "sq", None),), SEQ, 8)
            keep_warm(layer, 8)
            pe.wait_ge(S(tag + "r"), 1)
            for n in range(4):
                b = fill(f"{tag}{n}")
                for q in range(2):
                    ins = nc.tensor.matmul(b[:, q * SEQ:(q + 1) * SEQ],
                                           ident[0:8, 2 * n + q:2 * n + q + 1].to_broadcast([8, P]), rhead[0:8, 0:SEQ],
                                           start=True, stop=True)
                is_full(ins, f"{tag}{n}")
            keep_warm(layer, 6)

        def pe_token_slot(name, s0, it, j, hi, lo):
            u0 = pair_first[name] + j
            slot_in(s0, it)
            pair_in(u0, it, 2)
            for c in range(2):
                ins = token_slot(s0, PS[u0 % 2][:, c, 0:NCOL], hi, lo, slice(0, NCOL), P, c * P)
            ins.then_inc(slot_done, 1)

        def pe_tokens(pe, name, hi, lo):
            slots(pe, name, lambda s0, it, j: pe_token_slot(name, s0, it, j, hi, lo))

        def pe_second(pe):
            x_hi, x_lo = xhi[:, :, 0:SEQ], xlo[:, :, 0:SEQ]
            pe_layer("rq", x_hi, x_lo, ready="xlo_ret", sums="ret")
            pe_layer("rk", x_hi, x_lo)
            pe_token_scale(pe, "ret")
            pe_tokens(pe, "rv", x_hi, x_lo)
            pe.wait_ge(S("rqk"), 1)
            for hh in range(4):
                b = fill(f"rs{hh}")
                for e in range(2):
                    nc.tensor.matmul(b[:, 0:SEQ], rk[:, 2 * hh + e, 0:P], rq[:, 2 * hh + e], start=e == 0, stop=e == 1)
                for e in range(2):
                    ins = nc.tensor.matmul(b[:, SEQ:384], rk[:, 2 * hh + e, P:SEQ], rq[:, 2 * hh + e, P:SEQ],
                                           start=e == 0, stop=e == 1)
                is_full(ins, f"rs{hh}")
            pair_done(pe, pair_first["rv"] + 6)
            pair_done(pe, pair_first["rv"] + 7)

            def gate(j):
                s, u = FIRST["rg"] + j, pair_first["rg"] + j
                slot_in(s, 0)
                pair_in(u, 0, 0)
                feature_slot(s, u % 2, x_hi, x_lo).then_inc(slot_done, 1)

            def product(hh):
                after(pe, f"rs{hh}")
                for e in range(2):
                    b = fill(f"ro{hh}_{e}")
                    for q in range(2):
                        a = slice((4 * hh + 2 * e + q) * P, (4 * hh + 2 * e + q + 1) * P)
                        lo = slice(q * SEQ, q * SEQ + P)
                        up = slice(q * SEQ + P, (q + 1) * SEQ)
                        nc.tensor.matmul(b[:, lo], rv[:, 0, a], rp[:, hh, 0:P], start=True, stop=True)
                        nc.tensor.matmul(b[:, up], rv[:, 0, a], rp[:, hh, P:SEQ], start=True, stop=False)
                        ins = nc.tensor.matmul(b[:, up], rv[:, 1, a], rp[:, hh, SEQ:384], start=False, stop=True)
                    is_full(ins, f"ro{hh}_{e}")

            def squares(hh):
                after(pe, f"ro{hh}_0")
                after(pe, f"ro{hh}_1")
                b = fill(f"rn{hh}")
                for e in range(4):
                    ins = nc.tensor.matmul(b[:, 0:SEQ], ones[:], rsq[:, hh % 2, e], start=e == 0, stop=e == 3)
                is_full(ins, f"rn{hh}")

            todo = {"gate": gate, "product": product, "squares": squares}
            for name, n in RETENTION:
                if name in todo:
                    todo[name](n)
            pe_groups("ro", rhi, rlo, 2, KT, 8, norm="postret", ready=("rlo", [2, 4]))
            pe_post(pe, "postret", "ro")
            pe_ffn(pe, 0)
            pe_layer("dk", x_hi, x_lo, ready="xlo_diff", sums="diff")
            pe.wait_ge(S("x2lo"), 1)
            pe_layer("dq", x2hi, x2lo)
            pe_token_scale(pe, "diff")
            for n in range(4):
                pe_token_slot("dv", FIRST["dv"] + n, 0, n, x_hi, x_lo)
                pair_done(pe, pair_first["dq"] + n)
                for t in range(2):
                    W = P + t * P
                    for c in range(2):
                        b = fill(f"ds{t}_{n}_{c}")
                        r = slice(64 * c, 64 * c + 64)
                        for q in range(2):
                            ins = nc.tensor.matmul(b[:, q * SEQ:q * SEQ + W], dq[r, 2 * n + q, t * P:t * P + P],
                                                   dk[r, 2 * n + q, 0:W], start=True, stop=True)
                        is_full(ins, f"ds{t}_{n}_{c}")
            for t in range(2):
                for hh in range(H1 + 1):
                    if hh < H1:
                        pe.wait_ge(S("am"), t * H1 + hh + 1)
                        b = fill(f"dt{t}_{hh}")
                        for c in range(1 + t):
                            ins = nc.tensor.transpose(b[:, c * P:c * P + P], ams[t][:, hh, c * P:c * P + P], ident)
                        is_full(ins, f"dt{t}_{hh}")
                    if hh:
                        g = hh - 1
                        after(pe, f"dt{t}_{g}")
                        name = f"dp{t}_{g // 4}"
                        b = fill(name) if g % 4 == 0 else AUX[USE[name][0]]
                        for c in range(1 + t):
                            ins = nc.tensor.matmul(b[:, (g % 4) * P:(g % 4) * P + P], dv[:, c, g * P:g * P + P],
                                                   aT[:, g % 2, c], start=c == 0, stop=c == t)
                        if g % 4 == 3:
                            is_full(ins, name)
                        else:
                            ins.then_inc(S("dp_mm"), 1)
            pe_head_norm(pe, "nd", "do")
            pe_layer("do", dhi, dlo, ready="ndlo", norm="postdiff")
            pe_post(pe, "postdiff", "do")
            pe_ffn(pe, 1)

        def pe_ffn(pe, k):
            pe_layer(f"fu{k}", xhi[:, :, 0:SEQ], xlo[:, :, 0:SEQ], lead=2, ready=f"xlo_ffn{k}",
                     sums=f"ffn{k}")
            pe_groups(f"fd{k}", fhi, flo, 3, FT2 - 2 * KT, 12, norm=f"postffn{k}",
                      ready=("f_lo", [FT2 * k + n for n in (KT, 2 * KT, FT2)]))
            pe_post(pe, f"postffn{k}", f"fd{k}")

        @block.gpsimd
        def _(pool):
            own = Chain(pool, pool_own)
            nc.gpsimd.memset(ones[:], 1.0)
            nc.gpsimd.memset(eps[:, 0:1], EPS)
            nc.gpsimd.memset(eps[:, 1:2], P * EPS)
            nc.gpsimd.memset(small[:], 0.0).then_inc(set_up, 1)
            pool_body(pool, own)

        @block.scalar
        def _(act):
            act_body(act, Chain(act, act_own))

        @block.vector
        def _(dve):
            dve_body(dve, Chain(dve, dve_own))

        @block.tensor
        def _(pe):
            pe_body(pe)



def tiles_of(v):
    return np.ascontiguousarray(v.reshape(-1, P).T)


def slots_of(w):
    k, n = w.shape
    if k % D:
        w = np.concatenate([w, np.zeros((-k % D, n), w.dtype)])
        k = w.shape[0]
    return w.reshape(k // D, KT, P, n // NCOL, NCOL).transpose(3, 0, 2, 1, 4).reshape(-1, P, KT, NCOL)


def pairs_of(w):
    g, u = w[:, :FF2].reshape(D, FT2, P), w[:, FF2:].reshape(D, FT2, P)
    return slots_of(np.stack([g, u], 2).reshape(D, 2 * FF2))


def constants():
    f = np.float32
    i = np.arange(P)
    same16 = (i[:, None] // 16) == (i[None, :] // 16)
    up = i[:, None] <= i[None, :]
    c = {"ident": np.eye(P), "window": np.tile(np.arange(32) == 15, (P, 1)), "upper": up, "upper16": up & same16, "ones16": same16,
         "spread": (i[:, None] == i[None, :] % 16), "head": i[:, None] // 16 == np.arange(8)[None, :]}
    lev = []
    for n in range(NLEVEL):
        b = 1 << n
        col = i[None, :] // b
        lev.append(-((col % 2 == 1) & (i[:, None] // b == col - 1)).astype(f))
    c["levels"] = np.concatenate(lev, 1)
    pos = np.arange(T1, dtype=f)
    for tag, dim in (("a", 128), ("i", 64)):
        inv = (f(10000.0) ** (-np.arange(0, dim, 2, dtype=f) / f(dim))).astype(f)
        ang = pos[None, :] * inv[i % (dim // 2)][:, None]
        c["cos" + tag], c["sin" + tag] = np.cos(ang), np.sin(ang)
        turn = np.zeros((P, P), f)
        for m in range(P):
            lo = m % dim < dim // 2
            turn[m + dim // 2 if lo else m - dim // 2, m] = -1.0 if lo else 1.0
        c["turn" + tag] = turn
    past = [np.where(pos[None, :] <= (META + t * P + i)[:, None], 0.0, -BIG) for t in range(2)]
    c["past"] = np.concatenate(past, 1)
    p2 = np.arange(SEQ, dtype=f)
    inv = (f(1.0) / (f(10000.0) ** np.linspace(0.0, 1.0, P, dtype=f))).astype(f)
    ang = inv[:, None] * p2[None, :]
    c["rcos"], c["rsin"] = np.cos(ang), np.sin(ang)
    log_gamma = np.log1p(-np.power(2.0, -5.0 - np.arange(4)))
    rel = p2[None, :] - i[:, None]
    c["decay"] = np.concatenate([np.where(rel >= 0, np.exp(lg * np.maximum(rel, 0)) / 16.0, 0.0) for lg in log_gamma], 1)
    c["past2"] = np.concatenate([np.where(p2[None, :] <= (t * P + i)[:, None], 0.0, -BIG) for t in range(2)], 1)
    return (np.concatenate([np.asarray(c[n], f) for n, _ in CONST1], 1),
            np.concatenate([np.asarray(c[n], f) for n, _ in CONST2], 1))


def laid_out(v):
    w = v["w_in"][0]
    at = np.cumsum([0, 1024, 1024, 1024, 1024, 8, 8, 1024, 256, 256, 512, 64, 8, 1024, 1024])
    gq, gk, gv, gz, gb, ga, aq, ak, av, iq, ik, iw, gate_a, gate_b = (w[:, a:b] for a, b in zip(at[:-1], at[1:]))
    small = np.concatenate([ik, ik, gb, ga, iw, np.zeros((D, NCOL - 152), w.dtype)], 1)
    ain = v["a_w_in_2"][0]
    kv = v["w_kv_2"]
    parts = {"small": small, "qkv": w[:, 0:3072], "iq": iq, "av": av, "ak": ak, "aq": aq, "z": gz, "ga": gate_a,
             "gb": gate_b, "wbd": v["w_branch_dsa"][0], "wbg": v["w_branch_gdn"][0], "wout": v["w_out"][0],
             "up": v["w_up"][0], "down": v["w_down"][0], "rq": ain[:, 0:1024], "rk": ain[:, 1024:2048],
             "rv": ain[:, 2048:4096], "rg": ain[:, 4096:6144], "ro": v["a_w_out_2"][0],
             "fd0": v["ffn_w_down_2"][0], "fd1": v["ffn_w_down_2"][1], "dk": kv[:, 0:1024], "dv": kv[:, 1024:2048],
             "dq": v["b_w_q_2"][0], "do": v["b_w_out_2"][0]}
    made = []
    for name, count in STREAM:
        if name[:2] == "fu":
            s = pairs_of(v["ffn_w_up_2"][int(name[2])])
        else:
            s = slots_of(parts[name])
        assert s.shape[0] == count, (name, s.shape, count)
        made.append(s)
    cols = {"pre_mix": tiles_of(v["pre_mix_norm"][0]),
            "conv": v["conv_w"][0].reshape(4, 24, P).transpose(2, 1, 0).reshape(P, 96),
            "gdn": tiles_of(v["gdn_norm"][0]), "post_mix": tiles_of(v["post_mix_norm"][0]),
            "pre_mlp": tiles_of(v["pre_mlp_norm"][0]), "post_mlp": tiles_of(v["post_mlp_norm"][0]),
            "a_pre": tiles_of(v["a_norm_pre_2"][0]), "a_post": tiles_of(v["a_norm_post_2"][0]),
            "kv": tiles_of(v["kv_norm_2"]), "b_pre": tiles_of(v["b_norm_pre_2"][0]),
            "b_post": tiles_of(v["b_norm_post_2"][0]), "subln": tiles_of(v["b_subln_2"][0]),
            "alog": np.tile(v["a_log"][0][None], (P, 1)), "dtb": np.tile(v["dt_bias"][0][None], (P, 1)),
            "lam": np.tile(v["b_lambda_2"][0].reshape(1, 256), (P, 1))}
    for k in range(2):
        cols[f"f_pre{k}"] = tiles_of(v["ffn_norm_pre_2"][k])
        cols[f"f_post{k}"] = tiles_of(v["ffn_norm_post_2"][k])
        cols[f"f_conv{k}"] = v["ffn_conv_w_2"][k].reshape(3, 2 * FT2, P).transpose(2, 1, 0).reshape(P, -1)
        cols[f"f_bias{k}"] = tiles_of(v["ffn_conv_b_2"][k])
    c1, c2 = constants()
    x = np.concatenate([v["meta_tokens"], v["x"][0]], 0).T.reshape(KT, P, T1).transpose(1, 0, 2)
    return {"stream": np.concatenate(made), "params": np.concatenate([cols[n] for n, _ in PARAMS], 1),
            "const1": c1, "const2": c2, "x": x}


def kernel(**inputs):
    import concourse.bacc as bacc
    from concourse.bass_utils import run_bass_kernel_spmd as run

    v = {name: np.asarray(a) for name, a in inputs.items()}
    arrays = {"in_" + n: np.ascontiguousarray(a) for n, a in laid_out(v).items()}
    nc = bacc.Bacc("TRN2", target_bir_lowering=False, num_devices=1)
    args = {n[3:]: nc.dram_tensor(n, a.shape, F32, kind="ExternalInput").ap() for n, a in arrays.items()}
    out = nc.dram_tensor("out", (P, KT, SEQ), F32, kind="ExternalOutput").ap()
    program(nc, args["stream"], args["params"], args["const1"], args["const2"], args["x"], out)
    r = run(nc, [arrays], core_ids=[0])
    y = r.results[0]["out"]
    return y.transpose(2, 1, 0).reshape(1, SEQ, D)
```
